# Optimizing a Trainium2 kernel written in Bass

```python
import jax, jax.numpy as jnp
from jax import lax
import numpy as np
import math

D_MODEL = 1024
BATCH = 1
SEQ = 256
DEPTH = 2

HEAD_DIM = 64
MLA_HEADS = 8
MLA_Q_RANK = 256
MLA_KV_RANK = 128
MLA_NOPE = 64
MLA_ROPE = 32
MLA_V = 64
DSA_HEADS = 4
IDX_HEADS = 8
IDX_DIM = 32
DSA_TOPK_MAX = 256
DIL_CONFIGS = ((128, 1), (512, 4), (2048, 16))
DIL_HEADS = 4
MIX_WIDTH = (MLA_HEADS + DSA_HEADS + DIL_HEADS) * HEAD_DIM
ROPE_THETA = 500000.0
ROT_HEAD_DIMS = HEAD_DIM // 4
ROT_IDX_DIMS = IDX_DIM // 4
Q_BLOCK = 128
N_GROUPS = 4
EXPERTS_PER_GROUP = 8
TOP_K_IN_GROUP = 2
EXPERT_HIDDEN = 256
DEEPNORM_ALPHA = (2.0 * DEPTH) ** 0.25
DEEPNORM_BETA = (8.0 * DEPTH) ** -0.25
LN_EPS = 1e-5
RMS_EPS = 1e-6
NEG_INF = -1e30
IN_SPLITS = (MLA_Q_RANK, MLA_KV_RANK, MLA_ROPE,
             DSA_HEADS * HEAD_DIM, HEAD_DIM, HEAD_DIM,
             IDX_HEADS * IDX_DIM, IDX_DIM, IDX_HEADS,
             3 * len(DIL_CONFIGS) * DIL_HEADS * HEAD_DIM)
IN_COLS = sum(IN_SPLITS)


def layer_norm(x, g, b):
    xf = x.astype(jnp.float32)
    mu = jnp.mean(xf, -1, keepdims=True)
    var = jnp.mean(jnp.square(xf - mu), -1, keepdims=True)
    return ((xf - mu) * lax.rsqrt(var + LN_EPS) * g.astype(jnp.float32) + b.astype(jnp.float32)).astype(x.dtype)

def rms_norm(x, g):
    xf = x.astype(jnp.float32)
    y = xf * lax.rsqrt(jnp.mean(jnp.square(xf), -1, keepdims=True) + RMS_EPS)
    return (y * g.astype(jnp.float32)).astype(x.dtype)

def rope_table(positions, rot_dims):
    inv = ROPE_THETA ** (-jnp.arange(0, rot_dims, 2, dtype=jnp.float32) / rot_dims)
    ang = positions.astype(jnp.float32)[..., None] * inv
    return jnp.cos(ang), jnp.sin(ang)

def apply_rope(x, cos, sin):
    half = cos.shape[-1]
    r = 2 * half
    c, s = cos[:, :, None, :], sin[:, :, None, :]
    xf = x[..., :r].astype(jnp.float32)
    x1, x2 = xf[..., :half], xf[..., half:]
    rot = jnp.concatenate([x1 * c - x2 * s, x2 * c + x1 * s], -1).astype(x.dtype)
    return jnp.concatenate([rot, x[..., r:]], -1)

def _to_blocks(a):
    B, S = a.shape[:2]
    return jnp.moveaxis(a.reshape(B, S // Q_BLOCK, Q_BLOCK, *a.shape[2:]), 1, 0)

def _from_blocks(a):
    nb, B, qb = a.shape[:3]
    return jnp.moveaxis(a, 0, 1).reshape(B, nb * qb, *a.shape[3:])

def _block_starts(S):
    return jnp.arange(S // Q_BLOCK, dtype=jnp.int32) * Q_BLOCK

def mla_mixer(cq, ckv, kpe, q_norm, kv_norm, w_uq, w_ukv, cos, sin):
    B, S = cq.shape[:2]
    q = jnp.einsum('bsr,rc->bsc', rms_norm(cq, q_norm), w_uq).reshape(B, S, MLA_HEADS, MLA_NOPE + MLA_ROPE)
    q = jnp.concatenate([q[..., :MLA_NOPE], apply_rope(q[..., MLA_NOPE:], cos, sin)], -1)
    kv = jnp.einsum('bsr,rc->bsc', rms_norm(ckv, kv_norm), w_ukv).reshape(B, S, MLA_HEADS, MLA_NOPE + MLA_V)
    k_pe = apply_rope(kpe[:, :, None, :], cos, sin)
    k = jnp.concatenate([kv[..., :MLA_NOPE], jnp.broadcast_to(k_pe, (B, S, MLA_HEADS, MLA_ROPE))], -1)
    v = kv[..., MLA_NOPE:]
    scale = (MLA_NOPE + MLA_ROPE) ** -0.5
    key_pos = jnp.arange(S, dtype=jnp.int32)

    def block(args):
        q0, qb = args
        qpos = q0 + jnp.arange(Q_BLOCK, dtype=jnp.int32)
        s = jnp.einsum('bqhd,bkhd->bhqk', qb, k, preferred_element_type=jnp.float32) * scale
        s = jnp.where(key_pos[None, :] <= qpos[:, None], s, NEG_INF)
        p = jax.nn.softmax(s, -1).astype(v.dtype)
        return jnp.einsum('bhqk,bkhd->bqhd', p, v)

    o = _from_blocks(lax.map(block, (_block_starts(S), _to_blocks(q))))
    return o.reshape(B, S, MLA_HEADS * MLA_V)

def dsa_mixer(q, k, v, qi, ki, wi, cos_h, sin_h, cos_i, sin_i):
    B, S = q.shape[:2]
    q = apply_rope(q.reshape(B, S, DSA_HEADS, HEAD_DIM), cos_h, sin_h)
    k = apply_rope(k[:, :, None, :], cos_h, sin_h)[:, :, 0]
    qi = apply_rope(qi.reshape(B, S, IDX_HEADS, IDX_DIM), cos_i, sin_i)
    ki = apply_rope(ki[:, :, None, :], cos_i, sin_i)[:, :, 0]
    top_k = min(DSA_TOPK_MAX, S // 4)
    key_pos = jnp.arange(S, dtype=jnp.int32)
    gather = jax.vmap(lambda arr, idx: arr[idx])
    idx_scale = IDX_DIM ** -0.5 * IDX_HEADS ** -0.5

    def block(args):
        q0, qb, qib, wb = args
        qpos = q0 + jnp.arange(Q_BLOCK, dtype=jnp.int32)
        rel = jax.nn.relu(jnp.einsum('bqhd,bsd->bqhs', qib, ki, preferred_element_type=jnp.float32))
        score = jnp.einsum('bqhs,bqh->bqs', rel, wb.astype(jnp.float32)) * idx_scale
        score = jnp.where(key_pos[None, None, :] <= qpos[None, :, None], score, NEG_INF)
        _, sel = lax.top_k(score, top_k)
        k_sel = gather(k, sel)
        v_sel = gather(v, sel)
        valid = sel <= qpos[None, :, None]
        s = jnp.einsum('bqhd,bqkd->bhqk', qb, k_sel, preferred_element_type=jnp.float32) * HEAD_DIM ** -0.5
        s = jnp.where(valid[:, None], s, NEG_INF)
        p = jax.nn.softmax(s, -1).astype(v.dtype)
        return jnp.einsum('bhqk,bqkd->bqhd', p, v_sel)

    o = _from_blocks(lax.map(block, (_block_starts(S), _to_blocks(q), _to_blocks(qi), _to_blocks(wi))))
    return o.reshape(B, S, DSA_HEADS * HEAD_DIM)

def dilated_window_attention(q, k, v, window, dilation):
    S = q.shape[1]
    n_keys = window // dilation + 1
    offs = dilation * jnp.arange(n_keys, dtype=jnp.int32)

    def block(args):
        q0, qb = args
        qpos = q0 + jnp.arange(Q_BLOCK, dtype=jnp.int32)
        idx = qpos[:, None] - offs[None, :]
        valid = idx >= 0
        idx = jnp.maximum(idx, 0)
        k_sel = k[:, idx]
        v_sel = v[:, idx]
        s = jnp.einsum('bqhd,bqkhd->bqhk', qb, k_sel, preferred_element_type=jnp.float32) * HEAD_DIM ** -0.5
        s = jnp.where(valid[None, :, None, :], s, NEG_INF)
        lse = jax.nn.logsumexp(s, -1)
        p = jnp.exp(s - lse[..., None]).astype(v.dtype)
        return jnp.einsum('bqhk,bqkhd->bqhd', p, v_sel), lse

    o, lse = lax.map(block, (_block_starts(S), _to_blocks(q)))
    return _from_blocks(o), _from_blocks(lse)

def dilated_mixer(qkv, cos, sin):
    B, S = qkv.shape[:2]
    n_cfg = len(DIL_CONFIGS)
    qkv = qkv.reshape(B, S, 3, n_cfg * DIL_HEADS, HEAD_DIM)
    q = apply_rope(qkv[:, :, 0], cos, sin)
    k = apply_rope(qkv[:, :, 1], cos, sin)
    v = qkv[:, :, 2]
    outs, lses = [], []
    for g, (window, dilation) in enumerate(DIL_CONFIGS):
        sl = slice(g * DIL_HEADS, (g + 1) * DIL_HEADS)
        o, lse = dilated_window_attention(q[:, :, sl], k[:, :, sl], v[:, :, sl], window, dilation)
        outs.append(o)
        lses.append(lse)
    wts = jax.nn.softmax(jnp.stack(lses, 0), axis=0)
    o = jnp.sum(wts[..., None] * jnp.stack(outs, 0).astype(jnp.float32), 0).astype(qkv.dtype)
    return o.reshape(B, S, DIL_HEADS * HEAD_DIM)

def hybrid_mixer(x, tabs, w_in, q_norm, kv_norm, w_uq, w_ukv, w_o):
    (cos_m, sin_m), (cos_h, sin_h), (cos_i, sin_i) = tabs
    u = jnp.einsum('bsd,dc->bsc', x, w_in)
    cuts = [int(c) for c in np.cumsum(IN_SPLITS)[:-1]]
    a_cq, a_ckv, a_kpe, b_q, b_k, b_v, b_qi, b_ki, b_wi, c_qkv = jnp.split(u, cuts, axis=-1)
    o_a = mla_mixer(a_cq, a_ckv, a_kpe, q_norm, kv_norm, w_uq, w_ukv, cos_m, sin_m)
    o_b = dsa_mixer(b_q, b_k, b_v, b_qi, b_ki, b_wi, cos_h, sin_h, cos_i, sin_i)
    o_c = dilated_mixer(c_qkv, cos_h, sin_h)
    o = jnp.concatenate([o_a, o_b, o_c], -1)
    return jnp.einsum('bsc,cd->bsd', o, w_o)

def hier_moe(x, rg_w, rg_b, re_w, re_b, w_gate, w_up, w_down):
    B, S, D = x.shape
    t = x.reshape(B * S, D)
    lg = jnp.einsum('td,dg->tg', t, rg_w, preferred_element_type=jnp.float32) + rg_b.astype(jnp.float32)
    g_star = jnp.argmax(lg, -1)
    g_hot = jax.nn.one_hot(g_star, N_GROUPS, dtype=jnp.float32)
    p_top = jnp.sum(jax.nn.softmax(lg, -1) * g_hot, -1, keepdims=True)
    le = jnp.einsum('td,gde->tge', t, re_w, preferred_element_type=jnp.float32) + re_b.astype(jnp.float32)
    le = jnp.einsum('tge,tg->te', le, g_hot)
    top_v, top_i = lax.top_k(le, TOP_K_IN_GROUP)
    w_sel = jax.nn.softmax(top_v, -1)
    gate_e = jnp.sum(jax.nn.one_hot(top_i, EXPERTS_PER_GROUP, dtype=jnp.float32) * w_sel[..., None], 1)
    gate = (g_hot[:, :, None] * (p_top * gate_e)[:, None, :]).astype(x.dtype)
    y = jnp.zeros_like(t)
    for g in range(N_GROUPS):
        h = jax.nn.silu(jnp.einsum('td,edf->tef', t, w_gate[g])) * jnp.einsum('td,edf->tef', t, w_up[g])
        y = y + jnp.einsum('tef,efd->td', h * gate[:, g, :, None], w_down[g])
    return y.reshape(B, S, D)

def first_inputs(seed: int = 0) -> dict:
    key = jax.random.key(seed)
    ks = jax.random.split(key, 20)

    def nrm(k, shape, scale):
        return jax.random.normal(k, shape, jnp.float32) * scale

    x = nrm(ks[0], (BATCH, SEQ, D_MODEL), 1.0)
    positions = (jax.random.randint(ks[1], (BATCH, 1), 0, 4096, dtype=jnp.int32)
                 + jnp.arange(SEQ, dtype=jnp.int32)[None, :])
    G, E, F = N_GROUPS, EXPERTS_PER_GROUP, EXPERT_HIDDEN
    return {
        "x": x,
        "positions": positions,
        "w_in": nrm(ks[2], (DEPTH, D_MODEL, IN_COLS), D_MODEL ** -0.5),
        "mla_q_norm": 1.0 + nrm(ks[3], (DEPTH, MLA_Q_RANK), 0.02),
        "mla_kv_norm": 1.0 + nrm(ks[4], (DEPTH, MLA_KV_RANK), 0.02),
        "mla_w_uq": nrm(ks[5], (DEPTH, MLA_Q_RANK, MLA_HEADS * (MLA_NOPE + MLA_ROPE)), MLA_Q_RANK ** -0.5),
        "mla_w_ukv": nrm(ks[6], (DEPTH, MLA_KV_RANK, MLA_HEADS * (MLA_NOPE + MLA_V)), MLA_KV_RANK ** -0.5),
        "w_o": nrm(ks[7], (DEPTH, MIX_WIDTH, D_MODEL), MIX_WIDTH ** -0.5 * DEEPNORM_BETA),
        "ln1_g": 1.0 + nrm(ks[8], (DEPTH, D_MODEL), 0.02),
        "ln1_b": nrm(ks[9], (DEPTH, D_MODEL), 0.02),
        "router_group_w": nrm(ks[10], (DEPTH, D_MODEL, G), D_MODEL ** -0.5),
        "router_group_b": nrm(ks[11], (DEPTH, G), 0.01),
        "router_expert_w": nrm(ks[12], (DEPTH, G, D_MODEL, E), D_MODEL ** -0.5),
        "router_expert_b": nrm(ks[13], (DEPTH, G, E), 0.01),
        "expert_w_gate": nrm(ks[14], (DEPTH, G, E, D_MODEL, F), D_MODEL ** -0.5),
        "expert_w_up": nrm(ks[15], (DEPTH, G, E, D_MODEL, F), D_MODEL ** -0.5),
        "expert_w_down": nrm(ks[16], (DEPTH, G, E, F, D_MODEL), F ** -0.5 * DEEPNORM_BETA),
        "ln2_g": 1.0 + nrm(ks[17], (DEPTH, D_MODEL), 0.02),
        "ln2_b": nrm(ks[18], (DEPTH, D_MODEL), 0.02),
    }

def first_block(x, positions, w_in, mla_q_norm, mla_kv_norm, mla_w_uq, mla_w_ukv, w_o, ln1_g, ln1_b,
              router_group_w, router_group_b, router_expert_w, router_expert_b,
              expert_w_gate, expert_w_up, expert_w_down, ln2_g, ln2_b):
    tabs = (rope_table(positions, MLA_ROPE),
            rope_table(positions, ROT_HEAD_DIMS),
            rope_table(positions, ROT_IDX_DIMS))
    for l in range(DEPTH):
        mix = hybrid_mixer(x, tabs, w_in[l], mla_q_norm[l], mla_kv_norm[l], mla_w_uq[l], mla_w_ukv[l], w_o[l])
        x = layer_norm(DEEPNORM_ALPHA * x + mix, ln1_g[l], ln1_b[l])
        moe = hier_moe(x, router_group_w[l], router_group_b[l], router_expert_w[l], router_expert_b[l],
                       expert_w_gate[l], expert_w_up[l], expert_w_down[l])
        x = layer_norm(DEEPNORM_ALPHA * x + moe, ln2_g[l], ln2_b[l])
    return x


GRID_W = 64
CTX_LEN = 256
N_MIXERS = 3
D_FF = 4 * D_MODEL
DEEPNORM_ALPHA_2 = (2 * DEPTH) ** 0.25
DEEPNORM_BETA_2 = (8 * DEPTH) ** -0.25

GLA_HEADS = 4
GLA_DK = D_MODEL // 2
GLA_DV = D_MODEL
GLA_HK = GLA_DK // GLA_HEADS
GLA_HV = GLA_DV // GLA_HEADS
GLA_RANK = 16
GLA_GATE_NORM = 16.0
GLA_CHUNK = 64
GLA_IN = 2 * GLA_DK + 2 * GLA_DV + 2 * GLA_RANK

SSD_DI = 2 * D_MODEL
SSD_HEADDIM = 64
SSD_HEADS = SSD_DI // SSD_HEADDIM
SSD_GROUPS = 8
SSD_REP = SSD_HEADS // SSD_GROUPS
SSD_STATE = 128
SSD_CONV = 5
SSD_CHUNK = 64
SSD_GN = SSD_GROUPS * SSD_STATE
SSD_CONV_DIM = SSD_DI + 2 * SSD_GN
SSD_IN = SSD_DI + SSD_CONV_DIM + 2 * SSD_HEADS

HY_ORDER = 2
HY_SHORT = 3
HY_EMB = 33
HY_FW = 64
HY_DECAY_TARGET = 1e-2
HY_FAST_DECAY = 0.3
HY_SLOW_DECAY = 1.5
HY_FILTER_GAIN = 0.05


def layer_norm_2(h, g, b):
    hf = h.astype(jnp.float32)
    mu = jnp.mean(hf, -1, keepdims=True)
    var = jnp.mean(jnp.square(hf - mu), -1, keepdims=True)
    return ((hf - mu) * lax.rsqrt(var + LN_EPS) * g + b).astype(h.dtype)

def rms_norm_2(h, g):
    hf = h.astype(jnp.float32)
    return (hf * lax.rsqrt(jnp.mean(hf * hf, -1, keepdims=True) + RMS_EPS) * g).astype(h.dtype)

def modulate(h, shift, scale):
    return h * (1 + scale) + shift

def snake(h):
    b, l, ch = h.shape
    rows = l // GRID_W
    g = h.reshape(b, rows, GRID_W, ch)
    odd = (jnp.arange(rows) % 2 == 1)[None, :, None, None]
    return jnp.where(odd, g[:, :, ::-1], g).reshape(b, l, ch)

def dwconv(u, w, bias):
    k, ch = w.shape
    out = lax.conv_general_dilated(u, w.astype(u.dtype)[:, None, :], window_strides=(1,),
                                   padding=[(k // 2, k // 2)],
                                   dimension_numbers=('NWC', 'WIO', 'NWC'),
                                   feature_group_count=ch)
    return out + bias

def to_heads(t, dh):
    b, l, _ = t.shape
    return t.reshape(b, l, -1, dh).transpose(0, 2, 1, 3)

def sq_relu_mlp(h, w1, w2):
    return jnp.square(jax.nn.relu(h @ w1)) @ w2

def gla_chunk_scan(q, k, v, log_a, s0):
    b, h, l, _ = q.shape
    nc = l // GLA_CHUNK

    def chunks(t):
        return jnp.moveaxis(t.reshape(b, h, nc, GLA_CHUNK, t.shape[-1]), 2, 0)

    mask = jnp.tril(jnp.ones((GLA_CHUNK, GLA_CHUNK), dtype=bool))[:, :, None]

    def step(s, inp):
        qi, ki, vi, gi = inp
        cum = jnp.cumsum(gi, axis=2)
        diff = cum[:, :, :, None, :] - cum[:, :, None, :, :]
        decay = jnp.exp(jnp.where(mask, diff, -jnp.inf))
        attn = jnp.einsum('bhid,bhjd,bhijd->bhij', qi, ki, decay)
        o = jnp.einsum('bhij,bhjv->bhiv', attn, vi) + jnp.einsum('bhid,bhdv->bhiv', qi * jnp.exp(cum), s)
        last = cum[:, :, -1:, :]
        s_new = s * jnp.exp(last[:, :, 0, :, None]) + jnp.einsum('bhjd,bhjv->bhdv', ki * jnp.exp(last - cum), vi)
        return s_new, o

    s_fin, oc = lax.scan(step, s0, tuple(map(chunks, (q, k, v, log_a))))
    return jnp.moveaxis(oc, 0, 2).reshape(b, h, l, v.shape[-1]), s_fin

def gla_mixer(uc, ul, w_in, w_a2, b_a2, norm_g, w_out, need_ctx):
    split_at = [GLA_DK, 2 * GLA_DK, 2 * GLA_DK + GLA_DV, 2 * GLA_DK + 2 * GLA_DV]

    def run(h, s_init, need_y):
        b, l, _ = h.shape
        q, k, v, g, a = jnp.split(h @ w_in, split_at, axis=-1)
        q = to_heads(q, GLA_HK) * GLA_HK ** -0.5
        k = to_heads(k, GLA_HK)
        v = to_heads(v, GLA_HV)
        logit = jnp.einsum('blzr,zrd->zbld', a.reshape(b, l, 2, GLA_RANK), w_a2) + b_a2[:, None, None, :]
        log_a = jax.nn.log_sigmoid(logit.astype(jnp.float32)) / GLA_GATE_NORM
        o_f, s_f = gla_chunk_scan(q, k, v, to_heads(log_a[0], GLA_HK), s_init[0])
        o_b, s_b = gla_chunk_scan(q[:, :, ::-1], k[:, :, ::-1], v[:, :, ::-1],
                                  to_heads(log_a[1], GLA_HK)[:, :, ::-1], s_init[1])
        if not need_y:
            return None, (s_f, s_b)
        o = rms_norm_2(o_f + o_b[:, :, ::-1], norm_g)
        o = o.transpose(0, 2, 1, 3).reshape(b, l, GLA_DV)
        return (o * jax.nn.silu(g)) @ w_out, (s_f, s_b)

    zeros = jnp.zeros((uc.shape[0], GLA_HEADS, GLA_HK, GLA_HV), jnp.float32)
    yc, ctx_states = run(uc, (zeros, zeros), need_ctx)
    yl, _ = run(ul, ctx_states, True)
    return yc, yl

def ssd_chunk_scan(xs, dt, a, bm, cm, s0):
    b, l = xs.shape[:2]
    nc = l // SSD_CHUNK

    def chunks(t):
        return jnp.moveaxis(t.reshape(b, nc, SSD_CHUNK, *t.shape[2:]), 1, 0)

    mask = jnp.tril(jnp.ones((SSD_CHUNK, SSD_CHUNK), dtype=bool))[None, :, :, None, None]

    def step(s, inp):
        xi, dti, bi, ci = inp
        cum = jnp.cumsum(dti * a, axis=1)
        seg = cum[:, :, None] - cum[:, None, :]
        decay = jnp.exp(jnp.where(mask, seg, -jnp.inf))
        xdt = xi * dti[..., None]
        cb = jnp.einsum('bign,bjgn->bijg', ci, bi)
        y = jnp.einsum('bijg,bijgr,bjgrp->bigrp', cb, decay, xdt)
        y = y + jnp.einsum('bign,bigr,bgrpn->bigrp', ci, jnp.exp(cum), s)
        last = cum[:, -1]
        s_new = s * jnp.exp(last)[..., None, None] + jnp.einsum(
            'bjgn,bjgr,bjgrp->bgrpn', bi, jnp.exp(last[:, None] - cum), xdt)
        return s_new, y

    s_fin, ys = lax.scan(step, s0, tuple(map(chunks, (xs, dt, bm, cm))))
    return jnp.moveaxis(ys, 0, 1).reshape(xs.shape), s_fin

def ssd_mixer(uc, ul, w_in, conv_w, conv_b, dt_bias, a_log, d_skip, norm_g, w_out, need_ctx):
    a = (-jnp.exp(a_log.astype(jnp.float32))).reshape(2, SSD_GROUPS, SSD_REP)
    d_gr = d_skip.reshape(SSD_GROUPS, SSD_REP, 1)

    def run(h, s_init, need_y):
        b, l, _ = h.shape
        z, xbc, dt = jnp.split(h @ w_in, [SSD_DI, SSD_DI + SSD_CONV_DIM], axis=-1)
        xbc = jax.nn.silu(dwconv(xbc, conv_w, conv_b))
        xs, bm, cm = jnp.split(xbc, [SSD_DI, SSD_DI + SSD_GN], axis=-1)
        xs = xs.reshape(b, l, SSD_GROUPS, SSD_REP, SSD_HEADDIM)
        bm = bm.reshape(b, l, SSD_GROUPS, SSD_STATE)
        cm = cm.reshape(b, l, SSD_GROUPS, SSD_STATE)
        dt = jax.nn.softplus(dt.astype(jnp.float32).reshape(b, l, 2, SSD_GROUPS, SSD_REP)
                             + dt_bias.reshape(2, SSD_GROUPS, SSD_REP))
        y_f, s_f = ssd_chunk_scan(xs, dt[:, :, 0], a[0], bm, cm, s_init[0])
        y_b, s_b = ssd_chunk_scan(xs[:, ::-1], dt[:, ::-1, 1], a[1], bm[:, ::-1], cm[:, ::-1], s_init[1])
        if not need_y:
            return None, (s_f, s_b)
        y = (y_f + y_b[:, ::-1] + xs * d_gr).reshape(b, l, SSD_DI)
        return rms_norm_2(y * jax.nn.silu(z), norm_g) @ w_out, (s_f, s_b)

    zeros = jnp.zeros((uc.shape[0], SSD_GROUPS, SSD_REP, SSD_HEADDIM, SSD_STATE), jnp.float32)
    yc, ctx_states = run(uc, (zeros, zeros), need_ctx)
    yl, _ = run(ul, ctx_states, True)
    return yc, yl

def hyena_pos_emb(l):
    bands = (HY_EMB - 1) // 2
    t = jnp.linspace(0.0, 1.0, l)[:, None]
    w = 2 * math.pi * jnp.arange(l, dtype=jnp.float32)[:, None] / l
    ang = jnp.linspace(1e-4, bands - 1, bands)[None, :] * w
    return jnp.concatenate([t, jnp.cos(ang), -jnp.sin(ang)], axis=-1)

def hyena_filters(l, f_w1, f_b1, f_w2, f_b2, f_w3, f_b3, f_w4, f_freq):
    act = lambda t: jnp.sin(f_freq * t)
    hh = act(hyena_pos_emb(l) @ f_w1 + f_b1)
    hh = act(hh @ f_w2 + f_b2)
    hh = act(hh @ f_w3 + f_b3)
    hh = (hh @ f_w4).reshape(l, HY_ORDER, 2, D_MODEL)
    t = jnp.linspace(0.0, 1.0, l)[:, None]
    deltas = jnp.abs(jnp.linspace(math.log(HY_DECAY_TARGET) / HY_FAST_DECAY,
                                  math.log(HY_DECAY_TARGET) / HY_SLOW_DECAY, D_MODEL))
    hh = hh * jnp.exp(-t * deltas)[:, None, None, :]
    fwd, bwd = hh[:, :, 0], hh[:, :, 1]
    return jnp.concatenate([fwd, jnp.zeros_like(fwd[:1]), bwd[:0:-1]], axis=0)

def fft_long_conv(u, h2l, bias):
    l = u.shape[1]
    uf = jnp.fft.rfft(u.astype(jnp.float32), n=2 * l, axis=1)
    hf = jnp.fft.rfft(h2l.astype(jnp.float32), n=2 * l, axis=0)
    y = jnp.fft.irfft(uf * hf, n=2 * l, axis=1)[:, :l]
    return (y + u * bias).astype(u.dtype)

def hyena_mixer(uc, ul, w_in, conv_w, conv_b, f_w1, f_b1, f_w2, f_b2, f_w3, f_b3, f_w4, f_freq,
                h_bias, w_out, need_ctx):
    def run(h):
        l = h.shape[1]
        v, x1, x2 = jnp.split(dwconv(h @ w_in, conv_w, conv_b), 3, axis=-1)
        filt = hyena_filters(l, f_w1, f_b1, f_w2, f_b2, f_w3, f_b3, f_w4, f_freq)
        z = x1 * fft_long_conv(v, filt[:, 0], h_bias[0])
        return (x2 * fft_long_conv(z, filt[:, 1], h_bias[1])) @ w_out

    yc = run(uc) if need_ctx else None
    return yc, run(ul)

def second_inputs(seed: int = 0) -> dict:
    key = jax.random.key(seed)
    ks = iter(jax.random.split(key, 40))
    nrm = lambda shape, s: jax.random.normal(next(ks), shape, jnp.float32) * s
    uni = lambda shape, lo, hi: jax.random.uniform(next(ks), shape, jnp.float32, minval=lo, maxval=hi)
    inv_softplus = lambda y: y + jnp.log(-jnp.expm1(-y))
    D = D_MODEL
    ng, ns, nh = (len(range(m, DEPTH, N_MIXERS)) for m in range(N_MIXERS))
    return {
        'x': nrm((BATCH, SEQ, D), 1.0),
        'c': nrm((BATCH, D), 1.0),
        'ctx': nrm((BATCH, CTX_LEN, D), 1.0),
        'c_ctx': nrm((D,), 1.0),
        'ada_w': nrm((DEPTH, D, 6 * D), D ** -0.5),
        'ada_b': nrm((DEPTH, 6 * D), 0.02),
        'ln_g': 1.0 + nrm((DEPTH, 2, D), 0.02),
        'ln_b': nrm((DEPTH, 2, D), 0.02),
        'ffn_w1': nrm((DEPTH, D, D_FF), D ** -0.5),
        'ffn_w2': nrm((DEPTH, D_FF, D), D_FF ** -0.5 * DEEPNORM_BETA_2),
        'gla_w_in': nrm((ng, D, GLA_IN), D ** -0.5),
        'gla_w_a2': nrm((ng, 2, GLA_RANK, GLA_DK), GLA_RANK ** -0.5),
        'gla_b_a2': nrm((ng, 2, GLA_DK), 0.1),
        'gla_norm': 1.0 + nrm((ng, GLA_HV), 0.02),
        'gla_w_out': nrm((ng, GLA_DV, D), GLA_DV ** -0.5 * DEEPNORM_BETA_2),
        'ssd_w_in': nrm((ns, D, SSD_IN), D ** -0.5),
        'ssd_conv_w': nrm((ns, SSD_CONV, SSD_CONV_DIM), SSD_CONV ** -0.5),
        'ssd_conv_b': nrm((ns, SSD_CONV_DIM), 0.02),
        'ssd_dt_bias': inv_softplus(jnp.exp(uni((ns, 2, SSD_HEADS), math.log(1e-3), math.log(1e-1)))),
        'ssd_a_log': jnp.log(uni((ns, 2, SSD_HEADS), 1.0, 16.0)),
        'ssd_d': 1.0 + nrm((ns, SSD_HEADS), 0.1),
        'ssd_norm': 1.0 + nrm((ns, SSD_DI), 0.02),
        'ssd_w_out': nrm((ns, SSD_DI, D), SSD_DI ** -0.5 * DEEPNORM_BETA_2),
        'hy_w_in': nrm((nh, D, 3 * D), D ** -0.5),
        'hy_conv_w': nrm((nh, HY_SHORT, 3 * D), HY_SHORT ** -0.5),
        'hy_conv_b': nrm((nh, 3 * D), 0.02),
        'hy_f_w1': nrm((nh, HY_EMB, HY_FW), HY_EMB ** -0.5),
        'hy_f_b1': nrm((nh, HY_FW), 0.1),
        'hy_f_w2': nrm((nh, HY_FW, HY_FW), HY_FW ** -0.5),
        'hy_f_b2': nrm((nh, HY_FW), 0.1),
        'hy_f_w3': nrm((nh, HY_FW, HY_FW), HY_FW ** -0.5),
        'hy_f_b3': nrm((nh, HY_FW), 0.1),
        'hy_f_w4': nrm((nh, HY_FW, HY_ORDER * 2 * D), HY_FW ** -0.5 * HY_FILTER_GAIN),
        'hy_f_freq': 1.0 + nrm((nh, HY_FW), 0.1),
        'hy_bias': nrm((nh, HY_ORDER, D), 1.0),
        'hy_w_out': nrm((nh, D, D), D ** -0.5 * DEEPNORM_BETA_2),
    }

def second_block(x, c, ctx, c_ctx, ada_w, ada_b, ln_g, ln_b, ffn_w1, ffn_w2,
              gla_w_in, gla_w_a2, gla_b_a2, gla_norm, gla_w_out,
              ssd_w_in, ssd_conv_w, ssd_conv_b, ssd_dt_bias, ssd_a_log, ssd_d, ssd_norm, ssd_w_out,
              hy_w_in, hy_conv_w, hy_conv_b, hy_f_w1, hy_f_b1, hy_f_w2, hy_f_b2, hy_f_w3, hy_f_b3,
              hy_f_w4, hy_f_freq, hy_bias, hy_w_out):
    hl, hc = x, ctx
    s_lat = jax.nn.silu(c)
    s_ctx = jax.nn.silu(c_ctx)
    for i in range(DEPTH):
        kind, j = i % N_MIXERS, i // N_MIXERS
        need_ctx = i < DEPTH - 1
        m_l = jnp.split((s_lat @ ada_w[i] + ada_b[i])[:, None, :], 6, axis=-1)
        m_c = jnp.split(s_ctx @ ada_w[i] + ada_b[i], 6, axis=-1)
        ul = snake(modulate(hl, m_l[0], m_l[1]))
        uc = modulate(hc, m_c[0], m_c[1])
        if kind == 0:
            yc, yl = gla_mixer(uc, ul, gla_w_in[j], gla_w_a2[j], gla_b_a2[j], gla_norm[j], gla_w_out[j], need_ctx)
        elif kind == 1:
            yc, yl = ssd_mixer(uc, ul, ssd_w_in[j], ssd_conv_w[j], ssd_conv_b[j], ssd_dt_bias[j],
                               ssd_a_log[j], ssd_d[j], ssd_norm[j], ssd_w_out[j], need_ctx)
        else:
            yc, yl = hyena_mixer(uc, ul, hy_w_in[j], hy_conv_w[j], hy_conv_b[j], hy_f_w1[j], hy_f_b1[j],
                                 hy_f_w2[j], hy_f_b2[j], hy_f_w3[j], hy_f_b3[j], hy_f_w4[j], hy_f_freq[j],
                                 hy_bias[j], hy_w_out[j], need_ctx)
        hl = layer_norm_2(DEEPNORM_ALPHA_2 * hl + m_l[2] * snake(yl), ln_g[i, 0], ln_b[i, 0])
        hl = layer_norm_2(DEEPNORM_ALPHA_2 * hl + m_l[5] * sq_relu_mlp(modulate(hl, m_l[3], m_l[4]), ffn_w1[i], ffn_w2[i]),
                        ln_g[i, 1], ln_b[i, 1])
        if need_ctx:
            hc = layer_norm_2(DEEPNORM_ALPHA_2 * hc + m_c[2] * yc, ln_g[i, 0], ln_b[i, 0])
            hc = layer_norm_2(DEEPNORM_ALPHA_2 * hc + m_c[5] * sq_relu_mlp(modulate(hc, m_c[3], m_c[4]), ffn_w1[i], ffn_w2[i]),
                            ln_g[i, 1], ln_b[i, 1])
    return hl


def setup_inputs(seed=0):
    out = dict(first_inputs(seed))
    for name, value in second_inputs(seed + 1).items():
        if name != "x":
            out[name + "_2"] = value
    return out


def reference(
    x, positions, w_in, mla_q_norm, mla_kv_norm, mla_w_uq, mla_w_ukv, w_o, ln1_g, ln1_b,
    router_group_w, router_group_b, router_expert_w, router_expert_b, expert_w_gate,
    expert_w_up, expert_w_down, ln2_g, ln2_b, c_2, ctx_2, c_ctx_2, ada_w_2, ada_b_2, ln_g_2,
    ln_b_2, ffn_w1_2, ffn_w2_2, gla_w_in_2, gla_w_a2_2, gla_b_a2_2, gla_norm_2, gla_w_out_2,
    ssd_w_in_2, ssd_conv_w_2, ssd_conv_b_2, ssd_dt_bias_2, ssd_a_log_2, ssd_d_2, ssd_norm_2,
    ssd_w_out_2, hy_w_in_2, hy_conv_w_2, hy_conv_b_2, hy_f_w1_2, hy_f_b1_2, hy_f_w2_2,
    hy_f_b2_2, hy_f_w3_2, hy_f_b3_2, hy_f_w4_2, hy_f_freq_2, hy_bias_2, hy_w_out_2,
):
    x = first_block(
        x, positions, w_in, mla_q_norm, mla_kv_norm, mla_w_uq, mla_w_ukv, w_o, ln1_g, ln1_b,
        router_group_w, router_group_b, router_expert_w, router_expert_b, expert_w_gate,
        expert_w_up, expert_w_down, ln2_g, ln2_b,
    )
    return second_block(
        x, c_2, ctx_2, c_ctx_2, ada_w_2, ada_b_2, ln_g_2, ln_b_2, ffn_w1_2, ffn_w2_2,
        gla_w_in_2, gla_w_a2_2, gla_b_a2_2, gla_norm_2, gla_w_out_2, ssd_w_in_2, ssd_conv_w_2,
        ssd_conv_b_2, ssd_dt_bias_2, ssd_a_log_2, ssd_d_2, ssd_norm_2, ssd_w_out_2, hy_w_in_2,
        hy_conv_w_2, hy_conv_b_2, hy_f_w1_2, hy_f_b1_2, hy_f_w2_2, hy_f_b2_2, hy_f_w3_2,
        hy_f_b3_2, hy_f_w4_2, hy_f_freq_2, hy_bias_2, hy_w_out_2,
    )


_drawn_inputs = setup_inputs


def setup_inputs(seed=0):
    import zlib

    import numpy as np

    out = dict(_drawn_inputs(seed))
    spreads = {}
    factors = {'mla_q_norm': 8.0,
     'mla_kv_norm': 8.0,
     'router_group_b': 8.0,
     'router_expert_b': 7.84,
     'gla_b_a2_2': 5.053,
     'gla_norm_2': 23.309,
     'ssd_conv_b_2': 8.0,
     'ssd_d_2': 8.0,
     'ssd_norm_2': 27.277}
    for name, (base, spread) in spreads.items():
        noise = np.random.default_rng([zlib.crc32(name.encode()), seed]).standard_normal(out[name].shape)
        drawn = base * np.exp(spread * noise) if base else spread * noise
        out[name] = __import__('jax').numpy.asarray(drawn.astype(out[name].dtype))
    for name, factor in factors.items():
        out[name] = (out[name] * factor).astype(out[name].dtype)
    return out
```

```python
import math
from contextlib import ExitStack

import numpy as np
import concourse.bass as bass
from concourse import mybir

F32 = mybir.dt.float32
I32 = mybir.dt.int32
ALU = mybir.AluOpType
ACT = mybir.ActivationFunctionType
AX = mybir.AxisListType.X

P = 128
D = 1024
KT = D // P
SEQ = 256
TT = SEQ // P
DEPTH = 2
ALPHA = (2.0 * DEPTH) ** 0.25
LN_EPS, RMS_EPS = 1e-5, 1e-6
NEG = -1e30
TAKEN = -3e38

MLA_H, QR, KVR, NOPE, ROPE = 8, 256, 128, 64, 32
HD, IDX_H, IDX_D, TOPK = 64, 8, 32, 64
C_CQ, C_CKV, C_KPE = 0, 256, 384
C_BQ, C_BK, C_BV, C_QI, C_KI, C_WI, C_DIL = 416, 672, 736, 800, 1056, 1088, 1096
IN_COLS = 3400
DIL_COLS = 12 * HD
CHUNK = 512
N_IN = -(-IN_COLS // CHUNK)
QH = NOPE + ROPE
GROUPS, EXP_PER, NEXP, EH = 4, 8, 32, 256
NROUT = GROUPS + NEXP

HALF_M, HALF_H, HALF_I = 16, 8, 4
NFREQ = HALF_M + HALF_H + HALF_I


def host_constants():
    out = {}
    out["ident"] = np.eye(P, dtype=np.float32)
    perm = np.zeros((P, P), np.float32)
    for i in range(P):
        perm[(i if i < 64 else 191 - i), i] = 1.0
    out["snake"] = perm
    q = np.arange(P)[:, None]
    masks = np.zeros((P, 4, 3 * P), np.float32)
    for t in range(TT):
        k = np.arange((t + 1) * P)[None, :]
        diff = q + t * P - k
        kinds = [diff >= 0, (diff >= 0) & (diff <= 128), (diff >= 0) & (diff % 4 == 0), (diff >= 0) & (diff % 16 == 0)]
        for n, ok in enumerate(kinds):
            masks[:, n, (P if t else 0):(3 * P if t else P)] = np.where(ok, 0.0, NEG)
    out["masks"] = masks
    freqs = []
    for half in (HALF_M, HALF_H, HALF_I):
        rot = 2 * half
        freqs.append(np.float32(500000.0) ** (-np.arange(0, rot, 2, dtype=np.float32) / np.float32(rot)))
    out["freqs"] = np.concatenate(freqs).astype(np.float32)
    out["ramp"] = np.arange(8, 0, -1).astype(np.float32)
    return out


def bc(ap, axis, n):
    v = ap.unsqueeze(axis)
    shape = list(v.shape)
    shape[axis] = n
    return v.broadcast_to(shape)


class Ring:

    def __init__(self, full, empty):
        self.full, self.empty = full, empty
        self.uses = [0] * 8
        self.at = {}

    def plan(self, key, bank):
        self.at[key] = (bank, self.uses[bank])
        self.uses[bank] += 1

    def bank(self, key):
        return self.at[key][0]

    def claim(self, eng, key, l=0, step=0):
        b, i = self.at[key]
        eng.wait_ge(self.empty[b], l * self.uses[b] + (i + 1) + step)

    def filled(self, eng, key, l=0, step=0):
        b, i = self.at[key]
        eng.wait_ge(self.full[b], l * self.uses[b] + (i + 2) + step)

    def read(self, eng, key, l=0, step=0):
        b, i = self.at[key]
        eng.wait_ge(self.empty[b], l * self.uses[b] + (i + 2) + step)

    def fill_done(self, ins, key):
        ins.then_inc(self.full[self.at[key][0]], 1)

    def read_done(self, ins, key):
        ins.then_inc(self.empty[self.at[key][0]], 1)


def plan_block1(full, empty):
    r = Ring(full, empty)
    keys = [("xT", t, h) for t in range(TT) for h in range(2)]
    keys += [("u", c, t) for c in range(N_IN) for t in range(TT)]
    keys += [("cT", t) for t in range(TT)]
    keys += [("q", n, t) for n in range(2) for t in range(TT)]
    keys += [("kv", n, t) for n in range(2) for t in range(TT)]
    keys += [("qiT", t, h) for t in range(TT) for h in range(2)] + [("kiT",)]
    keys += [("rel", 0, j) for j in range(2)] + [("rel", 1, j) for j in range(4)]
    for u in range(-1, 12):
        g2, t2 = divmod(u + 1, 2)
        if u < 11:
            if t2 == 0:
                keys += [("qT", g2, 0), ("qT", g2, 1), ("kT", g2, 0)] + ([("kT", g2, 1)] if g2 < 5 else [])
            keys += [("s", u + 1, j) for j in range(t2 + 1)]
        if u >= 0:
            keys += [("pT", u, j) for j in range(u % 2 + 1)] + [("o", u)]
    keys += [("oT", t, h) for t in range(TT) for h in range(2)]
    keys += [("mix", n, t) for n in range(2) for t in range(TT)]
    keys += [("x2T", t, h) for t in range(TT) for h in range(2)]
    keys += [("rout", t) for t in range(TT)] + [("gT",)]
    for n, k in enumerate(keys):
        r.plan(k, n % 8)
    for t in range(TT):
        for n in range(2):
            r.plan(("y", t, n), 2 * t + n)
    for e in range(NEXP):
        r.plan(("gate", e), 4 + 2 * (e % 2))
        r.plan(("up", e), 5 + 2 * (e % 2))
    return r


def block1(nc, io, c, X, dram_gate):
    with ExitStack() as ctx:
        def sb(name, shape, dt=F32):
            return ctx.enter_context(nc.sbuf_tensor(name, shape, dt))

        def sem(name):
            return ctx.enter_context(nc.semaphore(name))

        ident, tab = c["ident"], c["tab"]
        bank = c["banks"]
        XT = sb("XT", [P, KT, SEQ])
        U = sb("U", [P, TT, IN_COLS])
        WD = sb("WD", [P, 2, KT, CHUNK])
        EW = sb("EW", [P, 2, 6144])
        QT = sb("QT", [P, 2, 4, SEQ])
        KTt = sb("KTt", [P, 2, 4, SEQ])
        PR = sb("PR", [P, 2, 4, SEQ])
        PT = sb("PT", [P, 2, 4, SEQ])
        REL = sb("REL", [P, IDX_H, SEQ])
        QIT = sb("QIT", [IDX_D, IDX_H, SEQ])
        KIT = sb("KIT", [IDX_D, SEQ])
        MASK = sb("MASK", [P, 4, 3 * P])
        DMASK = sb("DMASK", [P, 3 * P])
        O = sb("O", [P, TT, D])
        OG = REL[:].rearrange("p h n -> p (h n)")[:, 0:1536].rearrange("p (t g n) -> p t g n", t=TT, g=3)
        RW = sb("RW", [P, KT, NROUT])
        RB = sb("RB", [P, NROUT])
        GN = sb("GN", [P, QR + KVR])
        MX = sb("MX", [P, 12, 4])
        SM = sb("SM", [P, 12, 4])
        ST = sb("ST", [P, 64])
        M8 = sb("M8", [P, 8])
        DW = sb("DW", [P, 3, TT, 3, 4])
        RT = sb("RT", [P, 6, TT, NROUT])
        GTT = sb("GTT", [NEXP, SEQ])
        BN = sb("BN", [P, TT, 2, 6])
        MV = sb("MV", [P, TT, 2])
        QM = EW[:, 1, 0:1536].rearrange("p (t n) -> p t n", t=TT)
        KM = EW[:, 1, 1536:3072].rearrange("p (t h n) -> p t h n", t=TT, h=MLA_H)
        VM = EW[:, 1, 3072:4096].rearrange("p (t n) -> p t n", t=TT)
        CQN = EW[:, 1, 4096:4864].rearrange("p (t n) -> p t n", t=TT)
        CQT = EW[:, 1, 4864:5632].rearrange("p (k n) -> p k n", k=3)
        LN1 = U[:, 0, 0:2 * D].rearrange("p (a n) -> p a n", a=2)
        LN2 = U[:, 1, 0:2 * D].rearrange("p (a n) -> p a n", a=2)
        SG = [U[:, 0, 2048:2560], U[:, 0, 2560:3072]]
        H = [U[:, 1, 2048:2560], U[:, 1, 2560:3072]]
        GB = [U[:, 0, 3072:3328], U[:, 1, 3072:3328]]

        full = [sem(f"a_full{b}") for b in range(8)]
        empty = [sem(f"a_empty{b}") for b in range(8)]
        r = plan_block1(full, empty)
        w_in = [sem(f"a_dense_landed{s}") for s in range(2)]
        gu_in = [sem(f"a_gateup_landed{s}") for s in range(2)]
        dn_in = [sem(f"a_down_landed{s}") for s in range(2)]
        dn_done = sem("a_down_used")
        consts_in = sem("a_layer_consts")
        ln_in = sem("a_ln_params")
        mask_in = sem("a_masks")
        cqn = sem("a_latents_normed")
        rope_b = sem("a_sparse_roped")
        rope_c = sem("a_dilated_roped")
        rope_q = sem("a_mla_roped")
        sc0 = sem("a_index_scored")
        smax = sem("a_scores_max")
        pexp = sem("a_probs")
        dilm = sem("a_dilated_max")
        dile = sem("a_dilated_exp")
        sq_in, sq_out = sem("a_var"), sem("a_std")
        o_ready = sem("a_mixed_ready")
        x_ready = sem("a_x_ready")
        rexp_in, rexp_out = sem("a_router_logits"), sem("a_router_exp")
        gate_rdy = sem("a_gates")
        gate_st = sem("a_gates_stored")
        gb_in = [sem(f"a_gate_row_landed{s}") for s in range(2)]
        h_rdy = sem("a_hidden_ready")
        start = sem("a_counters_started")

        gate_w = io["expert_w_gate"].rearrange("l g e (k p) f -> (l g e) p k f", p=P)
        up_w = io["expert_w_up"].rearrange("l g e (k p) f -> (l g e) p k f", p=P)
        down_w = io["expert_w_down"].rearrange("l g e (k p) n -> (l g e) p k n", p=P)

        def one(ap):
            return ap.rearrange("o p k n -> (o p) k n")

        block = ctx.enter_context(nc.Block())

        def chunk_src(l, n, half):
            if n < N_IN:
                c0, c1 = n * CHUNK, min(IN_COLS, (n + 1) * CHUNK)
                src = io["w_in"].rearrange("l (k p) n -> l p k n", p=P)[bass.ds(l, 1), :, 4 * half:4 * half + 4, c0:c1]
                return one(src), WD[:, n % 2, 4 * half:4 * half + 4, 0:c1 - c0]
            if n == N_IN:
                flat = WD[:, n % 2, :, :].rearrange("p k n -> p (k n)")
                if half == 0:
                    return (one(io["mla_w_uq"].rearrange("l (k p) n -> l p k n", p=P)[bass.ds(l, 1)]),
                            flat[:, 0:1536].rearrange("p (k n) -> p k n", k=2))
                return (one(io["mla_w_ukv"].rearrange("l (k p) n -> l p k n", p=P)[bass.ds(l, 1)]),
                        flat[:, 1536:2560].rearrange("p (k n) -> p k n", k=1))
            n0 = (n - N_IN - 1) * CHUNK
            src = io["w_o"].rearrange("l (k p) n -> l p k n", p=P)[bass.ds(l, 1), :, 4 * half:4 * half + 4, n0:n0 + CHUNK]
            return one(src), WD[:, n % 2, 4 * half:4 * half + 4, :]

        NCH = N_IN + 3
        last_use = [("u", n, 1) for n in range(N_IN)] + [("kv", 1, 1)] + [("mix", n, 1) for n in range(2)]

        @block.sync
        def _(sp):
            for s in full + empty + [dn_done, dn_done, h_rdy, h_rdy]:
                sp.sem_inc(s, 1)
            sp.sem_inc(start, 1)
            sp.dma_start(MASK[:], io["masks"]).then_inc(mask_in, 16)

            def expert(l, e, s):
                idx = l * NEXP + e
                sp.dma_start(EW[:, s, 0:2048].rearrange("p (k n) -> p k n", k=KT),
                             one(gate_w[bass.ds(idx, 1)])).then_inc(gu_in[s], 16)
                sp.dma_start(EW[:, s, 2048:4096].rearrange("p (k n) -> p k n", k=KT),
                             one(up_w[bass.ds(idx, 1)])).then_inc(gu_in[s], 16)

            def expert_down(l, e, s):
                idx = l * NEXP + e
                sp.dma_start(EW[:, s, 4096:6144].rearrange("p (k n) -> p k n", k=2),
                             one(down_w[bass.ds(idx, 1)])).then_inc(dn_in[s], 16)

            with sp.Fori(0, DEPTH, 1) as l:
                for n in range(NCH):
                    if n >= 2:
                        r.filled(sp, last_use[n - 2], l)
                    for half in range(2):
                        src, dst = chunk_src(l, n, half)
                        sp.dma_start(dst, src).then_inc(w_in[n % 2], 16)
                sp.wait_ge(dn_done, l * NEXP + 2)
                expert(l, 0, 0)
                expert_down(l, 0, 0)
                r.filled(sp, ("o", 11), l)
                expert(l, 1, 1)
                expert_down(l, 1, 1)
                with sp.Fori(0, NEXP // 2 - 1, 1) as i:
                    for s in range(2):
                        r.filled(sp, ("up", s), l, i)
                        expert(l, 2 * i + 2 + s, s)
                        sp.wait_ge(dn_done, l * NEXP + 2 * i + (s + 3))
                        expert_down(l, 2 * i + 2 + s, s)

        @block.gpsimd
        def _(pool):
            pool.wait_ge(start, 1)
            with pool.Fori(0, DEPTH, 1) as l:
                lay = bass.ds(l, 1)
                pool.wait_ge(dn_done, l * NEXP + 2)
                pool.nop(nofuse=True)
                pool.dma_start(GN[:, 0:QR].unsqueeze(1), io["mla_q_norm"][lay, :].partition_broadcast(P)).then_inc(consts_in, 16)
                pool.dma_start(GN[:, QR:QR + KVR].unsqueeze(1), io["mla_kv_norm"][lay, :].partition_broadcast(P)).then_inc(consts_in, 16)
                pool.dma_start(RW[:, :, 0:GROUPS],
                               one(io["router_group_w"].rearrange("l (k p) g -> l p k g", p=P)[lay])).then_inc(consts_in, 16)
                for g in range(GROUPS):
                    pool.dma_start(RW[:, :, GROUPS + 8 * g:GROUPS + 8 * g + 8],
                                   one(io["router_expert_w"].rearrange("l g (k p) e -> l g p k e", p=P)[lay, g])).then_inc(consts_in, 16)
                pool.dma_start(RB[:, 0:GROUPS].unsqueeze(1), io["router_group_b"][lay, :].partition_broadcast(P)).then_inc(consts_in, 16)
                pool.dma_start(RB[:, GROUPS:].unsqueeze(1),
                               io["router_expert_b"].rearrange("l g e -> l (g e)")[lay, :].partition_broadcast(P)).then_inc(consts_in, 16)
                r.filled(pool, ("o", 11), l)
                pool.nop(nofuse=True)
                for n, name in enumerate(("ln1_g", "ln1_b")):
                    pool.dma_start(LN1[:, n, :].unsqueeze(1), io[name][lay, :].partition_broadcast(P)).then_inc(ln_in, 16)
                for n, name in enumerate(("ln2_g", "ln2_b")):
                    pool.dma_start(LN2[:, n, :].unsqueeze(1), io[name][lay, :].partition_broadcast(P)).then_inc(ln_in, 16)
                r.read(pool, ("gT",), l)
                pool.nop(nofuse=True)
                pool.dma_start(dram_gate[lay].rearrange("o e n -> (o e) n"), GTT[:]).then_inc(gate_st, 16)
                pool.wait_ge(gate_st, l * 16 + 16)
                pool.nop(nofuse=True)
                for s in range(2):
                    pool.dma_start(GB[s].unsqueeze(1), dram_gate[lay, s, :].partition_broadcast(P)).then_inc(gb_in[s], 16)
                with pool.Fori(0, NEXP // 2 - 1, 1) as i:
                    for s in range(2):
                        pool.wait_ge(h_rdy, l * NEXP + 2 * i + (s + 3))
                        pool.nop(nofuse=True)
                        pool.dma_start(GB[s].unsqueeze(1),
                                       dram_gate.rearrange("l e n -> (l e) n")[bass.ds(l * NEXP + 2 * i + (s + 2), 1), :]
                                       .partition_broadcast(P)).then_inc(gb_in[s], 16)

        @block.tensor
        def _(pe):
            pe.wait_ge(start, 1)

            def turn(l, key, blocks, step=P):
                r.claim(pe, key, l)
                pe.nop(nofuse=True)
                for j, src in enumerate(blocks):
                    m = src.shape[1]
                    last = nc.tensor.transpose(bank[r.bank(key)][0:m, j * P:(j + 1) * P], src, ident[:])
                r.fill_done(last, key)

            def dense(l, key, lhs, rhs, n):
                r.claim(pe, key, l)
                for k in range(len(lhs)):
                    last = nc.tensor.matmul(bank[r.bank(key)][:, 0:n], lhs[k], rhs[k],
                                            start=(k == 0), stop=(k == len(lhs) - 1))
                r.fill_done(last, key)

            def group_src(g, h, t, what):
                if g < 2:
                    hh = 4 * g + h
                    return QM[:, t, hh * QH:(hh + 1) * QH] if what == "q" else KM[:, t, hh, :]
                if g < 5:
                    c0 = C_DIL + ((g - 2) * 4 + h) * HD + (DIL_COLS if what == "k" else 0)
                    return U[:, t, c0:c0 + HD]
                return U[:, t, C_BQ + h * HD:C_BQ + (h + 1) * HD] if what == "q" else U[:, t, C_BK:C_BK + HD]

            def values(g, h, k):
                if g < 2:
                    return VM[:, k, (4 * g + h) * HD:(4 * g + h + 1) * HD]
                if g < 5:
                    c0 = C_DIL + 2 * DIL_COLS + ((g - 2) * 4 + h) * HD
                    return U[:, k, c0:c0 + HD]
                return U[:, k, C_BV:C_BV + HD]

            def group_turns(l, g):
                if g == 0:
                    pe.wait_ge(rope_q, l + 1)
                    r.read(pe, ("kv", 1, 1), l)
                if g == 2:
                    pe.wait_ge(rope_c, l + 1)
                for t in range(TT):
                    turn(l, ("qT", g, t), [group_src(g, h, t, "q") for h in range(4)])
                if g < 5:
                    for t in range(TT):
                        turn(l, ("kT", g, t), [group_src(g, h, t, "k") for h in range(4)])
                else:
                    turn(l, ("kT", g, 0), [group_src(g, 0, t, "k") for t in range(TT)])

            def scores(l, u):
                g, t = divmod(u, 2)
                dd = QH if g < 2 else HD
                r.read(pe, ("qT", g, 1), l)
                r.read(pe, ("qT", g, 0), l)
                r.read(pe, ("kT", g, 0), l)
                if g < 5:
                    r.read(pe, ("kT", g, 1), l)
                n = (t + 1) * P
                per = 4 if t == 0 else 2
                for j in range(t + 1):
                    key = ("s", u, j)
                    r.claim(pe, key, l)
                    for i in range(per):
                        h = j * per + i
                        last = nc.tensor.matmul(bank[r.bank(key)][:, i * n:(i + 1) * n],
                                                QT[0:dd, g % 2, h, t * P:(t + 1) * P],
                                                KTt[0:dd, g % 2, h if g < 5 else 0, 0:n], start=True, stop=True)
                    r.fill_done(last, key)

            def prob_turns(l, u):
                t = u % 2
                pe.wait_ge(pexp, l * 12 + (u + 1))
                if t == 0:
                    turn(l, ("pT", u, 0), [PR[:, u % 2, h, 0:P] for h in range(4)])
                else:
                    for j in range(2):
                        turn(l, ("pT", u, j), [PR[:, u % 2, 2 * j + i, k * P:(k + 1) * P] for i in range(2) for k in range(2)])

            def outputs(l, u):
                g, t = divmod(u, 2)
                key = ("o", u)
                for j in range(t + 1):
                    r.read(pe, ("pT", u, j), l)
                r.claim(pe, key, l)
                for h in range(4):
                    for k in range(t + 1):
                        last = nc.tensor.matmul(bank[r.bank(key)][:, h * HD:(h + 1) * HD],
                                                PT[:, u % 2, h, k * P:(k + 1) * P], values(g, h, k),
                                                start=(k == 0), stop=(k == t))
                r.fill_done(last, key)

            def gate_up(l, e, s, i):
                pe.wait_ge(gu_in[s], l * 16 * NEXP + 32 * i + 32)
                for w0, what in ((0, "gate"), (2048, "up")):
                    key = (what, s)
                    w = EW[:, s, w0:w0 + 2048].rearrange("p (k n) -> p k n", k=KT)
                    r.claim(pe, key, l, i)
                    for f in range(2):
                        for k in range(KT):
                            last = nc.tensor.matmul(bank[r.bank(key)][:, f * SEQ:(f + 1) * SEQ],
                                                    w[:, k, f * P:(f + 1) * P], XT[:, k, :],
                                                    start=(k == 0), stop=(k == KT - 1))
                    r.fill_done(last, key)

            def down(l, s, i, first=False, final=False):
                pe.wait_ge(dn_in[s], l * 8 * NEXP + 16 * i + 16)
                pe.wait_ge(h_rdy, l * NEXP + 2 * i + (s + 3))
                w = EW[:, s, 4096:6144].rearrange("p (k n) -> p k n", k=2)
                for t in range(TT):
                    for n in range(2):
                        key = ("y", t, n)
                        if first:
                            r.claim(pe, key, l)
                        for f in range(2):
                            last = nc.tensor.matmul(bank[r.bank(key)][:, :], H[s][:, f * SEQ + t * P:f * SEQ + (t + 1) * P],
                                                    w[:, f, n * CHUNK:(n + 1) * CHUNK],
                                                    start=(first and f == 0), stop=(final and f == 1),
                                                    skip_group_check=True)
                        if final:
                            r.fill_done(last, key)
                last.then_inc(dn_done, 1) if not final else None

            with pe.Fori(0, DEPTH, 1) as l:
                pe.wait_ge(x_ready, 2 * l + 1)
                for t in range(TT):
                    for h in range(2):
                        turn(l, ("xT", t, h), [X[:, t, (4 * h + j) * P:(4 * h + j + 1) * P] for j in range(4)])
                for t in range(TT):
                    for h in range(2):
                        r.read(pe, ("xT", t, h), l)
                for n in range(N_IN):
                    pe.wait_ge(w_in[n % 2], l * 16 * NCH + 32 * (n // 2) + 32)
                    w = min(CHUNK, IN_COLS - n * CHUNK)
                    for t in range(TT):
                        dense(l, ("u", n, t), [XT[:, k, t * P:(t + 1) * P] for k in range(KT)],
                              [WD[:, n % 2, k, 0:w] for k in range(KT)], w)
                pe.wait_ge(cqn, l + 1)
                for t in range(TT):
                    turn(l, ("cT", t), [CQN[:, t, j * P:(j + 1) * P] for j in range(3)])
                pe.wait_ge(w_in[N_IN % 2], l * 16 * NCH + 32 * (N_IN // 2) + 32)
                flat = WD[:, N_IN % 2, :, :].rearrange("p k n -> p (k n)")
                wuq = flat[:, 0:1536].rearrange("p (k n) -> p k n", k=2)
                wukv = flat[:, 1536:2560]
                for t in range(TT):
                    r.read(pe, ("cT", t), l)
                for n in range(2):
                    for t in range(TT):
                        dense(l, ("q", n, t), [CQT[:, k, t * P:(t + 1) * P] for k in range(2)],
                              [wuq[:, k, 384 * n:384 * n + 384] for k in range(2)], 384)
                for n in range(2):
                    for t in range(TT):
                        dense(l, ("kv", n, t), [CQT[:, 2, t * P:(t + 1) * P]], [wukv[:, 512 * n:512 * n + 512]], 512)
                pe.wait_ge(rope_b, l + 1)
                for t in range(TT):
                    for h in range(2):
                        turn(l, ("qiT", t, h), [U[:, t, C_QI + (4 * h + j) * IDX_D:C_QI + (4 * h + j + 1) * IDX_D] for j in range(4)])
                turn(l, ("kiT",), [U[:, t, C_KI:C_KI + IDX_D] for t in range(TT)])
                for t in range(TT):
                    for h in range(2):
                        r.read(pe, ("qiT", t, h), l)
                r.read(pe, ("kiT",), l)
                for t in range(TT):
                    n = (t + 1) * P
                    per = 4 if t == 0 else 2
                    for j in range(IDX_H // per):
                        key = ("rel", t, j)
                        r.claim(pe, key, l)
                        for i in range(per):
                            last = nc.tensor.matmul(bank[r.bank(key)][:, i * n:(i + 1) * n],
                                                    QIT[:, j * per + i, t * P:(t + 1) * P], KIT[:, 0:n], start=True, stop=True)
                        r.fill_done(last, key)
                group_turns(l, 0)
                scores(l, 0)
                for u in range(12):
                    if u < 11:
                        if u % 2 == 1:
                            group_turns(l, (u + 1) // 2)
                        scores(l, u + 1)
                    prob_turns(l, u)
                    outputs(l, u)
                pe.wait_ge(o_ready, l + 1)
                for t in range(TT):
                    for h in range(2):
                        turn(l, ("oT", t, h), [O[:, t, (4 * h + j) * P:(4 * h + j + 1) * P] for j in range(4)])
                for t in range(TT):
                    for h in range(2):
                        r.read(pe, ("oT", t, h), l)
                for n in range(2):
                    m = N_IN + 1 + n
                    pe.wait_ge(w_in[m % 2], l * 16 * NCH + 32 * (m // 2) + 32)
                    for t in range(TT):
                        dense(l, ("mix", n, t), [XT[:, k, t * P:(t + 1) * P] for k in range(KT)],
                              [WD[:, m % 2, k, :] for k in range(KT)], CHUNK)
                pe.wait_ge(x_ready, 2 * l + 2)
                for t in range(TT):
                    for h in range(2):
                        turn(l, ("x2T", t, h), [X[:, t, (4 * h + j) * P:(4 * h + j + 1) * P] for j in range(4)])
                for t in range(TT):
                    for h in range(2):
                        r.read(pe, ("x2T", t, h), l)
                pe.wait_ge(consts_in, (l + 1) * 16 * 9)
                for t in range(TT):
                    dense(l, ("rout", t), [XT[:, k, t * P:(t + 1) * P] for k in range(KT)],
                          [RW[:, k, :] for k in range(KT)], NROUT)
                pe.wait_ge(gate_rdy, l + 1)
                key = ("gT",)
                r.claim(pe, key, l)
                for t in range(TT):
                    last = nc.tensor.transpose(bank[r.bank(key)][0:NEXP, t * P:(t + 1) * P], RT[:, 5, t, 0:NEXP], ident[:])
                r.fill_done(last, key)
                gate_up(l, 0, 0, 0)
                gate_up(l, 1, 1, 0)
                down(l, 0, 0, first=True)
                with pe.Fori(0, NEXP // 2 - 1, 1) as i:
                    gate_up(l, 0, 0, i + 1)
                    down(l, 1, i)
                    gate_up(l, 1, 1, i + 1)
                    down(l, 0, i + 1)
                down(l, 1, NEXP // 2 - 1, final=True)
                pe.drain().then_inc(dn_done, 1)

        @block.scalar
        def _(act):
            act.wait_ge(start, 1)

            def copy(l, key, dst, src, func=ACT.Copy):
                r.filled(act, key, l)
                r.read_done(nc.scalar.activation(dst, src, func), key)

            def copy_turns(l, name, dst):
                for t in range(TT):
                    for h in range(2):
                        key = (name, t, h)
                        copy(l, key, dst[:, 4 * h:4 * h + 4, t * P:(t + 1) * P],
                             bank[r.bank(key)][:, :].rearrange("p (k n) -> p k n", k=4))

            def group_copies(l, g):
                dd = QH if g < 2 else HD
                for what, dst in (("qT", QT), ("kT", KTt)):
                    for t in range(TT):
                        key = (what, g, t)
                        if key not in r.at:
                            continue
                        if g >= 2 and what == "qT" and t == 0:
                            r.filled(act, ("s", 2 * (g - 2) + 1, 1), l)
                        if what == "kT" and g == 5:
                            copy(l, key, dst[0:dd, g % 2, 0, :], bank[r.bank(key)][0:dd, 0:SEQ])
                        else:
                            copy(l, key, dst[0:dd, g % 2, :, t * P:(t + 1) * P],
                                 bank[r.bank(key)][0:dd, :].rearrange("p (h n) -> p h n", h=4))

            with act.Fori(0, DEPTH, 1) as l:
                copy_turns(l, "xT", XT)
                for n in range(N_IN):
                    w = min(CHUNK, IN_COLS - n * CHUNK)
                    for t in range(TT):
                        key = ("u", n, t)
                        copy(l, key, U[:, t, n * CHUNK:n * CHUNK + w], bank[r.bank(key)][:, 0:w])
                act.wait_ge(sq_in, 3 * l + 1)
                nc.scalar.activation(ST[:, 4:8], ST[:, 0:4], ACT.Sqrt).then_inc(sq_out, 1)
                for t in range(TT):
                    key = ("cT", t)
                    copy(l, key, CQT[:, :, t * P:(t + 1) * P], bank[r.bank(key)][:, 0:384].rearrange("p (k n) -> p k n", k=3))
                for n in range(2):
                    for t in range(TT):
                        key = ("q", n, t)
                        copy(l, key, QM[:, t, n * 384:(n + 1) * 384], bank[r.bank(key)][:, 0:384])
                for n in range(2):
                    for t in range(TT):
                        key = ("kv", n, t)
                        r.filled(act, key, l)
                        b = bank[r.bank(key)][:, :].rearrange("p (h d) -> p h d", h=4)
                        nc.scalar.activation(KM[:, t, 4 * n:4 * n + 4, 0:NOPE], b[:, :, 0:NOPE], ACT.Copy)
                        r.read_done(nc.scalar.activation(
                            VM[:, t, 256 * n:256 * n + 256].rearrange("p (h d) -> p h d", h=4), b[:, :, NOPE:], ACT.Copy), key)
                for t in range(TT):
                    for h in range(2):
                        key = ("qiT", t, h)
                        copy(l, key, QIT[:, 4 * h:4 * h + 4, t * P:(t + 1) * P],
                             bank[r.bank(key)][0:IDX_D, :].rearrange("p (h n) -> p h n", h=4))
                copy(l, ("kiT",), KIT[:], bank[r.bank(("kiT",))][0:IDX_D, 0:SEQ])
                for t in range(TT):
                    n = (t + 1) * P
                    per = 4 if t == 0 else 2
                    if t == 1:
                        act.wait_ge(sc0, l + 1)
                    for j in range(IDX_H // per):
                        key = ("rel", t, j)
                        copy(l, key, REL[:, j * per:(j + 1) * per, 0:n],
                             bank[r.bank(key)][:, 0:per * n].rearrange("p (h n) -> p h n", h=per), ACT.Relu)
                group_copies(l, 0)
                for u in range(12):
                    g, t = divmod(u, 2)
                    if u < 11 and u % 2 == 1:
                        group_copies(l, (u + 1) // 2)
                    n = (t + 1) * P
                    act.wait_ge(smax, l * 12 + (u + 1))
                    for h in range(4):
                        last = nc.scalar.activation(PR[:, u % 2, h, 0:n], PR[:, u % 2, h, 0:n], ACT.Exp,
                                                    bias=MX[:, u, h:h + 1], scale=1.0, accum_out=SM[:, u, h:h + 1])
                    last.then_inc(pexp, 1)
                    if u >= 2:
                        r.filled(act, ("o", u - 2), l)
                    if t == 0:
                        key = ("pT", u, 0)
                        copy(l, key, PT[:, 0, :, 0:P], bank[r.bank(key)][:, :].rearrange("p (h n) -> p h n", h=4))
                    else:
                        for j in range(2):
                            key = ("pT", u, j)
                            copy(l, key, PT[:, 1, 2 * j:2 * j + 2, :], bank[r.bank(key)][:, :].rearrange("p (h n) -> p h n", h=2))
                    if u == 10:
                        act.wait_ge(dilm, l + 1)
                        nc.scalar.activation(DW[:, 1], DW[:, 0], ACT.Exp).then_inc(dile, 1)
                copy_turns(l, "oT", XT)
                act.wait_ge(sq_in, 3 * l + 2)
                nc.scalar.activation(ST[:, 10:12], ST[:, 8:10], ACT.Sqrt).then_inc(sq_out, 1)
                copy_turns(l, "x2T", XT)
                act.wait_ge(rexp_in, 2 * l + 1)
                nc.scalar.activation(RT[:, 1, :, 0:GROUPS], RT[:, 1, :, 0:GROUPS], ACT.Exp).then_inc(rexp_out, 1)
                act.wait_ge(rexp_in, 2 * l + 2)
                nc.scalar.activation(ST[:, 20:22], ST[:, 18:20], ACT.Exp).then_inc(rexp_out, 1)
                copy(l, ("gT",), GTT[:], bank[r.bank(("gT",))][0:NEXP, 0:SEQ])
                with act.Fori(0, NEXP // 2, 1) as i:
                    for s in range(2):
                        key = ("gate", s)
                        r.filled(act, key, l, i)
                        act.wait_ge(h_rdy, l * NEXP + 2 * i + (s + 1))
                        r.read_done(nc.scalar.activation(SG[s], bank[r.bank(key)][:, :], ACT.Silu), key)
                act.wait_ge(sq_in, 3 * l + 3)
                nc.scalar.activation(ST[:, 10:12], ST[:, 8:10], ACT.Sqrt).then_inc(sq_out, 1)

        @block.vector
        def _(v):
            v.wait_ge(start, 1)
            v.wait_ge(mask_in, 16)
            TMP = [PR[:, 0, :, :].rearrange("p h n -> p (h n)"), PR[:, 1, :, :].rearrange("p h n -> p (h n)")]

            def rope(src, heads, half, f0):
                n = TT * heads * half
                tmp = [TMP[j // 2][:, (j % 2) * n:(j % 2 + 1) * n].rearrange("p (t h d) -> p t h d", t=TT, h=heads)
                       for j in range(4)]
                cos = bc(tab[:, 0, :, f0:f0 + half], 2, heads)
                sin = bc(tab[:, 1, :, f0:f0 + half], 2, heads)
                x1, x2 = src[:, :, :, 0:half], src[:, :, :, half:2 * half]
                v.nop(nofuse=True)
                v.drain()
                nc.vector.tensor_tensor(tmp[0], x1, cos, ALU.mult)
                nc.vector.tensor_tensor(tmp[1], x2, sin, ALU.mult)
                nc.vector.tensor_tensor(tmp[2], x2, cos, ALU.mult)
                nc.vector.tensor_tensor(tmp[3], x1, sin, ALU.mult)
                v.drain()
                nc.vector.tensor_tensor(x1, tmp[0], tmp[1], ALU.subtract)
                return nc.vector.tensor_tensor(x2, tmp[2], tmp[3], ALU.add)

            def layer_norm(l, nth, LN, ready):
                v.drain()
                for t in range(TT):
                    for j in range(2):
                        nc.vector.bn_stats(BN[:, t, j, :], X[:, t, j * 512:(j + 1) * 512])
                v.drain()
                for t in range(TT):
                    nc.vector.bn_aggr(MV[:, t, :], BN[:, t, :, :].rearrange("p a b -> p (a b)"))
                v.drain()
                nc.vector.tensor_scalar(ST[:, 8:10], MV[:, :, 1], LN_EPS, None, ALU.add).then_inc(sq_in, 1)
                v.wait_ge(sq_out, 3 * l + nth)
                nc.vector.reciprocal(ST[:, 12:14], ST[:, 10:12])
                v.drain()
                for t in range(TT):
                    nc.vector.tensor_scalar(X[:, t, :], X[:, t, :], MV[:, t, 0:1], ST[:, 12 + t:13 + t], ALU.subtract, ALU.mult)
                v.wait_ge(ln_in, (l + 1) * 64)
                v.nop(nofuse=True)
                v.drain()
                nc.vector.tensor_tensor(X[:, :, :], X[:, :, :], bc(LN[:, 0, :], 1, TT), ALU.mult)
                v.drain()
                nc.vector.tensor_tensor(X[:, :, :], X[:, :, :], bc(LN[:, 1, :], 1, TT), ALU.add).then_inc(ready, 1)

            def soften(l, u):
                g, t = divmod(u, 2)
                n = (t + 1) * P
                per = 4 if t == 0 else 2
                m0 = 0 if t == 0 else P
                mask = (DMASK if g == 5 else MASK[:, (0, 0, 1, 2, 3)[g], :])[:, m0:m0 + n]
                if u >= 2:
                    r.filled(v, ("pT", u - 2, (u - 2) % 2), l)
                for j in range(t + 1):
                    key = ("s", u, j)
                    r.filled(v, key, l)
                    r.read_done(nc.vector.scalar_tensor_tensor(
                        PR[:, u % 2, j * per:(j + 1) * per, 0:n],
                        bank[r.bank(key)][:, 0:per * n].rearrange("p (h n) -> p h n", h=per),
                        (QH if g < 2 else HD) ** -0.5, bc(mask, 1, per), ALU.mult, ALU.add), key)
                v.drain()
                nc.vector.tensor_reduce(MX[:, u, :], PR[:, u % 2, :, 0:n], AX, ALU.max)
                v.drain()
                nc.vector.tensor_scalar(MX[:, u, :], MX[:, u, :], -1.0, None, ALU.mult).then_inc(smax, 1)

            def take_out(l, u):
                g, t = divmod(u, 2)
                key = ("o", u)
                r.filled(v, key, l)
                src = bank[r.bank(key)][:, 0:256]
                if 2 <= g < 5:
                    return r.read_done(nc.vector.tensor_copy(OG[:, t, g - 2, :], src), key)
                v.wait_ge(pexp, l * 12 + (u + 1))
                nc.vector.reciprocal(ST[:, 24:28], SM[:, u, :])
                v.drain()
                c0 = 256 * g if g < 2 else 512
                r.read_done(nc.vector.tensor_tensor(
                    O[:, t, c0:c0 + 256].rearrange("p (h d) -> p h d", h=4), src.rearrange("p (h d) -> p h d", h=4),
                    bc(ST[:, 24:28], 2, HD), ALU.mult), key)

            def first_max(dst, src, n, at):
                mx = ST[:, 28:30]
                nc.vector.tensor_reduce(mx, src, AX, ALU.max)
                v.drain()
                nc.vector.tensor_tensor(dst, src, bc(mx, 2, n), ALU.is_equal)
                v.drain()
                nc.vector.tensor_tensor(dst, dst, bc(c["ramp"][:, 0:n], 1, TT), ALU.mult)
                v.drain()
                nc.vector.tensor_reduce(ST[:, 30:32], dst, AX, ALU.max)
                v.drain()
                nc.vector.tensor_tensor(dst, dst, bc(ST[:, 30:32], 2, n), ALU.is_equal)
                v.drain()

            v.drain().then_inc(x_ready, 1)
            with v.Fori(0, DEPTH, 1) as l:
                for t in range(TT):
                    r.read(v, ("u", 0, t), l)
                for t in range(TT):
                    for j, (c0, c1) in enumerate(((C_CQ, C_CKV), (C_CKV, C_KPE))):
                        nc.vector.tensor_tensor_reduce(CQN[:, t, c0:c1], U[:, t, c0:c1], U[:, t, c0:c1],
                                                       1.0 / (c1 - c0), 0.0, ALU.mult, ALU.add, ST[:, 2 * t + j:2 * t + j + 1])
                v.drain()
                nc.vector.tensor_scalar(ST[:, 0:4], ST[:, 0:4], RMS_EPS, None, ALU.add).then_inc(sq_in, 1)
                v.wait_ge(sq_out, 3 * l + 1)
                v.wait_ge(consts_in, (l + 1) * 16 * 9)
                nc.vector.reciprocal(ST[:, 4:8], ST[:, 4:8])
                v.drain()
                for t in range(TT):
                    for j, (c0, c1) in enumerate(((C_CQ, C_CKV), (C_CKV, C_KPE))):
                        last = nc.vector.scalar_tensor_tensor(CQN[:, t, c0:c1], U[:, t, c0:c1], ST[:, 4 + 2 * t + j:5 + 2 * t + j],
                                                              GN[:, c0:c1], ALU.mult, ALU.mult)
                last.then_inc(cqn, 1)
                for n in (1, 2):
                    for t in range(TT):
                        r.read(v, ("u", n, t), l)
                rope(U[:, :, C_KPE:C_KPE + ROPE].unsqueeze(2), 1, HALF_M, 0)
                rope(U[:, :, C_BQ:C_BV].rearrange("p t (h d) -> p t h d", d=HD), 5, HALF_H, HALF_M)
                rope(U[:, :, C_QI:C_WI].rearrange("p t (h d) -> p t h d", d=IDX_D), 9, HALF_I, HALF_M + HALF_H)
                nc.vector.tensor_scalar(U[:, :, C_WI:C_DIL], U[:, :, C_WI:C_DIL], IDX_D ** -0.5 * IDX_H ** -0.5, None, ALU.mult)
                nc.vector.tensor_copy(KM[:, :, :, NOPE:QH], bc(U[:, :, C_KPE:C_KPE + ROPE], 2, MLA_H))
                v.drain().then_inc(rope_b, 1)
                for n in range(2):
                    for t in range(TT):
                        r.read(v, ("q", n, t), l)
                rope(QM.rearrange("p t (h d) -> p t h d", d=QH)[:, :, :, NOPE:QH], MLA_H, HALF_M, 0).then_inc(rope_q, 1)
                for n in range(3, N_IN):
                    for t in range(TT):
                        r.read(v, ("u", n, t), l)
                rope(U[:, :, C_DIL:C_DIL + 2 * DIL_COLS].rearrange("p t (h d) -> p t h d", d=HD), 24, HALF_H, HALF_M).then_inc(rope_c, 1)
                for t in range(TT):
                    n = (t + 1) * P
                    m0 = 0 if t == 0 else P
                    per = 4 if t == 0 else 2
                    sc = DMASK[:, m0:m0 + n]
                    for h in range(IDX_H):
                        if h % per == 0:
                            r.read(v, ("rel", t, h // per), l)
                        last = nc.vector.scalar_tensor_tensor(sc, REL[:, h, 0:n], U[:, t, C_WI + h:C_WI + h + 1],
                                                              MASK[:, 0, m0:m0 + n] if h == 0 else sc, ALU.mult, ALU.add)
                        v.drain()
                    if t == 0:
                        v.drain().then_inc(sc0, 1)
                    for _ in range(TOPK // 8):
                        nc.vector.max(M8[:], sc)
                        v.drain()
                        nc.vector.match_replace(sc, M8[:], sc, TAKEN)
                        v.drain()
                    nc.vector.tensor_scalar(sc, sc, 0.5 * TAKEN, NEG, ALU.is_gt, ALU.mult)
                    v.drain()
                    nc.vector.tensor_tensor(sc, sc, MASK[:, 0, m0:m0 + n], ALU.add)
                v.drain()
                soften(l, 0)
                for u in range(12):
                    if u < 11:
                        soften(l, u + 1)
                    take_out(l, u)
                    if u == 9:
                        v.drain()
                        mg = MX[:, 4:10, :].rearrange("p (g t) h -> p t h g", g=3)
                        nc.vector.tensor_reduce(DW[:, 2, :, 0, :], mg, AX, ALU.min)
                        v.drain()
                        nc.vector.tensor_tensor(DW[:, 0], bc(DW[:, 2, :, 0, :], 2, 3),
                                                MX[:, 4:10, :].rearrange("p (g t) h -> p t g h", g=3), ALU.subtract).then_inc(dilm, 1)
                    if u == 10:
                        v.wait_ge(dile, l + 1)
                        nc.vector.tensor_tensor(DW[:, 0], DW[:, 1], SM[:, 4:10, :].rearrange("p (g t) h -> p t g h", g=3), ALU.mult)
                        v.drain()
                        nc.vector.tensor_reduce(DW[:, 2, :, 0, :], DW[:, 0].rearrange("p t g h -> p t h g"), AX, ALU.add)
                        v.drain()
                        nc.vector.reciprocal(DW[:, 2, :, 1, :], DW[:, 2, :, 0, :])
                        v.drain()
                        nc.vector.tensor_tensor(DW[:, 1], DW[:, 1], bc(DW[:, 2, :, 1, :], 2, 3), ALU.mult)
                        v.drain()
                        for t in range(TT):
                            og = OG[:, t].rearrange("p g (h d) -> p g h d", d=HD)
                            nc.vector.tensor_tensor(og, og, bc(DW[:, 1, t], 3, HD), ALU.mult)
                        v.drain()
                        nc.vector.tensor_tensor(O[:, :, 768:1024], OG[:, :, 0, :], OG[:, :, 1, :], ALU.add)
                        v.drain()
                        nc.vector.tensor_tensor(O[:, :, 768:1024], O[:, :, 768:1024], OG[:, :, 2, :], ALU.add)
                v.drain().then_inc(o_ready, 1)
                for n in range(2):
                    for t in range(TT):
                        key = ("mix", n, t)
                        xs = X[:, t, n * CHUNK:(n + 1) * CHUNK]
                        r.filled(v, key, l)
                        r.read_done(nc.vector.scalar_tensor_tensor(xs, xs, ALPHA, bank[r.bank(key)][:, :], ALU.mult, ALU.add), key)
                layer_norm(l, 2, LN1, x_ready)
                v.wait_ge(consts_in, (l + 1) * 16 * 9)
                for t in range(TT):
                    key = ("rout", t)
                    r.filled(v, key, l)
                    r.read_done(nc.vector.tensor_tensor(RT[:, 0, t, :], bank[r.bank(key)][:, 0:NROUT], RB[:], ALU.add), key)
                v.drain()
                lg, le = RT[:, 0, :, 0:GROUPS], RT[:, 0, :, GROUPS:]
                ghot = RT[:, 2, :, 0:GROUPS]
                first_max(ghot, lg, GROUPS, 3)
                nc.vector.tensor_tensor(RT[:, 1, :, 0:GROUPS], lg, bc(ST[:, 28:30], 2, GROUPS), ALU.subtract).then_inc(rexp_in, 1)
                le4 = le.rearrange("p t (g e) -> p t g e", g=GROUPS)
                sel4 = RT[:, 3, :, 0:NEXP].rearrange("p t (g e) -> p t g e", g=GROUPS)
                nc.vector.tensor_tensor(sel4, le4, bc(ghot, 3, EXP_PER), ALU.mult)
                v.drain()
                les = RT[:, 4, :, 0:8]
                nc.vector.tensor_reduce(les, RT[:, 3, :, 0:NEXP].rearrange("p t (g e) -> p t e g", g=GROUPS), AX, ALU.add)
                v.drain()
                hot1, hot2 = RT[:, 4, :, 8:16], RT[:, 4, :, 16:24]
                first_max(hot1, les, 8, 3)
                nc.vector.tensor_copy(ST[:, 16:18], ST[:, 28:30])
                nc.vector.scalar_tensor_tensor(les, hot1, TAKEN, les, ALU.mult, ALU.add)
                v.drain()
                first_max(hot2, les, 8, 3)
                nc.vector.tensor_tensor(ST[:, 18:20], ST[:, 28:30], ST[:, 16:18], ALU.subtract).then_inc(rexp_in, 1)
                v.wait_ge(rexp_out, 2 * l + 2)
                nc.vector.tensor_reduce(ST[:, 32:34], RT[:, 1, :, 0:GROUPS], AX, ALU.add)
                nc.vector.tensor_scalar(ST[:, 34:36], ST[:, 20:22], 1.0, None, ALU.add)
                v.drain()
                nc.vector.tensor_tensor(ST[:, 32:34], ST[:, 32:34], ST[:, 34:36], ALU.mult)
                v.drain()
                nc.vector.reciprocal(ST[:, 36:38], ST[:, 32:34])
                v.drain()
                nc.vector.tensor_tensor(ST[:, 38:40], ST[:, 36:38], ST[:, 20:22], ALU.mult)
                nc.vector.tensor_tensor(hot1, hot1, bc(ST[:, 36:38], 2, 8), ALU.mult)
                v.drain()
                nc.vector.tensor_tensor(hot2, hot2, bc(ST[:, 38:40], 2, 8), ALU.mult)
                v.drain()
                nc.vector.tensor_tensor(hot1, hot1, hot2, ALU.add)
                v.drain()
                nc.vector.tensor_tensor(RT[:, 5, :, 0:NEXP].rearrange("p t (g e) -> p t g e", g=GROUPS),
                                        bc(ghot, 3, EXP_PER), bc(hot1, 2, GROUPS), ALU.mult).then_inc(gate_rdy, 1)
                with v.Fori(0, NEXP // 2, 1) as i:
                    for s in range(2):
                        key = ("up", s)
                        r.filled(v, key, l, i)
                        r.read(v, ("gate", s), l, i)
                        r.read_done(nc.vector.tensor_tensor(SG[s], SG[s], bank[r.bank(key)][:, :], ALU.mult), key)
                        v.wait_ge(gb_in[s], l * 8 * NEXP + 16 * i + 16)
                        v.wait_ge(dn_done, l * NEXP + 2 * i + (s + 1))
                        v.nop(nofuse=True)
                        v.drain()
                        nc.vector.tensor_tensor(H[s].rearrange("p (f n) -> p f n", f=2), SG[s].rearrange("p (f n) -> p f n", f=2),
                                                bc(GB[s], 1, 2), ALU.mult).then_inc(h_rdy, 1)
                for t in range(TT):
                    for n in range(2):
                        key = ("y", t, n)
                        xs = X[:, t, n * CHUNK:(n + 1) * CHUNK]
                        r.filled(v, key, l)
                        r.read_done(nc.vector.scalar_tensor_tensor(xs, xs, ALPHA, bank[r.bank(key)][:, :], ALU.mult, ALU.add), key)
                layer_norm(l, 3, LN2, x_ready)


def setup(nc, io, c, X):
    ident, snake, ramp, tab = c["ident"], c["snake"], c["ramp"], c["tab"]
    with ExitStack() as ctx:
        def sb(name, shape, dt=F32):
            return ctx.enter_context(nc.sbuf_tensor(name, shape, dt))

        posi = sb("posi", [P, TT], I32)
        posf = sb("posf", [P, TT])
        freq = sb("freq", [P, NFREQ])
        ang = sb("ang", [P, TT, NFREQ])
        turns = sb("turns", [P, TT, NFREQ])
        absr = sb("absr", [P, 2, TT, NFREQ])
        loaded = ctx.enter_context(nc.semaphore("setup_loaded"))
        reduced = ctx.enter_context(nc.semaphore("setup_reduced"))
        block = ctx.enter_context(nc.Block())

        @block.sync
        def _(sp):
            sp.dma_start(posi[:].unsqueeze(2), io["positions"].rearrange("b (t p) -> p t b", p=P), allow_slow_non_contiguous=True).then_inc(loaded, 16)
            sp.dma_start(freq[:], io["freqs"].partition_broadcast(P)).then_inc(loaded, 16)
            sp.dma_start(ramp[:], io["ramp"].partition_broadcast(P)).then_inc(loaded, 16)
            sp.dma_start(ident[:], io["ident"]).then_inc(loaded, 16)
            sp.dma_start(snake[:], io["snake"]).then_inc(loaded, 16)
            sp.dma_start(X[:], io["x"][0].rearrange("(t p) n -> p t n", p=P)).then_inc(loaded, 16)
            sp.wait_ge(loaded, 96)

        @block.vector
        def _(v):
            v.wait_ge(loaded, 96)
            nc.vector.tensor_copy(posf[:], posi[:])
            v.drain()
            nc.vector.tensor_tensor(ang[:], bc(posf[:], 2, NFREQ), bc(freq[:], 1, TT), ALU.mult)
            v.drain()
            big = 1.5 * 2.0 ** 23
            nc.vector.tensor_scalar(turns[:], ang[:], 1.0 / (2 * math.pi), big, ALU.mult, ALU.add)
            v.drain()
            nc.vector.tensor_scalar(turns[:], turns[:], big, None, ALU.subtract)
            v.drain()
            c1 = 6.28125
            c2 = float(np.float32(round((2 * math.pi - c1) * 2 ** 21) / 2 ** 21))
            c3 = float(np.float32(2 * math.pi - c1 - c2))
            for part in (c1, c2, c3):
                nc.vector.scalar_tensor_tensor(ang[:], turns[:], -part, ang[:], ALU.mult, ALU.add)
                v.drain()
            nc.vector.tensor_scalar(ang[:], ang[:], 3.1415925, -3.1415925, ALU.min, ALU.max)
            v.drain()
            nc.vector.tensor_copy(absr[:, 1], ang[:])
            nc.vector.tensor_scalar(absr[:, 0], ang[:], -1.0, None, ALU.mult)
            v.drain()
            nc.vector.tensor_tensor(absr[:, 0], absr[:, 0], ang[:], ALU.max)
            v.drain()
            nc.vector.tensor_scalar(absr[:, 0], absr[:, 0], -1.0, math.pi / 2, ALU.mult, ALU.add).then_inc(reduced, 1)

        @block.scalar
        def _(act):
            act.wait_ge(reduced, 1)
            nc.scalar.activation(tab[:], absr[:], ACT.Sin)


def constants(nc, ctx):
    def sb(name, shape):
        return ctx.enter_context(nc.sbuf_tensor(name, shape, F32))

    c = {"ident": sb("ident", [P, P]), "snake": sb("snake_perm", [P, P]), "ramp": sb("ramp", [P, 8]),
         "tab": sb("tab", [P, 2, TT, NFREQ])}
    c["banks"] = [ctx.enter_context(nc.psum_tensor(f"bank{b}", [P, 512], F32)) for b in range(8)]
    return c


SLOTS = 2
NEGCLAMP = 43.0
GH, GK, GV, GR = 4, 128, 256, 16
GDK, GDV = 512, 1024
GLA_IN = 2 * GDK + 2 * GDV + 2 * GR
GATE_NORM = 16.0
DFF = 4096
NF = DFF // P
SDI, SH, SG_, SR_, SN = 2048, 32, 8, 4, 128
SCONV = 5
S_X, S_B, S_C, S_DT = 2048, 4096, 5120, 6144
NX = SDI // P
ADA = 6 * D


class Stage:

    def __init__(self, src, width, last):
        self.src, self.width, self.last = src, width, last


def plan_block2(full, empty):
    r = Ring(full, empty)
    keys = [("cc",)]

    def ada(i):
        out = [("ada", i, n) for n in range(12)] + [("mc", i)]
        return out + [("mb", i, k, s, n) for k in range(2) for s in range(2 if i == 0 else 1) for n in range(2)]

    def turned(tag):
        return [("uT", tag, k) for k in range(KT)]

    def ffn(i):
        nt = 4 if i == 0 else 2
        return (turned(f"f{i}") + [("f1", i, f) for f in range(NF)] + [("f2", i, n, t) for n in range(2) for t in range(nt)])

    keys += ada(0) + turned("m0")
    keys += [("gq", h) for h in range(GH)] + [("gk", h) for h in range(GH)] + [("ga", z) for z in range(2)]
    keys += [("gl", h, z) for h in range(2) for z in range(2)] + [("gv", n, t) for n in range(2) for t in range(4)]
    keys += [("gl", h, z) for h in range(2, 4) for z in range(2)] + [("gg", n, t) for n in range(2) for t in range(4)]

    def head_pre(h):
        return [("kT", h, z) for z in range(2)] + [("A", h, z) for z in range(2)]

    keys += head_pre(0)
    for h in range(GH):
        if h + 1 < GH:
            keys += head_pre(h + 1)
        keys += [("kvs", h, n) for n in range(3)] + [("go", h, s) for s in range(2)]
    keys += turned("o0") + [("gy", n, t) for n in range(2) for t in range(4)]
    keys += ffn(0) + ada(1) + turned("m1")
    keys += [("cw",)]
    conv = []
    for m in range(NX + 2 * SG_ + 1):
        if m < NX + 2 * SG_:
            conv.append(("sc", m))
        if 1 <= m <= NX + SG_:
            conv.append(("xt", m - 1))
    keys += conv
    keys += [("dt", t) for t in range(4)] + [("cum",), ("cd",)]
    for n, k in enumerate(keys):
        r.plan(k, n % 8)
    for g in range(-1, SG_):
        if g + 1 < SG_:
            r.plan(("cb", g + 1), (g + 1) % 2)
            r.plan(("ss", g + 1), 2)
        if g >= 0:
            r.plan(("sz", g // 2, g % 2), 3)
            for t in range(2):
                r.plan(("yo", g, t), 4 + t)
            for t in range(2):
                r.plan(("yi", g, t), 6 + t)
    keys = [("yT", j) for j in range(8)] + [("sy", n, t) for n in range(2) for t in range(2)] + ffn(1)
    for n, k in enumerate(keys):
        r.plan(k, n % 8)
    return r


def plan_chunks(io):
    def cols(name, c0, c1, r0=0, lead=0):
        w = io[name][lead]
        return w[r0:r0 + D, c0:c1].rearrange("(k p) n -> p k n", p=P)

    out = {}

    def add(key, src, last):
        out[key] = Stage(src, src.shape[2], last)

    def ada(i):
        for n in range(12):
            add(("ada", i, n), cols("ada_w_2", n * CHUNK, (n + 1) * CHUNK, lead=i), ("ada", i, n))

    def ffn(i):
        nt = 4 if i == 0 else 2
        for n in range(8):
            add(("f1", i, n), cols("ffn_w1_2", n * CHUNK, (n + 1) * CHUNK, lead=i), ("f1", i, 4 * n + 3))
        for n in range(2):
            for c in range(4):
                add(("f2", i, n, c), cols("ffn_w2_2", n * CHUNK, (n + 1) * CHUNK, r0=c * D, lead=i),
                    ("f2", i, n, nt - 1) if c == 3 else None)

    ada(0)
    add("gq", cols("gla_w_in_2", 0, GDK), ("gq", 3))
    add("gk", cols("gla_w_in_2", GDK, 2 * GDK), ("gk", 3))
    add("ga", cols("gla_w_in_2", 2 * GDK + 2 * GDV, GLA_IN), ("ga", 1))
    for what, c0 in (("gv", 2 * GDK), ("gg", 2 * GDK + GDV)):
        for n in range(2):
            add((what, n), cols("gla_w_in_2", c0 + n * CHUNK, c0 + (n + 1) * CHUNK), (what, n, 3))
    for n in range(2):
        add(("gy", n), cols("gla_w_out_2", n * CHUNK, (n + 1) * CHUNK), ("gy", n, 3))
    ffn(0)
    ada(1)
    for n in range(8):
        add(("sc", n), cols("ssd_w_in_2", S_X + n * CHUNK, S_X + (n + 1) * CHUNK), ("sc", 4 * n + 3))
    add("dt", cols("ssd_w_in_2", S_DT, S_DT + 2 * SH), ("dt", 3))
    for n in range(4):
        add(("sz", n), cols("ssd_w_in_2", n * CHUNK, (n + 1) * CHUNK), ("sz", n, 1))
    for n in range(2):
        for c in range(2):
            add(("sy", n, c), cols("ssd_w_out_2", n * CHUNK, (n + 1) * CHUNK, r0=c * D), ("sy", n, 1) if c == 1 else None)
    ffn(1)
    return out


def block2_constants():
    j = np.arange(P)[:, None, None] + P * np.arange(2)[None, :, None]
    i = np.arange(2 * P)[None, None, :]
    uf, ub = (j <= i).astype(np.float32), (j >= i).astype(np.float32)
    neg = np.stack([np.where(uf > 0, 0, NEG), np.where(ub > 0, 0, NEG)], 1).astype(np.float32)
    first = np.ones(512, np.float32)
    first[::P] = 0.0
    a = np.arange(P)
    tri = np.stack([a[:, None] <= a[None, :], a[:, None] >= a[None, :]], 1).astype(np.float32)
    return {"sums": np.stack([uf, ub], 1), "neg": neg, "restart": first, "tri": tri}


def block2(nc, io, c, XA, dram_cum):
    with ExitStack() as ctx:
        def sb(name, shape, dt=F32):
            return ctx.enter_context(nc.sbuf_tensor(name, shape, dt))

        def sem(name):
            return ctx.enter_context(nc.semaphore(name))

        ident, snake, bank = c["ident"], c["snake"], c["banks"]
        UT = sb("UT", [P, KT, 2 * SEQ])
        W = sb("W", [P, SLOTS, KT, CHUNK])
        MB = sb("MB", [P, 2, 2, D])
        LNP = sb("LNP", [P, 2, D])
        NEGM = sb("NEGM", [P, 2, 2, SEQ])
        SC = sb("SC", [P, 2, KT])
        COLS = sb("COLS", [P, 4, KT, 2])
        GB2 = sb("GB2", [P, 8])
        ST = sb("ST2", [P, 96])
        BN = sb("BN2", [P, 4, 2, 6])
        MV = sb("MV2", [P, 4, 2])
        ARENA = 26624
        A_ = sb("ARENA", [P, ARENA])
        cur = [0]

        def carve(n):
            a = cur[0]
            cur[0] += n
            assert cur[0] <= ARENA, cur[0]
            return A_[:, a:a + n]

        QD = carve(2048).rearrange("p (h n) -> p h n", h=GH)
        KD = carve(2048).rearrange("p (h n) -> p h n", h=GH)
        V = carve(4096).rearrange("p (t n) -> p t n", t=4)
        G = carve(4096).rearrange("p (t n) -> p t n", t=4)
        lg = carve(4096)
        LG = lg.rearrange("p (h z n) -> p h z n", h=GH, z=2)
        OT = lg.rearrange("p (h t n) -> p h t n", h=GH, t=4)
        HAT = carve(4096).rearrange("p (b z a n) -> p b z a n", b=2, z=2, a=2)
        KTOK = carve(2048).rearrange("p (b z c n) -> p b z c n", b=2, z=2, c=4)
        AM = carve(1024).rearrange("p (b n) -> p b n", b=2)
        S = carve(512).rearrange("p (z n) -> p z n", z=2)
        TRI = carve(256).rearrange("p (z n) -> p z n", z=2)
        RST = carve(512)
        SRS = carve(1536).rearrange("p (s z n) -> p s z n", s=3, z=2)
        GGAIN = carve(256)
        CC = A_[0:8, 12288:12672].rearrange("p (a n) -> p a n", a=3)
        MROW = A_[0:2, 0:ADA]
        ABIAS = A_[0:2, ADA:2 * ADA]
        AT = A_[0:GR, 20480:21504].rearrange("p (z n) -> p z n", z=2)
        WA2 = A_[0:GR, 21504:22528].rearrange("p (z n) -> p z n", z=2)
        TMPR = A_[:, 18432:19456].rearrange("p (b n) -> p b n", b=2)
        HT = A_[:, 0:NF * 512].rearrange("p (f n) -> p f n", f=NF)
        cur[0] = 0
        BDL = carve(2048).rearrange("p (g n) -> p g n", g=SG_)
        CDL = carve(2048).rearrange("p (g n) -> p g n", g=SG_)
        XTOK = carve(8192).rearrange("p (t n) -> p t n", t=4)
        NG = carve(2048)
        BTOK = NG.rearrange("p (t g n) -> p t g n", t=2, g=SG_)
        Z = carve(4096).rearrange("p (t n) -> p t n", t=2)
        CBC = carve(2048).rearrange("p (z h n) -> p z h n", z=2, h=4)
        SEG = carve(4096).rearrange("p (j z h n) -> p j z h n", j=2, z=2, h=4)
        SSB = carve(1024).rearrange("p (b n) -> p b n", b=2)
        YI = carve(1024).rearrange("p (t n) -> p t n", t=2)
        CDS = A_[0:32, 25600:26112].rearrange("p (z n) -> p z n", z=2)
        XW = MB[:, :, 1, :].rearrange("p b (t n) -> p b t n", t=2)
        o = 18432
        PRE = A_[:, o:o + 1040].rearrange("p (b s n) -> p b s n", b=2, s=2)
        ACC = A_[:, o + 1040:o + 2064].rearrange("p (b s n) -> p b s n", b=2, s=2)
        XD = A_[:, o + 2064:o + 3088].rearrange("p (b n) -> p b n", b=2)
        CW = A_[:, o + 3088:o + 3280].rearrange("p (m k) -> p m k", k=6)
        SUMS = A_[:, o + 4096:o + 5120].rearrange("p (z j n) -> p z j n", z=2, j=2)
        CVR = A_[0:6, 12288:16384]
        DT = sb("DT", [P, 4, 64])
        DA = sb("DA", [P, 4, 64])
        CUM = sb("CUM", [P, 5, 64])
        WST = sb("WST", [P, 2, 64])
        EC = sb("EC", [P, 2, 64])
        NCUM = sb("NCUM", [P, 2, 64])
        DROW = sb("DROW", [P, 3, 64])

        full = [sem(f"b_full{b}") for b in range(8)]
        empty = [sem(f"b_empty{b}") for b in range(8)]
        r = plan_block2(full, empty)
        chunks = plan_chunks(io)
        order = list(chunks)
        number = {k: n for n, k in enumerate(order)}
        landed = [sem(f"b_weights_landed{s}") for s in range(SLOTS)]
        part_done = sem("b_partial_chunk_used")
        partial = [k for k in order if chunks[k].last is None]
        start = sem("b_counters_started")
        rows_in = sem("b_rows_in")
        abias_in = sem("b_ada_bias")
        w2_in = sem("b_gla_small")
        ln_in = sem("b_ln_params")
        conv_in = sem("b_conv_rows")
        ssd_in = sem("b_ssd_small")
        ng_in = sem("b_norm_gain")
        gn_in = sem("b_gate_weights")
        gain_in = sem("b_gla_gain")
        cum_st = sem("b_cum_stored")
        cbc_in = sem("b_cum_spread")
        sums_in = sem("b_sum_matrices")
        mrow = sem("b_ada_rows")
        cols_rdy = sem("b_ada_cols")
        x_rdy = sem("b_x_ready")
        sq_in, sq_out = sem("b_var"), sem("b_std")
        lsg_in, lsg_out = sem("b_gate_exponent"), sem("b_gate_log")
        hx_in, hx_out = sem("b_decay_exponents"), sem("b_decays")
        hats = sem("b_hats")
        am_rdy = sem("b_attn_masked")
        st_rdy = sem("b_states")
        o_rdy = sem("b_gla_out")
        acc_rdy = sem("b_conv_sum")
        pads = sem("b_conv_pads")
        xd_rdy = sem("b_conv_out")
        sp_in, sp_out = sem("b_dt_exponent"), sem("b_dt_log")
        da_rdy = sem("b_dt_ready")
        ec_in, ec_out = sem("b_cum_ready"), sem("b_cum_exp")
        xw_rdy = sem("b_state_inputs")
        seg_rdy, seg_exp = sem("b_segments"), sem("b_segments_exp")
        w_rdy = sem("b_segment_weights")
        y_rdy = sem("b_ssd_out")

        block = ctx.enter_context(nc.Block())

        @block.sync
        def _(sp):
            for s in full + empty:
                sp.sem_inc(s, 1)
            sp.sem_inc(start, 1)
            for n, key in enumerate(order):
                if n >= SLOTS:
                    old = order[n - SLOTS]
                    if chunks[old].last is None:
                        sp.wait_ge(part_done, partial.index(old) + 1)
                    else:
                        r.filled(sp, chunks[old].last)
                for half in range(2):
                    sp.dma_start(W[:, n % SLOTS, 4 * half:4 * half + 4, 0:chunks[key].width],
                                 chunks[key].src[:, 4 * half:4 * half + 4, :]).then_inc(landed[n % SLOTS], 16)

        @block.gpsimd
        def _(pool):
            pool.wait_ge(start, 1)
            pool.dma_start(CC[:, 0, :], io["c_2"].rearrange("b (k p) -> (b k) p", p=P)).then_inc(rows_in, 16)
            pool.dma_start(CC[:, 1, :], io["c_ctx_2"].rearrange("(k p) -> k p", p=P)).then_inc(rows_in, 16)
            pool.dma_start(CC[:, 2, :], io["gla_b_a2_2"][0].rearrange("z (h p) -> (z h) p", p=P)).then_inc(rows_in, 16)
            pool.dma_start(ABIAS, io["ada_b_2"][0, :].partition_broadcast(2)).then_inc(abias_in, 16)
            pool.dma_start(TRI, io["tri"]).then_inc(w2_in, 16)
            pool.dma_start(RST, io["restart"].partition_broadcast(P)).then_inc(w2_in, 16)
            pool.dma_start(XA[:, 2:4, :], io["ctx_2"][0].rearrange("(t p) n -> p t n", p=P)).then_inc(w2_in, 16)
            pool.dma_start(NEGM[:], io["neg"]).then_inc(w2_in, 16)

            def ln_load(i, j):
                n = 2 * i + j
                if n:
                    pool.wait_ge(x_rdy, n)
                pool.dma_start(LNP[:, 0, :], io["ln_g_2"][i, j, :].partition_broadcast(P)).then_inc(ln_in, 16)
                pool.dma_start(LNP[:, 1, :], io["ln_b_2"][i, j, :].partition_broadcast(P)).then_inc(ln_in, 16)

            ln_load(0, 0)
            r.read(pool, ("mb", 0, 1, 1, 1))
            pool.dma_start(WA2, io["gla_w_a2_2"][0].rearrange("z r n -> r z n")).then_inc(gn_in, 16)
            pool.dma_start(GGAIN, io["gla_norm_2"][0, :].partition_broadcast(P)).then_inc(gain_in, 16)
            ln_load(0, 1)
            r.read(pool, ("f2", 0, 1, 3))
            pool.dma_start(ABIAS, io["ada_b_2"][1, :].partition_broadcast(2)).then_inc(abias_in, 16)
            for k in range(SCONV):
                pool.dma_start(CVR[k:k + 1, :], io["ssd_conv_w_2"][0, k:k + 1, :]).then_inc(conv_in, 16)
            pool.dma_start(CVR[5:6, :], io["ssd_conv_b_2"][0:1, :]).then_inc(conv_in, 16)
            pool.dma_start(DROW[:, 0, :], io["ssd_dt_bias_2"].rearrange("a z h -> a (z h)")[0, :].partition_broadcast(P)).then_inc(ssd_in, 16)
            pool.dma_start(DROW[:, 1, :], io["ssd_a_log_2"].rearrange("a z h -> a (z h)")[0, :].partition_broadcast(P)).then_inc(ssd_in, 16)
            pool.dma_start(DROW[:, 2, 0:SH], io["ssd_d_2"][0, :].partition_broadcast(P)).then_inc(ssd_in, 16)
            ln_load(1, 0)
            r.read(pool, ("mb", 1, 1, 0, 1))
            pool.dma_start(SUMS, io["sums"]).then_inc(sums_in, 16)
            r.read(pool, ("cd",))
            pool.dma_start(dram_cum.rearrange("z h n -> h z n"), CDS[:]).then_inc(cum_st, 16)
            pool.wait_ge(cum_st, 16)
            for g in range(SG_):
                if g >= 1:
                    pool.wait_ge(seg_rdy, 2 * g)
                for z in range(2):
                    pool.dma_start(CBC[:, z], dram_cum[z, 4 * g:4 * g + 4, :].partition_broadcast(P)).then_inc(cbc_in, 16)
            r.filled(pool, ("ss", SG_ - 1))
            pool.dma_start(NG, io["ssd_norm_2"][0, :].partition_broadcast(P)).then_inc(ng_in, 16)
            ln_load(1, 1)

        @block.tensor
        def _(pe):
            pe.wait_ge(start, 1)

            def weights(key):
                n = number[key]
                pe.wait_ge(landed[n % SLOTS], 32 * (n // SLOTS + 1))
                return W[:, n % SLOTS]

            def mm(key, cols, lhs, rhs, start=True, stop=True, rows=P):
                return nc.tensor.matmul(bank[r.bank(key)][0:rows, cols[0]:cols[1]], lhs, rhs, start=start, stop=stop)

            def turn(key, j, src):
                m = src.shape[1]
                k = src.shape[0]
                return nc.tensor.transpose(bank[r.bank(key)][0:m, j * P:j * P + k], src, ident[0:k, 0:k])

            def ada(i):
                for n in range(12):
                    w = weights(("ada", i, n))
                    key = ("ada", i, n)
                    r.claim(pe, key)
                    for k in range(KT):
                        last = mm(key, (0, CHUNK), SC[:, :, k], w[:, k, :], k == 0, k == KT - 1, rows=2)
                    r.fill_done(last, key)
                pe.wait_ge(mrow, i + 1)
                key = ("mc", i)
                r.claim(pe, key)
                for a, kind in enumerate((0, 1, 3, 4)):
                    for k in range(KT):
                        c0 = (a * KT + k) * 2
                        last = nc.tensor.transpose(bank[r.bank(key)][:, c0:c0 + 2],
                                                   MROW[:, kind * D + k * P:kind * D + (k + 1) * P], ident[0:2, 0:2])
                r.fill_done(last, key)
                for a, kind in enumerate((2, 5)):
                    for s in range(2 if i == 0 else 1):
                        for n in range(2):
                            key = ("mb", i, a, s, n)
                            r.claim(pe, key)
                            last = mm(key, (0, CHUNK), ident[0:2, s:s + 1].broadcast_to([2, P]),
                                      MROW[:, kind * D + n * CHUNK:kind * D + (n + 1) * CHUNK])
                            r.fill_done(last, key)

            def turned(tag, src, nt, snaked):
                for k in range(KT):
                    key = ("uT", tag, k)
                    r.claim(pe, key)
                    for t in range(nt):
                        if snaked and t < 2:
                            last = mm(key, (t * P, (t + 1) * P), src(t, k), snake[:])
                        else:
                            last = turn(key, t, src(t, k))
                    r.fill_done(last, key)

            def x_tile(t, k):
                return XA[:, t, k * P:(k + 1) * P]

            def out_tile(t, k):
                return OT[:, k // 2, t, (k % 2) * P:(k % 2 + 1) * P]

            def await_turned(tag):
                for k in range(KT):
                    r.read(pe, ("uT", tag, k))

            def across(key, w, m, n0, n1, rows=P):
                r.claim(pe, key)
                for k in range(KT):
                    last = mm(key, (0, n1 - n0), w[:, k, m[0]:m[1]], UT[:, k, n0:n1], k == 0, k == KT - 1, rows=m[1] - m[0])
                r.fill_done(last, key)

            def along(key, w, t, width):
                r.claim(pe, key)
                for k in range(KT):
                    last = mm(key, (0, width), UT[:, k, t * P:(t + 1) * P], w[:, k, 0:width], k == 0, k == KT - 1)
                r.fill_done(last, key)

            def ffn(i, nt, nth):
                pe.wait_ge(x_rdy, nth)
                turned(f"f{i}", x_tile, nt, False)
                await_turned(f"f{i}")
                for n in range(8):
                    w = weights(("f1", i, n))
                    for j in range(4):
                        across(("f1", i, 4 * n + j), w, (j * P, (j + 1) * P), 0, nt * P)
                for f in range(NF):
                    r.read(pe, ("f1", i, f))
                for n in range(2):
                    for c4 in range(4):
                        w = weights(("f2", i, n, c4))
                        for t in range(nt):
                            key = ("f2", i, n, t)
                            if c4 == 0:
                                r.claim(pe, key)
                            for k in range(KT):
                                f = c4 * KT + k
                                last = mm(key, (0, CHUNK), HT[:, f, t * P:(t + 1) * P], w[:, k, :], f == 0, f == NF - 1)
                            if c4 == 3:
                                r.fill_done(last, key)
                        if c4 < 3:
                            last.then_inc(part_done, 1)

            pe.wait_ge(rows_in, 48)
            key = ("cc",)
            r.claim(pe, key)
            for j in range(3):
                last = nc.tensor.transpose(bank[r.bank(key)][:, 8 * j:8 * j + 8], CC[:, j, :], ident[0:8, 0:8])
            r.fill_done(last, key)
            r.read(pe, key)
            ada(0)
            pe.wait_ge(w2_in, 64)
            turned("m0", x_tile, 4, True)
            await_turned("m0")
            w = weights("gq")
            for h in range(GH):
                across(("gq", h), w, (h * P, (h + 1) * P), 0, 512)
            w = weights("gk")
            for h in range(GH):
                across(("gk", h), w, (h * P, (h + 1) * P), 0, 512)
            w = weights("ga")
            for z in range(2):
                across(("ga", z), w, (z * GR, (z + 1) * GR), 0, 512)
            pe.wait_ge(gn_in, 16)
            for z in range(2):
                r.read(pe, ("ga", z))

            def logits(h):
                for z in range(2):
                    key = ("gl", h, z)
                    r.claim(pe, key)
                    r.fill_done(mm(key, (0, 512), WA2[:, z, h * P:(h + 1) * P], AT[:, z, :]), key)

            for what, h0 in (("gv", 0), ("gg", 2)):
                logits(h0)
                logits(h0 + 1)
                for n in range(2):
                    w = weights((what, n))
                    for t in range(4):
                        along((what, n, t), w, t, CHUNK)
            for n in range(2):
                for t in range(4):
                    r.read(pe, ("gv", n, t))

            def head_pre(h):
                pe.wait_ge(hats, h + 1)
                for z in range(2):
                    key = ("kT", h, z)
                    r.claim(pe, key)
                    for ch in range(4):
                        last = turn(key, ch, HAT[:, h % 2, z, 1, ch * P:(ch + 1) * P])
                    r.fill_done(last, key)
                for z in range(2):
                    key = ("A", h, z)
                    r.claim(pe, key)
                    for ch in range(4):
                        sl = slice(ch * P, (ch + 1) * P)
                        last = mm(key, (ch * P, (ch + 1) * P), HAT[:, h % 2, z, 1, sl], HAT[:, h % 2, z, 0, sl])
                    r.fill_done(last, key)

            STEPS = ((2, 3), (3, 2), (0, 1))
            head_pre(0)
            for h in range(GH):
                if h + 1 < GH:
                    head_pre(h + 1)
                vcol = slice(h * GV, (h + 1) * GV)
                for z in range(2):
                    r.read(pe, ("kT", h, z))
                for n in range(3):
                    key = ("kvs", h, n)
                    r.claim(pe, key)
                    for z in range(2):
                        ch = STEPS[n][z]
                        last = mm(key, (z * GV, (z + 1) * GV), KTOK[:, h % 2, z, ch, :], V[:, ch, vcol])
                    r.fill_done(last, key)
                pe.wait_ge(am_rdy, h + 1)
                pe.wait_ge(st_rdy, h + 1)
                enter = {(3, 0): 0, (0, 0): 1, (1, 0): 2, (2, 1): 0, (1, 1): 1, (0, 1): 2}
                for s in range(2):
                    key = ("go", h, s)
                    r.claim(pe, key)
                    for j in range(2):
                        ch = 2 * s + j
                        cols = (j * GV, (j + 1) * GV)
                        terms = [(AM[:, h % 2, ch * P:(ch + 1) * P], V[:, ch, vcol])]
                        for z in range(2):
                            if (ch, z) in enter:
                                terms.append((HAT[:, h % 2, z, 0, ch * P:(ch + 1) * P], SRS[:, enter[(ch, z)], z, :]))
                        for q, (a, b) in enumerate(terms):
                            last = mm(key, cols, a, b, q == 0, q == len(terms) - 1)
                    r.fill_done(last, key)
            pe.wait_ge(o_rdy, 1)
            turned("o0", out_tile, 4, True)
            await_turned("o0")
            for n in range(2):
                w = weights(("gy", n))
                for t in range(4):
                    along(("gy", n, t), w, t, CHUNK)
            ffn(0, 4, 1)
            pe.wait_ge(x_rdy, 2)
            ada(1)
            turned("m1", x_tile, 4, True)
            await_turned("m1")
            pe.wait_ge(conv_in, 96)
            key = ("cw",)
            r.claim(pe, key)
            for m in range(NX + 2 * SG_):
                last = nc.tensor.transpose(bank[r.bank(key)][:, 6 * m:6 * m + 6], CVR[:, m * P:(m + 1) * P], ident[0:6, 0:6])
            r.fill_done(last, key)
            for m in range(NX + 2 * SG_ + 1):
                if m < NX + 2 * SG_:
                    if m % 4 == 0:
                        w = weights(("sc", m // 4))
                    across(("sc", m), w, ((m % 4) * P, (m % 4 + 1) * P), 0, 512 if m < NX + SG_ else SEQ)
                if 1 <= m <= NX + SG_:
                    key = ("xt", m - 1)
                    pe.wait_ge(xd_rdy, m)
                    r.claim(pe, key)
                    for t in range(4) if m - 1 < NX else range(2, 4):
                        last = turn(key, t, XD[:, (m - 1) % 2, t * P:(t + 1) * P])
                    r.fill_done(last, key)
            w = weights("dt")
            for t in range(4):
                along(("dt", t), w, t, 64)
            pe.wait_ge(da_rdy, 1)
            pe.wait_ge(sums_in, 16)
            key = ("cum",)
            r.claim(pe, key)
            for s in range(2):
                for it in range(2):
                    for z in range(2):
                        terms = [jt for jt in range(2) if (jt <= it if z == 0 else jt >= it)]
                        c0 = (2 * s + it) * 64 + z * 32
                        for q, jt in enumerate(terms):
                            last = mm(key, (c0, c0 + 32), SUMS[:, z, jt, it * P:(it + 1) * P], DA[:, 2 * s + jt, z * 32:z * 32 + 32],
                                      q == 0, q == len(terms) - 1)
            for jt in range(2):
                last = mm(key, (256, 320), SUMS[:, 0, 0, P:2 * P], DA[:, 2 + jt, :], jt == 0, jt == 1)
            r.fill_done(last, key)
            key = ("cd",)
            r.claim(pe, key)
            for z in range(2):
                for jt in range(2):
                    last = mm(key, (z * SEQ, (z + 1) * SEQ), DA[:, jt, z * 32:z * 32 + 32], SUMS[:, z, jt, :], jt == 0, jt == 1, rows=32)
            r.fill_done(last, key)

            def group_pre(g):
                key = ("cb", g)
                r.claim(pe, key)
                for jt in range(2):
                    last = mm(key, (jt * SEQ, (jt + 1) * SEQ), BDL[:, g, jt * P:(jt + 1) * P], CDL[:, g, :])
                r.fill_done(last, key)
                pe.wait_ge(xw_rdy, g + 1)
                key = ("ss", g)
                r.claim(pe, key)
                for t in range(2):
                    last = mm(key, (0, 512), BTOK[:, t, g, :], XW[:, g % 2, t, :], t == 0, t == 1)
                r.fill_done(last, key)

            pe.wait_ge(xd_rdy, NX + 2 * SG_)
            r.read(pe, ("xt", NX + SG_ - 1))
            group_pre(0)
            for g in range(SG_):
                if g + 1 < SG_:
                    group_pre(g + 1)
                if g % 2 == 0:
                    w = weights(("sz", g // 2))
                along(("sz", g // 2, g % 2), w, g % 2, CHUNK)
                pe.wait_ge(w_rdy, 2 * g + 2)
                for it in range(2):
                    key = ("yo", g, it)
                    r.claim(pe, key)
                    for h in range(4):
                        for jt in range(2):
                            last = mm(key, (h * HD, (h + 1) * HD), SEG[:, jt, 1, h, it * P:(it + 1) * P],
                                      XTOK[:, jt, g * 256 + h * HD:g * 256 + (h + 1) * HD], jt == 0, jt == 1)
                    r.fill_done(last, key)
                r.read(pe, ("ss", g))
                for it in range(2):
                    key = ("yi", g, it)
                    r.claim(pe, key)
                    r.fill_done(mm(key, (0, 512), CDL[:, g, it * P:(it + 1) * P], SSB[:, g % 2, :]), key)
            pe.wait_ge(y_rdy, 1)
            for j in range(8):
                key = ("yT", j)
                r.claim(pe, key)
                for q in range(2):
                    for t in range(2):
                        k = 2 * j + q
                        last = mm(key, ((2 * q + t) * P, (2 * q + t + 1) * P), XTOK[:, t, k * P:(k + 1) * P], snake[:])
                r.fill_done(last, key)
            for j in range(8):
                r.read(pe, ("yT", j))
            YT = UT[:, :, :].rearrange("p k (q n) -> p (k q) n", q=2)
            for n in range(2):
                for c2 in range(2):
                    w = weights(("sy", n, c2))
                    for t in range(2):
                        key = ("sy", n, t)
                        if c2 == 0:
                            r.claim(pe, key)
                        for k in range(KT):
                            kk = c2 * KT + k
                            last = mm(key, (0, CHUNK), YT[:, kk, t * P:(t + 1) * P], w[:, k, :], kk == 0, kk == 15)
                        if c2 == 1:
                            r.fill_done(last, key)
                    if c2 == 0:
                        last.then_inc(part_done, 1)
            ffn(1, 2, 3)

        @block.scalar
        def _(act):
            act.wait_ge(start, 1)

            def copy(key, dst, src, func=ACT.Copy, **kw):
                r.filled(act, key)
                r.read_done(nc.scalar.activation(dst, src, func, **kw), key)

            def ada(i):
                for a in range(2):
                    for s in range(2 if i == 0 else 1):
                        for n in range(2):
                            key = ("mb", i, a, s, n)
                            copy(key, MB[:, a, s, n * CHUNK:(n + 1) * CHUNK], bank[r.bank(key)][:, :])

            def turned(tag, nt, kind):
                for k in range(KT):
                    key = ("uT", tag, k)
                    b = bank[r.bank(key)]
                    r.filled(act, key)
                    if kind is None:
                        last = nc.scalar.activation(UT[:, k, 0:nt * P], b[:, 0:nt * P], ACT.Copy)
                    else:
                        for s in range(nt // 2):
                            last = nc.scalar.activation(UT[:, k, s * SEQ:(s + 1) * SEQ], b[:, s * SEQ:(s + 1) * SEQ], ACT.Identity,
                                                        bias=COLS[:, kind, k, s:s + 1], scale=COLS[:, kind + 1, k, s:s + 1])
                    r.read_done(last, key)

            def std(n, w):
                act.wait_ge(sq_in, n)
                nc.scalar.activation(ST[:, 16:16 + w], ST[:, 0:w], ACT.Sqrt).then_inc(sq_out, 1)

            key = ("cc",)
            r.filled(act, key)
            b = bank[r.bank(key)]
            nc.scalar.activation(SC[:], b[:, 0:16].rearrange("p (s k) -> p s k", s=2), ACT.Silu)
            r.read_done(nc.scalar.activation(GB2[:], b[:, 16:24], ACT.Copy), key)
            ada(0)
            act.wait_ge(cols_rdy, 1)
            turned("m0", 4, 0)
            for h in range(GH):
                copy(("gq", h), QD[:, h, :], bank[r.bank(("gq", h))][:, :], scale=GK ** -0.5)
            for h in range(GH):
                copy(("gk", h), KD[:, h, :], bank[r.bank(("gk", h))][:, :])
            for z in range(2):
                copy(("ga", z), AT[:, z, :], bank[r.bank(("ga", z))][0:GR, :])

            def log_sigmoid(h):
                for z in range(2):
                    act.wait_ge(lsg_in, 2 * h + z + 1)
                    sl = HAT[:, h % 2, z, 0, :]
                    nc.scalar.activation(sl, sl, ACT.Exp)
                    act.drain()
                    nc.scalar.activation(sl, sl, ACT.Ln, bias=1.0).then_inc(lsg_out, 1)

            def decays(h):
                act.wait_ge(hx_in, h + 1)
                hat = HAT[:, h % 2]
                nc.scalar.activation(hat[:, 0], hat[:, 0], ACT.Exp)
                nc.scalar.activation(hat[:, 1], hat[:, 1], ACT.Exp)
                f = ST[:, 40 + 24 * (h % 2):64 + 24 * (h % 2)]
                nc.scalar.activation(f, f, ACT.Exp).then_inc(hx_out, 1)

            for what, func, dst in (("gv", ACT.Copy, V), ("gg", ACT.Silu, G)):
                for n in range(2):
                    for t in range(4):
                        key = (what, n, t)
                        copy(key, dst[:, t, n * CHUNK:(n + 1) * CHUNK], bank[r.bank(key)][:, :], func)

            def key_turns(h):
                for z in range(2):
                    key = ("kT", h, z)
                    if h >= 2 and z == 0:
                        r.filled(act, ("kvs", h - 2, 2))
                    copy(key, KTOK[:, h % 2, z], bank[r.bank(key)][:, :].rearrange("p (c n) -> p c n", c=4))

            log_sigmoid(0)
            decays(0)
            key_turns(0)
            for h in range(1, GH):
                log_sigmoid(h)
                decays(h)
                key_turns(h)
            std(1, 16)
            turned("o0", 4, None)
            std(2, 4)
            turned("f0", 4, 2)
            std(3, 4)
            ada(1)
            act.wait_ge(cols_rdy, 2)
            turned("m1", 4, 0)
            act.wait_ge(pads, 1)
            copy(("cw",), CW, bank[r.bank(("cw",))][:, 0:192].rearrange("p (m k) -> p m k", k=6))
            for m in range(NX + 2 * SG_ + 1):
                if m < NX + 2 * SG_:
                    key = ("sc", m)
                    ns = 2 if m < NX + SG_ else 1
                    if m >= 2:
                        act.wait_ge(acc_rdy, m - 1)
                    copy(key, PRE[:, m % 2, 0:ns, 2:2 + SEQ], bank[r.bank(key)][:, 0:ns * SEQ].rearrange("p (s n) -> p s n", s=ns))
                if m >= 1:
                    q = m - 1
                    act.wait_ge(acc_rdy, m)
                    if 2 <= q < NX + SG_:
                        r.filled(act, ("xt", q - 2))
                    acc = ACC[:, q % 2]
                    bias = CW[:, q, 5:6]
                    if q < NX:
                        nc.scalar.activation(XD[:, q % 2, :].rearrange("p (s n) -> p s n", s=2), acc, ACT.Silu, bias=bias).then_inc(xd_rdy, 1)
                    elif q < NX + SG_:
                        nc.scalar.activation(BDL[:, q - NX, :], acc[:, 0, :], ACT.Silu, bias=bias)
                        nc.scalar.activation(XD[:, q % 2, SEQ:2 * SEQ], acc[:, 1, :], ACT.Silu, bias=bias).then_inc(xd_rdy, 1)
                    else:
                        nc.scalar.activation(CDL[:, q - NX - SG_, :], acc[:, 0, :], ACT.Silu, bias=bias).then_inc(xd_rdy, 1)
                    if q < NX + SG_:
                        key = ("xt", q)
                        b = bank[r.bank(key)][:, :].rearrange("p (t n) -> p t n", t=4)
                        if q < NX:
                            copy(key, XTOK[:, :, q * P:(q + 1) * P], b)
                        else:
                            copy(key, BTOK[:, :, q - NX, :], b[:, 2:4, :])
            act.wait_ge(sp_in, 1)
            nc.scalar.activation(DA[:], DA[:], ACT.Exp)
            act.drain()
            nc.scalar.activation(DA[:], DA[:], ACT.Ln, bias=1.0)
            nc.scalar.activation(DROW[:, 1, :], DROW[:, 1, :], ACT.Exp).then_inc(sp_out, 1)
            copy(("cum",), CUM[:], bank[r.bank(("cum",))][:, 0:320].rearrange("p (t n) -> p t n", t=5))
            copy(("cd",), CDS[:], bank[r.bank(("cd",))][0:32, :].rearrange("p (z n) -> p z n", z=2))
            act.wait_ge(ec_in, 1)
            nc.scalar.activation(WST[:], WST[:], ACT.Exp)
            nc.scalar.activation(EC[:], CUM[:, 0:2, :], ACT.Exp).then_inc(ec_out, 1)

            def state_copy(g):
                if g >= 2:
                    r.filled(act, ("yi", g - 2, 1))
                copy(("ss", g), SSB[:, g % 2, :], bank[r.bank(("ss", g))][:, :])

            state_copy(0)
            for g in range(SG_):
                if g + 1 < SG_:
                    state_copy(g + 1)
                key = ("sz", g // 2, g % 2)
                copy(key, Z[:, g % 2, (g // 2) * CHUNK:(g // 2 + 1) * CHUNK], bank[r.bank(key)][:, :], ACT.Silu)
                for jt in range(2):
                    act.wait_ge(seg_rdy, 2 * g + jt + 1)
                    for z in range(2):
                        i0, i1 = (jt * P, SEQ) if z == 0 else (0, (jt + 1) * P)
                        for h in range(4):
                            col = z * SH + 4 * g + h
                            last = nc.scalar.activation(SEG[:, jt, z, h, :], SEG[:, jt, z, h, :], ACT.Exp,
                                                        bias=NCUM[:, jt, col:col + 1])
                    last.then_inc(seg_exp, 1)
            std(4, 2)
            for j in range(8):
                key = ("yT", j)
                copy(key, UT[:, j, :], bank[r.bank(key)][:, :])
            std(5, 2)
            turned("f1", 2, 2)
            std(6, 2)

        @block.vector
        def _(v):
            v.wait_ge(start, 1)

            def ada(i):
                v.wait_ge(abias_in, 16 * (i + 1))
                for n in range(12):
                    key = ("ada", i, n)
                    sl = slice(n * CHUNK, (n + 1) * CHUNK)
                    r.filled(v, key)
                    r.read_done(nc.vector.tensor_tensor(MROW[:, sl], bank[r.bank(key)][0:2, :], ABIAS[:, sl], ALU.add), key)
                v.drain().then_inc(mrow, 1)
                key = ("mc", i)
                r.filled(v, key)
                b = bank[r.bank(key)][:, 0:64].rearrange("p (a k s) -> p a k s", a=4, k=KT)
                nc.vector.tensor_copy(COLS[:, 0::2], b[:, 0::2])
                r.read_done(nc.vector.tensor_scalar(COLS[:, 1::2], b[:, 1::2], 1.0, None, ALU.add), key)
                v.drain().then_inc(cols_rdy, 1)

            def residual(name, args, nt, a):
                for n in range(2):
                    sl = slice(n * CHUNK, (n + 1) * CHUNK)
                    for t in range(nt):
                        key = (name, *args, n, t)
                        tmp = TMPR[:, (n * nt + t) % 2, :]
                        r.filled(v, key)
                        r.read_done(nc.vector.tensor_tensor(tmp, bank[r.bank(key)][:, :], MB[:, a, t // 2, sl], ALU.mult), key)
                        v.drain()
                        nc.vector.scalar_tensor_tensor(XA[:, t, sl], XA[:, t, sl], ALPHA, tmp, ALU.mult, ALU.add)

            def layer_norm(nth, nsq, nt):
                v.drain()
                for t in range(nt):
                    for j in range(2):
                        nc.vector.bn_stats(BN[:, t, j, :], XA[:, t, j * 512:(j + 1) * 512])
                v.drain()
                for t in range(nt):
                    nc.vector.bn_aggr(MV[:, t, :], BN[:, t, :, :].rearrange("p a b -> p (a b)"))
                v.drain()
                nc.vector.tensor_scalar(ST[:, 0:nt], MV[:, 0:nt, 1], LN_EPS, None, ALU.add).then_inc(sq_in, 1)
                v.wait_ge(sq_out, nsq)
                nc.vector.reciprocal(ST[:, 32:32 + nt], ST[:, 16:16 + nt])
                v.drain()
                for t in range(nt):
                    nc.vector.tensor_scalar(XA[:, t, :], XA[:, t, :], MV[:, t, 0:1], ST[:, 32 + t:33 + t], ALU.subtract, ALU.mult)
                v.wait_ge(ln_in, 32 * nth)
                v.drain()
                nc.vector.tensor_tensor(XA[:, 0:nt, :], XA[:, 0:nt, :], bc(LNP[:, 0, :], 1, nt), ALU.mult)
                v.drain()
                nc.vector.tensor_tensor(XA[:, 0:nt, :], XA[:, 0:nt, :], bc(LNP[:, 1, :], 1, nt), ALU.add)
                v.drain().then_inc(x_rdy, 1)

            def ffn_hidden(i, nt):
                for f in range(NF):
                    key = ("f1", i, f)
                    b = bank[r.bank(key)][:, 0:nt * P]
                    r.filled(v, key)
                    nc.vector.tensor_scalar(HT[:, f, 0:nt * P], b, 0.0, None, ALU.max)
                    v.drain()
                    r.read_done(nc.vector.tensor_tensor(HT[:, f, 0:nt * P], HT[:, f, 0:nt * P], b, ALU.mult), key)

            ada(0)
            v.wait_ge(w2_in, 64)
            r.read(v, ("cc",))

            def gate_logits(h):
                for z in range(2):
                    key = ("gl", h, z)
                    r.filled(v, key)
                    r.read_done(nc.vector.tensor_scalar(LG[:, h, z, :], bank[r.bank(key)][:, :], GB2[:, z * GH + h:z * GH + h + 1],
                                                        None, ALU.add), key)

            for h in range(GH):
                gate_logits(h)
            v.drain()

            def head_hats(h):
                hat = HAT[:, h % 2]
                for z in range(2):
                    L = LG[:, h, z, :]
                    if h >= 2 and z == 0:
                        r.filled(v, ("go", h - 2, 1))
                    nc.vector.scalar_tensor_tensor(hat[:, z, 0, :], L, -1.0, L, ALU.mult, ALU.min).then_inc(lsg_in, 1)
                for z in range(2):
                    L = LG[:, h, z, :]
                    v.wait_ge(lsg_out, 2 * h + z + 1)
                    nc.vector.scalar_tensor_tensor(L, L, 0.0, hat[:, z, 0, :], ALU.min, ALU.subtract)
                    v.drain()
                    cum = hat[:, z, 1, :]
                    nc.vector.tensor_tensor_scan(cum, RST, L, 0.0, ALU.mult, ALU.add)
                    v.drain()
                    cu = cum.rearrange("p (c n) -> p c n", c=4)
                    f = ST[:, 40 + 24 * (h % 2) + 12 * z:52 + 24 * (h % 2) + 12 * z]
                    if z == 1:
                        nc.vector.tensor_tensor(L, L, cum, ALU.subtract)
                        nc.vector.tensor_copy(f[:, 0:4], cu[:, :, P - 1])
                        v.drain()
                        nc.vector.tensor_tensor(cu, L.rearrange("p (c n) -> p c n", c=4), bc(f[:, 0:4], 2, P), ALU.add)
                        v.drain()
                    end, mid = (P - 1, P // 2 - 1) if z == 0 else (0, P // 2)
                    nc.vector.tensor_scalar(f[:, 0:4], cu[:, :, end], 1.0 / GATE_NORM, None, ALU.mult)
                    nc.vector.tensor_scalar(f[:, 4:8], cu[:, :, mid], 1.0 / GATE_NORM, None, ALU.mult)
                    v.drain()
                    nc.vector.tensor_tensor(f[:, 8:12], f[:, 0:4], f[:, 4:8], ALU.subtract)
                    nc.vector.scalar_tensor_tensor(cu, cu, 1.0 / GATE_NORM, bc(f[:, 4:8], 2, P), ALU.mult, ALU.subtract)
                    v.drain()
                    nc.vector.tensor_scalar(hat[:, z, 0, :], cum, NEGCLAMP, None, ALU.min)
                    v.drain()
                    last = nc.vector.tensor_scalar(cum, cum, -1.0, NEGCLAMP, ALU.mult, ALU.min)
                v.drain().then_inc(hx_in, 1)
                v.wait_ge(hx_out, h + 1)
                for z in range(2):
                    nc.vector.tensor_tensor(hat[:, z, 0, :], hat[:, z, 0, :], QD[:, h, :], ALU.mult)
                    nc.vector.tensor_tensor(hat[:, z, 1, :], hat[:, z, 1, :], KD[:, h, :], ALU.mult)
                v.drain().then_inc(hats, 1)

            def attn_mask(h):
                am = AM[:, h % 2].rearrange("p (c n) -> p c n", c=4)
                tmp = LG[:, h, 0, :].rearrange("p (c n) -> p c n", c=4)
                for z, dst in ((0, am), (1, tmp)):
                    key = ("A", h, z)
                    r.filled(v, key)
                    r.read_done(nc.vector.tensor_tensor(dst, bank[r.bank(key)][:, :].rearrange("p (c n) -> p c n", c=4),
                                                        bc(TRI[:, z, :], 1, 4), ALU.mult), key)
                v.drain()
                nc.vector.tensor_tensor(am, am, tmp, ALU.add).then_inc(am_rdy, 1)

            STEPS = ((2, 3), (3, 2), (0, 1))

            def states(h):
                for n in range(3):
                    key = ("kvs", h, n)
                    r.filled(v, key)
                    b = bank[r.bank(key)]
                    for z in range(2):
                        f = ST[:, 40 + 24 * (h % 2) + 12 * z:52 + 24 * (h % 2) + 12 * z]
                        ch = STEPS[n][z]
                        kv = b[:, z * GV:(z + 1) * GV]
                        if n == 0:
                            last = nc.vector.tensor_scalar(S[:, z, :], kv, f[:, 8 + ch:9 + ch], None, ALU.mult)
                        else:
                            nc.vector.tensor_scalar(S[:, z, :], S[:, z, :], f[:, ch:ch + 1], None, ALU.mult)
                            v.drain()
                            last = nc.vector.scalar_tensor_tensor(S[:, z, :], kv, f[:, 8 + ch:9 + ch], S[:, z, :], ALU.mult, ALU.add)
                    r.read_done(last, key)
                    v.drain()
                    for z in range(2):
                        f = ST[:, 40 + 24 * (h % 2) + 12 * z:52 + 24 * (h % 2) + 12 * z]
                        nxt = (STEPS[n + 1] if n < 2 else (1, 0))[z]
                        nc.vector.tensor_scalar(SRS[:, n, z, :], S[:, z, :], f[:, 4 + nxt:5 + nxt], None, ALU.mult)
                    v.drain()
                v.drain().then_inc(st_rdy, 1)

            head_hats(0)
            attn_mask(0)
            for h in range(GH):
                if h + 1 < GH:
                    head_hats(h + 1)
                    attn_mask(h + 1)
                states(h)
                for s in range(2):
                    key = ("go", h, s)
                    r.filled(v, key)
                    r.read_done(nc.vector.tensor_copy(OT[:, h, 2 * s:2 * s + 2, :],
                                                      bank[r.bank(key)][:, :].rearrange("p (j n) -> p j n", j=2)), key)
            v.drain()
            SQ = HAT.rearrange("p b z a (c n) -> p (b z a c) n", n=GV)
            for t in range(4):
                for h in range(GH):
                    sl = OT[:, h, t, :]
                    nc.vector.tensor_tensor_reduce(SQ[:, t * GH + h, :], sl, sl, 1.0 / GV, 0.0,
                                                   ALU.mult, ALU.add, ST[:, t * GH + h:t * GH + h + 1])
            v.wait_ge(gain_in, 16)
            v.drain()
            for t in range(4):
                nc.vector.tensor_tensor(G[:, t].rearrange("p (h n) -> p h n", h=GH), G[:, t].rearrange("p (h n) -> p h n", h=GH),
                                        bc(GGAIN, 1, GH), ALU.mult)
            nc.vector.tensor_scalar(ST[:, 0:16], ST[:, 0:16], RMS_EPS, None, ALU.add).then_inc(sq_in, 1)
            v.wait_ge(sq_out, 1)
            nc.vector.reciprocal(ST[:, 16:32], ST[:, 16:32])
            v.drain()
            for t in range(4):
                for h in range(GH):
                    sl = slice(h * GV, (h + 1) * GV)
                    nc.vector.scalar_tensor_tensor(OT[:, h, t, :], OT[:, h, t, :], ST[:, 16 + t * GH + h:17 + t * GH + h], G[:, t, sl],
                                                   ALU.mult, ALU.mult)
            v.drain().then_inc(o_rdy, 1)
            residual("gy", (), 4, 0)
            layer_norm(1, 2, 4)
            ffn_hidden(0, 4)
            residual("f2", (0,), 4, 1)
            layer_norm(2, 3, 4)
            ada(1)
            for b in range(2):
                nc.vector.memset(PRE[:, b], 0.0)
            v.drain().then_inc(pads, 1)
            r.read(v, ("cw",))
            for m in range(NX + 2 * SG_):
                key = ("sc", m)
                ns = 2 if m < NX + SG_ else 1
                r.read(v, key)
                if m >= 2:
                    v.wait_ge(xd_rdy, m - 1)
                acc = ACC[:, m % 2, 0:ns]
                for k in range(SCONV):
                    src = PRE[:, m % 2, 0:ns, k:k + SEQ]
                    if k == 0:
                        last = nc.vector.tensor_scalar(acc, src, CW[:, m, 0:1], None, ALU.mult)
                    else:
                        last = nc.vector.scalar_tensor_tensor(acc, src, CW[:, m, k:k + 1], acc, ALU.mult, ALU.add)
                    if k < SCONV - 1:
                        v.drain()
                last.then_inc(acc_rdy, 1)
            v.wait_ge(ssd_in, 48)
            for t in range(4):
                key = ("dt", t)
                r.filled(v, key)
                r.read_done(nc.vector.tensor_tensor(DT[:, t, :], bank[r.bank(key)][:, 0:64], DROW[:, 0, :], ALU.add), key)
            v.drain()
            nc.vector.scalar_tensor_tensor(DA[:], DT[:], -1.0, DT[:], ALU.mult, ALU.min).then_inc(sp_in, 1)
            v.wait_ge(sp_out, 1)
            nc.vector.scalar_tensor_tensor(DT[:], DT[:], 0.0, DA[:], ALU.max, ALU.add)
            nc.vector.tensor_scalar(DROW[:, 1, :], DROW[:, 1, :], -1.0, None, ALU.mult)
            v.drain()
            nc.vector.tensor_tensor(DA[:], DT[:], bc(DROW[:, 1, :], 1, 4), ALU.mult).then_inc(da_rdy, 1)
            r.read(v, ("cum",))
            nc.vector.tensor_tensor(WST[:], bc(CUM[:, 4, :], 1, 2), CUM[:, 2:4, :], ALU.subtract)
            nc.vector.tensor_scalar(NCUM[:], CUM[:, 0:2, :], -1.0, None, ALU.mult)
            v.drain().then_inc(ec_in, 1)
            v.wait_ge(ec_out, 1)
            nc.vector.tensor_tensor(WST[:], WST[:], DT[:, 2:4, :], ALU.mult)
            for t in range(2):
                r.read(v, ("xt", NX - 1))
            v.drain()

            def state_inputs(g):
                if g >= 2:
                    r.filled(v, ("ss", g - 2))
                for t in range(2):
                    for z in range(2):
                        last = nc.vector.tensor_tensor(
                            XW[:, g % 2, t, z * 256:(z + 1) * 256].rearrange("p (h n) -> p h n", h=4),
                            XTOK[:, 2 + t, g * 256:(g + 1) * 256].rearrange("p (h n) -> p h n", h=4),
                            bc(WST[:, t, z * SH + 4 * g:z * SH + 4 * g + 4], 2, HD), ALU.mult)
                last.then_inc(xw_rdy, 1)

            def group_weights(g):
                v.wait_ge(cbc_in, 32 * (g + 1))
                if g >= 1:
                    r.filled(v, ("yo", g - 1, 1))
                for jt in range(2):
                    for z in range(2):
                        nc.vector.tensor_tensor(SEG[:, jt, z], CBC[:, z], bc(NEGM[:, z, jt, :], 1, 4), ALU.add)
                    v.drain().then_inc(seg_rdy, 1)

            def group_finish(g):
                key = ("cb", g)
                for jt in range(2):
                    v.wait_ge(seg_exp, 2 * g + jt + 1)
                    for h in range(4):
                        for z in range(2):
                            col = z * SH + 4 * g + h
                            sl = SEG[:, jt, z, h, :]
                            if z == 0:
                                nc.vector.tensor_scalar(sl, sl, DT[:, jt, col:col + 1], None, ALU.mult)
                    v.drain()
                    for h in range(4):
                        col = SH + 4 * g + h
                        nc.vector.scalar_tensor_tensor(SEG[:, jt, 1, h, :], SEG[:, jt, 1, h, :], DT[:, jt, col:col + 1],
                                                       SEG[:, jt, 0, h, :], ALU.mult, ALU.add)
                    if jt == 0:
                        r.filled(v, key)
                    v.drain()
                    last = nc.vector.tensor_tensor(SEG[:, jt, 1], SEG[:, jt, 1], bc(bank[r.bank(key)][:, jt * SEQ:(jt + 1) * SEQ], 1, 4), ALU.mult)
                    if jt == 1:
                        r.read_done(last, key)
                    v.drain().then_inc(w_rdy, 1)

            def group_outputs(g):
                gs = slice(g * 256, (g + 1) * 256)
                for t in range(2):
                    xs = XTOK[:, t, gs].rearrange("p (h n) -> p h n", h=4)
                    key = ("yo", g, t)
                    if t == 0:
                        r.filled(v, ("yo", g, 1))
                    r.filled(v, key)
                    nc.vector.tensor_tensor(xs, xs, bc(DROW[:, 2, 4 * g:4 * g + 4], 2, HD), ALU.mult)
                    v.drain()
                    r.read_done(nc.vector.tensor_tensor(xs, xs, bank[r.bank(key)][:, 0:256].rearrange("p (h n) -> p h n", h=4), ALU.add), key)
                    key = ("yi", g, t)
                    r.filled(v, key)
                    yi = YI[:, t].rearrange("p (z h n) -> p z h n", z=2, h=4)
                    b = bank[r.bank(key)][:, :].rearrange("p (z h n) -> p z h n", z=2, h=4)
                    for z in range(2):
                        last = nc.vector.tensor_tensor(yi[:, z], b[:, z], bc(EC[:, t, z * SH + 4 * g:z * SH + 4 * g + 4], 2, HD), ALU.mult)
                    r.read_done(last, key)
                    for z in range(2):
                        v.drain()
                        nc.vector.tensor_tensor(xs, xs, yi[:, z], ALU.add)

            state_inputs(0)
            for g in range(SG_):
                if g + 1 < SG_:
                    state_inputs(g + 1)
                group_weights(g)
                group_finish(g)
                group_outputs(g)
            v.drain()
            for g in range(SG_):
                r.read(v, ("sz", g // 2, g % 2))
            Y = XTOK[:, 0:2, :]
            nc.vector.tensor_tensor(Y, Y, Z, ALU.mult)
            v.drain()
            for t in range(2):
                nc.vector.tensor_tensor_reduce(Z[:, t, :], XTOK[:, t, :], XTOK[:, t, :], 1.0 / SDI, 0.0, ALU.mult, ALU.add, ST[:, t:t + 1])
            v.drain()
            nc.vector.tensor_scalar(ST[:, 0:2], ST[:, 0:2], RMS_EPS, None, ALU.add).then_inc(sq_in, 1)
            v.wait_ge(sq_out, 4)
            nc.vector.reciprocal(ST[:, 16:18], ST[:, 16:18])
            v.drain()
            v.wait_ge(ng_in, 16)
            for t in range(2):
                nc.vector.scalar_tensor_tensor(XTOK[:, t, :], XTOK[:, t, :], ST[:, 16 + t:17 + t], NG, ALU.mult, ALU.mult)
            v.drain().then_inc(y_rdy, 1)
            residual("sy", (), 2, 0)
            layer_norm(3, 5, 2)
            ffn_hidden(1, 2)
            residual("f2", (1,), 2, 1)
            layer_norm(4, 6, 2)


_FIRST = ["x", "positions", "w_in", "mla_q_norm", "mla_kv_norm", "mla_w_uq", "mla_w_ukv", "w_o", "ln1_g", "ln1_b",
          "router_group_w", "router_group_b", "router_expert_w", "router_expert_b", "expert_w_gate",
          "expert_w_up", "expert_w_down", "ln2_g", "ln2_b"]
_SECOND = ["c_2", "ctx_2", "c_ctx_2", "ada_w_2", "ada_b_2", "ln_g_2", "ln_b_2", "ffn_w1_2", "ffn_w2_2",
           "gla_w_in_2", "gla_w_a2_2", "gla_b_a2_2", "gla_norm_2", "gla_w_out_2", "ssd_w_in_2", "ssd_conv_w_2",
           "ssd_conv_b_2", "ssd_dt_bias_2", "ssd_a_log_2", "ssd_d_2", "ssd_norm_2", "ssd_w_out_2"]
PARTS = (1, 2)


def hybrid_kernel(nc, io, out):
    with ExitStack() as ctx:
        c = constants(nc, ctx)
        XA = ctx.enter_context(nc.sbuf_tensor("XA", [P, 4, D], F32))
        X = XA[:, 0:TT, :]
        dram_gate = nc.dram_tensor("gate_rows", [DEPTH, NEXP, SEQ], F32, kind="Internal").ap()
        dram_cum = nc.dram_tensor("cum_rows", [2, SH, SEQ], F32, kind="Internal").ap()
        setup(nc, io, c, X)
        if 1 in PARTS:
            block1(nc, io, c, X, dram_gate)
        if 2 in PARTS:
            block2(nc, io, c, XA, dram_cum)
        stored = ctx.enter_context(nc.semaphore("stored"))
        block = ctx.enter_context(nc.Block())

        @block.sync
        def _(sp):
            sp.dma_start(out[0].rearrange("(t p) n -> p t n", p=P), X).then_inc(stored, 16)
            sp.wait_ge(stored, 16)


def kernel(**inputs):
    import numpy as _np
    import concourse.bacc as _bacc
    from concourse import mybir as _mybir
    from concourse.bass_utils import run_bass_kernel_spmd as _run

    nc = _bacc.Bacc("TRN2", target_bir_lowering=False, num_devices=1)
    arrays, io = {}, {}
    for name, a in [(n, inputs[n]) for n in _FIRST + _SECOND] + list(host_constants().items()) + list(block2_constants().items()):
        a = _np.ascontiguousarray(a)
        arrays[f"in_{name}"] = a
        io[name] = nc.dram_tensor(f"in_{name}", a.shape, _mybir.dt.from_np(a.dtype), kind="ExternalInput").ap()
    out = nc.dram_tensor("out_0", (1, SEQ, D), F32, kind="ExternalOutput").ap()
    hybrid_kernel(nc, io, out)
    r = _run(nc, [arrays], core_ids=[0])
    return r.results[0]["out_0"]
```

```python
import math
from contextlib import ExitStack

import numpy as np
import concourse.bass as bass
from concourse import mybir

F32 = mybir.dt.float32
F32R = mybir.dt.float32r
I32 = mybir.dt.int32
ALU = mybir.AluOpType
ACT = mybir.ActivationFunctionType
AX = mybir.AxisListType.X

P = 128
D = 1024
KT = D // P
SEQ = 256
TT = SEQ // P
DEPTH = 2
ALPHA = (2.0 * DEPTH) ** 0.25
LN_EPS, RMS_EPS = 1e-5, 1e-6
NEG = -1e30
TAKEN = -3e38

MLA_H, QR, KVR, NOPE, ROPE = 8, 256, 128, 64, 32
HD, IDX_H, IDX_D, TOPK = 64, 8, 32, 64
C_CQ, C_CKV, C_KPE = 0, 256, 384
C_BQ, C_BK, C_BV, C_QI, C_KI, C_WI, C_DIL = 416, 672, 736, 800, 1056, 1088, 1096
IN_COLS = 3400
DIL_COLS = 12 * HD
CHUNK = 512
N_IN = -(-IN_COLS // CHUNK)
QH = NOPE + ROPE
GROUPS, EXP_PER, NEXP, EH = 4, 8, 32, 256
NROUT = GROUPS + NEXP

HALF_M, HALF_H, HALF_I = 16, 8, 4
NFREQ = HALF_M + HALF_H + HALF_I


def host_constants():
    out = {}
    out["ident"] = np.eye(P, dtype=np.float32)
    perm = np.zeros((P, P), np.float32)
    for i in range(P):
        perm[(i if i < 64 else 191 - i), i] = 1.0
    out["snake"] = perm
    q = np.arange(P)[:, None]
    masks = np.zeros((P, 4, 3 * P), np.float32)
    for t in range(TT):
        k = np.arange((t + 1) * P)[None, :]
        diff = q + t * P - k
        kinds = [diff >= 0, (diff >= 0) & (diff <= 128), (diff >= 0) & (diff % 4 == 0), (diff >= 0) & (diff % 16 == 0)]
        for n, ok in enumerate(kinds):
            masks[:, n, (P if t else 0):(3 * P if t else P)] = np.where(ok, 0.0, NEG)
    out["masks"] = masks
    freqs = []
    for half in (HALF_M, HALF_H, HALF_I):
        rot = 2 * half
        freqs.append(np.float32(500000.0) ** (-np.arange(0, rot, 2, dtype=np.float32) / np.float32(rot)))
    out["freqs"] = np.concatenate(freqs).astype(np.float32)
    out["ramp"] = np.arange(8, 0, -1).astype(np.float32)
    return out


def bc(ap, axis, n):
    v = ap.unsqueeze(axis)
    shape = list(v.shape)
    shape[axis] = n
    return v.broadcast_to(shape)


class Ring:

    def __init__(self, full, empty):
        self.full, self.empty = full, empty
        self.uses = [0] * 8
        self.at = {}

    def plan(self, key, bank):
        self.at[key] = (bank, self.uses[bank])
        self.uses[bank] += 1

    def bank(self, key):
        return self.at[key][0]

    def claim(self, eng, key, l=0, step=0):
        b, i = self.at[key]
        eng.wait_ge(self.empty[b], l * self.uses[b] + (i + 1) + step)

    def filled(self, eng, key, l=0, step=0):
        b, i = self.at[key]
        eng.wait_ge(self.full[b], l * self.uses[b] + (i + 2) + step)

    def read(self, eng, key, l=0, step=0):
        b, i = self.at[key]
        eng.wait_ge(self.empty[b], l * self.uses[b] + (i + 2) + step)

    def fill_done(self, ins, key):
        ins.then_inc(self.full[self.at[key][0]], 1)

    def read_done(self, ins, key):
        ins.then_inc(self.empty[self.at[key][0]], 1)


def plan_block1(full, empty):
    r = Ring(full, empty)
    keys = [("xT", t, h) for t in range(TT) for h in range(2)]
    keys += [("u", c, t) for c in range(N_IN) for t in range(TT)]
    keys += [("cT", t) for t in range(TT)]
    keys += [("q", n, t) for n in range(2) for t in range(TT)]
    keys += [("kv", n, t) for n in range(2) for t in range(TT)]
    keys += [("qiT", t, h) for t in range(TT) for h in range(2)] + [("kiT",)]
    keys += [("rel", 0, j) for j in range(2)] + [("rel", 1, j) for j in range(4)]
    for u in range(-1, 12):
        g2, t2 = divmod(u + 1, 2)
        if u < 11:
            if t2 == 0:
                keys += [("qT", g2, 0), ("qT", g2, 1), ("kT", g2, 0)] + ([("kT", g2, 1)] if g2 < 5 else [])
            keys += [("s", u + 1, j) for j in range(t2 + 1)]
        if u >= 0:
            keys += [("pT", u, j) for j in range(u % 2 + 1)] + [("o", u)]
    keys += [("oT", t, h) for t in range(TT) for h in range(2)]
    keys += [("mix", n, t) for n in range(2) for t in range(TT)]
    keys += [("x2T", t, h) for t in range(TT) for h in range(2)]
    keys += [("rout", t) for t in range(TT)]
    for n, k in enumerate(keys):
        r.plan(k, n % 8)
    r.plan(("gT",), 0)
    for t in range(TT):
        for n in range(2):
            r.plan(("y", t, n), 2 * t + n)
    for e in range(NEXP):
        r.plan(("gate", e), 4 + 2 * (e % 2))
        r.plan(("up", e), 5 + 2 * (e % 2))
    return r


def block1(nc, io, c, X, dram_gate):
    with ExitStack() as ctx:
        place = [ctx]

        def sb(name, shape, dt=F32):
            return place[0].enter_context(nc.sbuf_tensor(name, shape, dt))

        def sem(name):
            return ctx.enter_context(nc.semaphore(name))

        ident, tab = c["ident"], c["tab"]
        bank = c["banks"]
        XT = sb("XT", [P, KT, SEQ])
        WD = sb("WD", [P, 2, KT, CHUNK])
        MASK = sb("MASK", [P, 4, 3 * P])
        RW = sb("RW", [P, KT, NROUT])
        RB = sb("RB", [P, NROUT])
        GN = sb("GN", [P, QR + KVR])
        MX = sb("MX", [P, 12, 4])
        SM = sb("SM", [P, 12, 4])
        ST = sb("ST", [P, 64])
        M8 = sb("M8", [P, 8])
        DW = sb("DW", [P, 3, TT, 3, 4])
        RT = sb("RT", [P, 6, TT, NROUT])
        GTT = sb("GTT", [NEXP, SEQ])
        BN = sb("BN", [P, TT, 2, 6])
        MV = sb("MV", [P, TT, 2])

        place[0] = ExitStack()
        U = sb("U", [P, TT, IN_COLS])
        QT = sb("QT", [P, 2, 4, SEQ])
        KTt = sb("KTt", [P, 2, 4, SEQ])
        PR = sb("PR", [P, 2, 4, SEQ])
        PT = sb("PT", [P, 2, 4, SEQ])
        REL = sb("REL", [P, IDX_H, SEQ])
        QIT = sb("QIT", [IDX_D, IDX_H, SEQ])
        KIT = sb("KIT", [IDX_D, SEQ])
        DMASK = sb("DMASK", [P, 3 * P])
        O = sb("O", [P, TT, D])
        OG = REL[:].rearrange("p h n -> p (h n)")[:, 0:1536].rearrange("p (t g n) -> p t g n", t=TT, g=3)
        QM = sb("QM", [P, TT, MLA_H * QH])
        KM = sb("KM", [P, TT, MLA_H, QH])
        VM = sb("VM", [P, TT, MLA_H * HD])
        CQN = sb("CQN", [P, TT, QR + KVR])
        CQT = sb("CQT", [P, 3, SEQ])
        place[0].close()
        place[0] = ctx
        LN1 = sb("LN1", [P, 2, D])
        LN2 = sb("LN2", [P, 2, D])
        SG = [sb(f"SG{s}", [P, 2 * SEQ]) for s in range(2)]
        GB = [sb(f"GB{s}", [P, SEQ]) for s in range(2)]
        HF = sb("HF", [P, 2 * SEQ])
        HH = [sb(f"HH{s}", [P, 2 * SEQ], F32R) for s in range(2)]
        HL = [sb(f"HL{s}", [P, 2 * SEQ], F32R) for s in range(2)]
        XH = sb("XH", [P, KT, SEQ], F32R)
        XL = sb("XL", [P, KT, SEQ], F32R)
        WH = [sb(f"WH{k}", [P, 2048], F32R) for k in range(3)]
        WL = [sb(f"WL{k}", [P, 2048], F32R) for k in range(3)]
        STAGE = [WD[:, :, :, :].rearrange("p s k n -> p (s k n)")[:, 2048 * k:2048 * (k + 1)] for k in range(4)]

        def stage(k, s):
            return STAGE[3 if k == 2 and s == 1 else k]

        full = [sem(f"a_full{b}") for b in range(8)]
        empty = [sem(f"a_empty{b}") for b in range(8)]
        r = plan_block1(full, empty)
        w_in = [sem(f"a_dense_landed{s}") for s in range(2)]
        kinds = ("gate", "up", "down")
        ew_in = [sem(f"a_{k}_landed") for k in kinds + ("odd_down",)]
        hi_done = [sem(f"a_{k}_high_part") for k in kinds]
        lo_done = [sem(f"a_{k}_low_part") for k in kinds]
        xh_done, xl_done = sem("a_x_high_part"), sem("a_x_low_part")
        dn_done = sem("a_down_used")
        consts_in = sem("a_layer_consts")
        ln_in = sem("a_ln_params")
        mask_in = sem("a_masks")
        cqn = sem("a_latents_normed")
        rope_b = sem("a_sparse_roped")
        rope_c = sem("a_dilated_roped")
        rope_q = sem("a_mla_roped")
        sc0 = sem("a_index_scored")
        smax = sem("a_scores_max")
        pexp = sem("a_probs")
        dilm = sem("a_dilated_max")
        dile = sem("a_dilated_exp")
        sq_in, sq_out = sem("a_var"), sem("a_std")
        o_ready = sem("a_mixed_ready")
        x_ready = sem("a_x_ready")
        rexp_in, rexp_out = sem("a_router_logits"), sem("a_router_exp")
        gate_rdy = sem("a_gates")
        gate_st = sem("a_gates_stored")
        gb_in = [sem(f"a_gate_row_landed{s}") for s in range(2)]
        h_rdy = sem("a_hidden_ready")
        start = sem("a_counters_started")

        gate_w = io["expert_w_gate"].rearrange("l g e (k p) f -> (l g e) p k f", p=P)
        up_w = io["expert_w_up"].rearrange("l g e (k p) f -> (l g e) p k f", p=P)
        down_w = io["expert_w_down"].rearrange("l g e (k p) n -> (l g e) p k n", p=P)

        def one(ap):
            return ap.rearrange("o p k n -> (o p) k n")

        block = ctx.enter_context(nc.Block())

        def chunk_src(l, n, half):
            if n < N_IN:
                c0, c1 = n * CHUNK, min(IN_COLS, (n + 1) * CHUNK)
                src = io["w_in"].rearrange("l (k p) n -> l p k n", p=P)[bass.ds(l, 1), :, 4 * half:4 * half + 4, c0:c1]
                return one(src), WD[:, n % 2, 4 * half:4 * half + 4, 0:c1 - c0]
            if n == N_IN:
                flat = WD[:, n % 2, :, :].rearrange("p k n -> p (k n)")
                if half == 0:
                    return (one(io["mla_w_uq"].rearrange("l (k p) n -> l p k n", p=P)[bass.ds(l, 1)]),
                            flat[:, 0:1536].rearrange("p (k n) -> p k n", k=2))
                return (one(io["mla_w_ukv"].rearrange("l (k p) n -> l p k n", p=P)[bass.ds(l, 1)]),
                        flat[:, 1536:2560].rearrange("p (k n) -> p k n", k=1))
            n0 = (n - N_IN - 1) * CHUNK
            src = io["w_o"].rearrange("l (k p) n -> l p k n", p=P)[bass.ds(l, 1), :, 4 * half:4 * half + 4, n0:n0 + CHUNK]
            return one(src), WD[:, n % 2, 4 * half:4 * half + 4, :]

        NCH = N_IN + 3
        last_use = [("u", n, 1) for n in range(N_IN)] + [("kv", 1, 1)] + [("mix", n, 1) for n in range(2)]

        @block.sync
        def _(sp):
            for s in full + empty + lo_done + [dn_done, dn_done, h_rdy, h_rdy]:
                sp.sem_inc(s, 1)
            sp.sem_inc(start, 1)
            sp.dma_start(MASK[:], io["masks"]).then_inc(mask_in, 16)

            def expert(l, e, k, s):
                src = (gate_w, up_w, down_w)[k][bass.ds(l * NEXP + e, 1)]
                sp.dma_start(stage(k, s).rearrange("p (k n) -> p k n", k=2 if k == 2 else KT),
                             one(src)).then_inc(ew_in[3 if k == 2 and s == 1 else k], 16)

            with sp.Fori(0, DEPTH, 1) as l:
                for n in range(NCH):
                    if n >= 2:
                        r.filled(sp, last_use[n - 2], l)
                    elif n == 0:
                        sp.wait_ge(lo_done[0], l * NEXP + 1)
                        sp.wait_ge(lo_done[1], l * NEXP + 1)
                    else:
                        sp.wait_ge(lo_done[2], l * NEXP + 1)
                    for half in range(2):
                        src, dst = chunk_src(l, n, half)
                        sp.dma_start(dst, src).then_inc(w_in[n % 2], 16)
                r.filled(sp, ("mix", 0, 1), l)
                expert(l, 0, 0, 0)
                expert(l, 0, 1, 0)
                r.filled(sp, ("mix", 1, 1), l)
                expert(l, 0, 2, 0)
                for k in range(2):
                    sp.wait_ge(lo_done[k], l * NEXP + 2)
                    expert(l, 1, k, 1)
                expert(l, 1, 2, 1)
                with sp.Fori(0, NEXP // 2 - 1, 1) as i:
                    for s in range(2):
                        e = 2 * i + (s + 2)
                        for k in range(3):
                            sp.wait_ge(lo_done[k], l * NEXP + 2 * i + (s + 2 if k == 2 else s + 3))
                            expert(l, e, k, s)

        @block.gpsimd
        def _(pool):
            pool.wait_ge(start, 1)
            with pool.Fori(0, DEPTH, 1) as l:
                lay = bass.ds(l, 1)
                pool.wait_ge(dn_done, l * NEXP + 2)
                pool.nop(nofuse=True)
                pool.dma_start(GN[:, 0:QR].unsqueeze(1), io["mla_q_norm"][lay, :].partition_broadcast(P)).then_inc(consts_in, 16)
                pool.dma_start(GN[:, QR:QR + KVR].unsqueeze(1), io["mla_kv_norm"][lay, :].partition_broadcast(P)).then_inc(consts_in, 16)
                pool.dma_start(RW[:, :, 0:GROUPS],
                               one(io["router_group_w"].rearrange("l (k p) g -> l p k g", p=P)[lay])).then_inc(consts_in, 16)
                for g in range(GROUPS):
                    pool.dma_start(RW[:, :, GROUPS + 8 * g:GROUPS + 8 * g + 8],
                                   one(io["router_expert_w"].rearrange("l g (k p) e -> l g p k e", p=P)[lay, g])).then_inc(consts_in, 16)
                pool.dma_start(RB[:, 0:GROUPS].unsqueeze(1), io["router_group_b"][lay, :].partition_broadcast(P)).then_inc(consts_in, 16)
                pool.dma_start(RB[:, GROUPS:].unsqueeze(1),
                               io["router_expert_b"].rearrange("l g e -> l (g e)")[lay, :].partition_broadcast(P)).then_inc(consts_in, 16)
                r.filled(pool, ("o", 11), l)
                pool.nop(nofuse=True)
                for n, name in enumerate(("ln1_g", "ln1_b")):
                    pool.dma_start(LN1[:, n, :].unsqueeze(1), io[name][lay, :].partition_broadcast(P)).then_inc(ln_in, 16)
                for n, name in enumerate(("ln2_g", "ln2_b")):
                    pool.dma_start(LN2[:, n, :].unsqueeze(1), io[name][lay, :].partition_broadcast(P)).then_inc(ln_in, 16)
                r.read(pool, ("gT",), l)
                pool.nop(nofuse=True)
                pool.dma_start(dram_gate[lay].rearrange("o e n -> (o e) n"), GTT[:]).then_inc(gate_st, 16)
                pool.wait_ge(gate_st, l * 16 + 16)
                pool.nop(nofuse=True)
                for s in range(2):
                    pool.dma_start(GB[s][:].unsqueeze(1), dram_gate[lay, s, :].partition_broadcast(P)).then_inc(gb_in[s], 16)
                with pool.Fori(0, NEXP // 2 - 1, 1) as i:
                    for s in range(2):
                        pool.wait_ge(h_rdy, l * NEXP + 2 * i + (s + 3))
                        pool.nop(nofuse=True)
                        pool.dma_start(GB[s][:].unsqueeze(1),
                                       dram_gate.rearrange("l e n -> (l e) n")[bass.ds(l * NEXP + 2 * i + (s + 2), 1), :]
                                       .partition_broadcast(P)).then_inc(gb_in[s], 16)

        @block.tensor
        def _(pe):
            pe.wait_ge(start, 1)

            def turn(l, key, blocks, step=P):
                r.claim(pe, key, l)
                pe.nop(nofuse=True)
                for j, src in enumerate(blocks):
                    m = src.shape[1]
                    last = nc.tensor.transpose(bank[r.bank(key)][0:m, j * P:(j + 1) * P], src, ident[:])
                r.fill_done(last, key)

            def dense(l, key, lhs, rhs, n):
                r.claim(pe, key, l)
                for k in range(len(lhs)):
                    last = nc.tensor.matmul(bank[r.bank(key)][:, 0:n], lhs[k], rhs[k],
                                            start=(k == 0), stop=(k == len(lhs) - 1))
                r.fill_done(last, key)

            def group_src(g, h, t, what):
                if g < 2:
                    hh = 4 * g + h
                    return QM[:, t, hh * QH:(hh + 1) * QH] if what == "q" else KM[:, t, hh, :]
                if g < 5:
                    c0 = C_DIL + ((g - 2) * 4 + h) * HD + (DIL_COLS if what == "k" else 0)
                    return U[:, t, c0:c0 + HD]
                return U[:, t, C_BQ + h * HD:C_BQ + (h + 1) * HD] if what == "q" else U[:, t, C_BK:C_BK + HD]

            def values(g, h, k):
                if g < 2:
                    return VM[:, k, (4 * g + h) * HD:(4 * g + h + 1) * HD]
                if g < 5:
                    c0 = C_DIL + 2 * DIL_COLS + ((g - 2) * 4 + h) * HD
                    return U[:, k, c0:c0 + HD]
                return U[:, k, C_BV:C_BV + HD]

            def group_turns(l, g):
                if g == 0:
                    pe.wait_ge(rope_q, l + 1)
                    r.read(pe, ("kv", 1, 1), l)
                if g == 2:
                    pe.wait_ge(rope_c, l + 1)
                for t in range(TT):
                    turn(l, ("qT", g, t), [group_src(g, h, t, "q") for h in range(4)])
                if g < 5:
                    for t in range(TT):
                        turn(l, ("kT", g, t), [group_src(g, h, t, "k") for h in range(4)])
                else:
                    turn(l, ("kT", g, 0), [group_src(g, 0, t, "k") for t in range(TT)])

            def scores(l, u):
                g, t = divmod(u, 2)
                dd = QH if g < 2 else HD
                r.read(pe, ("qT", g, 1), l)
                r.read(pe, ("qT", g, 0), l)
                r.read(pe, ("kT", g, 0), l)
                if g < 5:
                    r.read(pe, ("kT", g, 1), l)
                n = (t + 1) * P
                per = 4 if t == 0 else 2
                for j in range(t + 1):
                    key = ("s", u, j)
                    r.claim(pe, key, l)
                    for i in range(per):
                        h = j * per + i
                        last = nc.tensor.matmul(bank[r.bank(key)][:, i * n:(i + 1) * n],
                                                QT[0:dd, g % 2, h, t * P:(t + 1) * P],
                                                KTt[0:dd, g % 2, h if g < 5 else 0, 0:n], start=True, stop=True)
                    r.fill_done(last, key)

            def prob_turns(l, u):
                t = u % 2
                pe.wait_ge(pexp, l * 12 + (u + 1))
                if t == 0:
                    turn(l, ("pT", u, 0), [PR[:, u % 2, h, 0:P] for h in range(4)])
                else:
                    for j in range(2):
                        turn(l, ("pT", u, j), [PR[:, u % 2, 2 * j + i, k * P:(k + 1) * P] for i in range(2) for k in range(2)])

            def outputs(l, u):
                g, t = divmod(u, 2)
                key = ("o", u)
                for j in range(t + 1):
                    r.read(pe, ("pT", u, j), l)
                r.claim(pe, key, l)
                for h in range(4):
                    for k in range(t + 1):
                        last = nc.tensor.matmul(bank[r.bank(key)][:, h * HD:(h + 1) * HD],
                                                PT[:, u % 2, h, k * P:(k + 1) * P], values(g, h, k),
                                                start=(k == 0), stop=(k == t))
                r.fill_done(last, key)

            def gate_up(l, e, s, i):
                for kind, what in ((0, "gate"), (1, "up")):
                    key = (what, s)
                    pe.wait_ge(lo_done[kind], l * NEXP + 2 * i + (s + 2))
                    wh = WH[kind][:].rearrange("p (k n) -> p k n", k=KT)
                    wl = WL[kind][:].rearrange("p (k n) -> p k n", k=KT)
                    r.claim(pe, key, l, i)
                    for f in range(2):
                        for k in range(KT):
                            terms = ((wh, XH), (wh, XL), (wl, XH))
                            for q, (a, b) in enumerate(terms):
                                last = nc.tensor.matmul(bank[r.bank(key)][:, f * SEQ:(f + 1) * SEQ],
                                                        a[:, k, f * P:(f + 1) * P], b[:, k, :],
                                                        start=(k == 0 and q == 0), stop=(k == KT - 1 and q == 2))
                    r.fill_done(last, key)

            def down(l, s, i, first=False, final=False):
                pe.wait_ge(lo_done[2], l * NEXP + 2 * i + (s + 2))
                pe.wait_ge(h_rdy, l * NEXP + 2 * i + (s + 3))
                wh = WH[2][:].rearrange("p (k n) -> p k n", k=2)
                wl = WL[2][:].rearrange("p (k n) -> p k n", k=2)
                for t in range(TT):
                    for n in range(2):
                        key = ("y", t, n)
                        if first:
                            r.claim(pe, key, l)
                        for f in range(2):
                            tok = slice(f * SEQ + t * P, f * SEQ + (t + 1) * P)
                            for q, (a, b) in enumerate(((HH[s], wh), (HH[s], wl), (HL[s], wh))):
                                last = nc.tensor.matmul(bank[r.bank(key)][:, :], a[:, tok], b[:, f, n * CHUNK:(n + 1) * CHUNK],
                                                        start=(first and f == 0 and q == 0), stop=(final and f == 1 and q == 2),
                                                        skip_group_check=True)
                        if final:
                            r.fill_done(last, key)
                last.then_inc(dn_done, 1) if not final else None

            with pe.Fori(0, DEPTH, 1) as l:
                pe.wait_ge(x_ready, 2 * l + 1)
                for t in range(TT):
                    for h in range(2):
                        turn(l, ("xT", t, h), [X[:, t, (4 * h + j) * P:(4 * h + j + 1) * P] for j in range(4)])
                for t in range(TT):
                    for h in range(2):
                        r.read(pe, ("xT", t, h), l)
                for n in range(N_IN):
                    pe.wait_ge(w_in[n % 2], l * 16 * NCH + 32 * (n // 2) + 32)
                    w = min(CHUNK, IN_COLS - n * CHUNK)
                    for t in range(TT):
                        dense(l, ("u", n, t), [XT[:, k, t * P:(t + 1) * P] for k in range(KT)],
                              [WD[:, n % 2, k, 0:w] for k in range(KT)], w)
                pe.wait_ge(cqn, l + 1)
                for t in range(TT):
                    turn(l, ("cT", t), [CQN[:, t, j * P:(j + 1) * P] for j in range(3)])
                pe.wait_ge(w_in[N_IN % 2], l * 16 * NCH + 32 * (N_IN // 2) + 32)
                flat = WD[:, N_IN % 2, :, :].rearrange("p k n -> p (k n)")
                wuq = flat[:, 0:1536].rearrange("p (k n) -> p k n", k=2)
                wukv = flat[:, 1536:2560]
                for t in range(TT):
                    r.read(pe, ("cT", t), l)
                for n in range(2):
                    for t in range(TT):
                        dense(l, ("q", n, t), [CQT[:, k, t * P:(t + 1) * P] for k in range(2)],
                              [wuq[:, k, 384 * n:384 * n + 384] for k in range(2)], 384)
                for n in range(2):
                    for t in range(TT):
                        dense(l, ("kv", n, t), [CQT[:, 2, t * P:(t + 1) * P]], [wukv[:, 512 * n:512 * n + 512]], 512)
                pe.wait_ge(rope_b, l + 1)
                for t in range(TT):
                    for h in range(2):
                        turn(l, ("qiT", t, h), [U[:, t, C_QI + (4 * h + j) * IDX_D:C_QI + (4 * h + j + 1) * IDX_D] for j in range(4)])
                turn(l, ("kiT",), [U[:, t, C_KI:C_KI + IDX_D] for t in range(TT)])
                for t in range(TT):
                    for h in range(2):
                        r.read(pe, ("qiT", t, h), l)
                r.read(pe, ("kiT",), l)
                for t in range(TT):
                    n = (t + 1) * P
                    per = 4 if t == 0 else 2
                    for j in range(IDX_H // per):
                        key = ("rel", t, j)
                        r.claim(pe, key, l)
                        for i in range(per):
                            last = nc.tensor.matmul(bank[r.bank(key)][:, i * n:(i + 1) * n],
                                                    QIT[:, j * per + i, t * P:(t + 1) * P], KIT[:, 0:n], start=True, stop=True)
                        r.fill_done(last, key)
                group_turns(l, 0)
                scores(l, 0)
                for u in range(12):
                    if u < 11:
                        if u % 2 == 1:
                            group_turns(l, (u + 1) // 2)
                        scores(l, u + 1)
                    prob_turns(l, u)
                    outputs(l, u)
                pe.wait_ge(o_ready, l + 1)
                for t in range(TT):
                    for h in range(2):
                        turn(l, ("oT", t, h), [O[:, t, (4 * h + j) * P:(4 * h + j + 1) * P] for j in range(4)])
                for t in range(TT):
                    for h in range(2):
                        r.read(pe, ("oT", t, h), l)
                for n in range(2):
                    m = N_IN + 1 + n
                    pe.wait_ge(w_in[m % 2], l * 16 * NCH + 32 * (m // 2) + 32)
                    for t in range(TT):
                        dense(l, ("mix", n, t), [XT[:, k, t * P:(t + 1) * P] for k in range(KT)],
                              [WD[:, m % 2, k, :] for k in range(KT)], CHUNK)
                pe.wait_ge(x_ready, 2 * l + 2)
                for t in range(TT):
                    for h in range(2):
                        turn(l, ("x2T", t, h), [X[:, t, (4 * h + j) * P:(4 * h + j + 1) * P] for j in range(4)])
                for t in range(TT):
                    for h in range(2):
                        r.read(pe, ("x2T", t, h), l)
                pe.wait_ge(consts_in, (l + 1) * 16 * 9)
                for t in range(TT):
                    dense(l, ("rout", t), [XT[:, k, t * P:(t + 1) * P] for k in range(KT)],
                          [RW[:, k, :] for k in range(KT)], NROUT)
                pe.wait_ge(xl_done, l + 1)
                gate_up(l, 0, 0, 0)
                pe.wait_ge(gate_rdy, l + 1)
                key = ("gT",)
                r.claim(pe, key, l)
                for t in range(TT):
                    last = nc.tensor.transpose(bank[r.bank(key)][0:NEXP, t * P:(t + 1) * P], RT[:, 5, t, 0:NEXP], ident[:])
                r.fill_done(last, key)
                gate_up(l, 1, 1, 0)
                down(l, 0, 0, first=True)
                with pe.Fori(0, NEXP // 2 - 1, 1) as i:
                    gate_up(l, 0, 0, i + 1)
                    down(l, 1, i)
                    gate_up(l, 1, 1, i + 1)
                    down(l, 0, i + 1)
                down(l, 1, NEXP // 2 - 1, final=True)
                pe.drain().then_inc(dn_done, 1)

        @block.scalar
        def _(act):
            act.wait_ge(start, 1)

            def copy(l, key, dst, src, func=ACT.Copy):
                r.filled(act, key, l)
                r.read_done(nc.scalar.activation(dst, src, func), key)

            def copy_turns(l, name, dst):
                for t in range(TT):
                    for h in range(2):
                        key = (name, t, h)
                        copy(l, key, dst[:, 4 * h:4 * h + 4, t * P:(t + 1) * P],
                             bank[r.bank(key)][:, :].rearrange("p (k n) -> p k n", k=4))

            def group_copies(l, g):
                dd = QH if g < 2 else HD
                for what, dst in (("qT", QT), ("kT", KTt)):
                    for t in range(TT):
                        key = (what, g, t)
                        if key not in r.at:
                            continue
                        if g >= 2 and what == "qT" and t == 0:
                            r.filled(act, ("s", 2 * (g - 2) + 1, 1), l)
                        if what == "kT" and g == 5:
                            copy(l, key, dst[0:dd, g % 2, 0, :], bank[r.bank(key)][0:dd, 0:SEQ])
                        else:
                            copy(l, key, dst[0:dd, g % 2, :, t * P:(t + 1) * P],
                                 bank[r.bank(key)][0:dd, :].rearrange("p (h n) -> p h n", h=4))

            def high_part(l, e, k, s):
                if k == 2:
                    act.wait_ge(ew_in[2 + s], l * 8 * NEXP + 8 * e + (16 - 8 * s))
                else:
                    act.wait_ge(ew_in[k], l * 16 * NEXP + 16 * e + 16)
                nc.scalar.activation(WH[k][:], stage(k, s), ACT.Copy).then_inc(hi_done[k], 1)

            def silu(l, e, s, step):
                key = ("gate", s)
                r.filled(act, key, l, step)
                act.wait_ge(h_rdy, l * NEXP + e + 1)
                r.read_done(nc.scalar.activation(SG[s][:], bank[r.bank(key)][:, :], ACT.Silu), key)

            with act.Fori(0, DEPTH, 1) as l:
                copy_turns(l, "xT", XT)
                for n in range(N_IN):
                    w = min(CHUNK, IN_COLS - n * CHUNK)
                    for t in range(TT):
                        key = ("u", n, t)
                        copy(l, key, U[:, t, n * CHUNK:n * CHUNK + w], bank[r.bank(key)][:, 0:w])
                act.wait_ge(sq_in, 3 * l + 1)
                nc.scalar.activation(ST[:, 4:8], ST[:, 0:4], ACT.Sqrt).then_inc(sq_out, 1)
                for t in range(TT):
                    key = ("cT", t)
                    copy(l, key, CQT[:, :, t * P:(t + 1) * P], bank[r.bank(key)][:, 0:384].rearrange("p (k n) -> p k n", k=3))
                for n in range(2):
                    for t in range(TT):
                        key = ("q", n, t)
                        copy(l, key, QM[:, t, n * 384:(n + 1) * 384], bank[r.bank(key)][:, 0:384])
                for n in range(2):
                    for t in range(TT):
                        key = ("kv", n, t)
                        r.filled(act, key, l)
                        b = bank[r.bank(key)][:, :].rearrange("p (h d) -> p h d", h=4)
                        nc.scalar.activation(KM[:, t, 4 * n:4 * n + 4, 0:NOPE], b[:, :, 0:NOPE], ACT.Copy)
                        r.read_done(nc.scalar.activation(
                            VM[:, t, 256 * n:256 * n + 256].rearrange("p (h d) -> p h d", h=4), b[:, :, NOPE:], ACT.Copy), key)
                for t in range(TT):
                    for h in range(2):
                        key = ("qiT", t, h)
                        copy(l, key, QIT[:, 4 * h:4 * h + 4, t * P:(t + 1) * P],
                             bank[r.bank(key)][0:IDX_D, :].rearrange("p (h n) -> p h n", h=4))
                copy(l, ("kiT",), KIT[:], bank[r.bank(("kiT",))][0:IDX_D, 0:SEQ])
                for t in range(TT):
                    n = (t + 1) * P
                    per = 4 if t == 0 else 2
                    if t == 1:
                        act.wait_ge(sc0, l + 1)
                    for j in range(IDX_H // per):
                        key = ("rel", t, j)
                        copy(l, key, REL[:, j * per:(j + 1) * per, 0:n],
                             bank[r.bank(key)][:, 0:per * n].rearrange("p (h n) -> p h n", h=per), ACT.Relu)
                group_copies(l, 0)
                for u in range(12):
                    g, t = divmod(u, 2)
                    if u < 11 and u % 2 == 1:
                        group_copies(l, (u + 1) // 2)
                    n = (t + 1) * P
                    act.wait_ge(smax, l * 12 + (u + 1))
                    for h in range(4):
                        last = nc.scalar.activation(PR[:, u % 2, h, 0:n], PR[:, u % 2, h, 0:n], ACT.Exp,
                                                    bias=MX[:, u, h:h + 1], scale=1.0, accum_out=SM[:, u, h:h + 1])
                    last.then_inc(pexp, 1)
                    if u >= 2:
                        r.filled(act, ("o", u - 2), l)
                    if t == 0:
                        key = ("pT", u, 0)
                        copy(l, key, PT[:, 0, :, 0:P], bank[r.bank(key)][:, :].rearrange("p (h n) -> p h n", h=4))
                    else:
                        for j in range(2):
                            key = ("pT", u, j)
                            copy(l, key, PT[:, 1, 2 * j:2 * j + 2, :], bank[r.bank(key)][:, :].rearrange("p (h n) -> p h n", h=2))
                    if u == 10:
                        act.wait_ge(dilm, l + 1)
                        nc.scalar.activation(DW[:, 1], DW[:, 0], ACT.Exp).then_inc(dile, 1)
                copy_turns(l, "oT", XT)
                act.wait_ge(sq_in, 3 * l + 2)
                nc.scalar.activation(ST[:, 10:12], ST[:, 8:10], ACT.Sqrt).then_inc(sq_out, 1)
                copy_turns(l, "x2T", XT)
                act.drain()
                nc.scalar.activation(XH[:], XT[:], ACT.Copy).then_inc(xh_done, 1)
                high_part(l, 0, 0, 0)
                high_part(l, 0, 1, 0)
                act.wait_ge(rexp_in, 2 * l + 1)
                nc.scalar.activation(RT[:, 1, :, 0:GROUPS], RT[:, 1, :, 0:GROUPS], ACT.Exp).then_inc(rexp_out, 1)
                act.wait_ge(rexp_in, 2 * l + 2)
                nc.scalar.activation(ST[:, 20:22], ST[:, 18:20], ACT.Exp).then_inc(rexp_out, 1)
                copy(l, ("gT",), GTT[:], bank[r.bank(("gT",))][0:NEXP, 0:SEQ])
                high_part(l, 0, 2, 0)
                silu(l, 0, 0, 0)
                high_part(l, 1, 0, 1)
                r.filled(act, ("up", 0), l)
                high_part(l, 1, 1, 1)
                with act.Fori(0, NEXP // 2 - 1, 1) as i:
                    for s, step in ((1, i), (0, i + 1)):
                        e = 2 * step + s
                        silu(l, e, s, step)
                        high_part(l, e + 1, 0, 1 - s)
                        r.filled(act, ("up", s), l, step)
                        high_part(l, e + 1, 1, 1 - s)
                        act.wait_ge(dn_done, l * NEXP + e + 2)
                        high_part(l, e, 2, s)
                silu(l, NEXP - 1, 1, NEXP // 2 - 1)
                act.wait_ge(dn_done, l * NEXP + NEXP + 1)
                high_part(l, NEXP - 1, 2, 1)
                act.wait_ge(sq_in, 3 * l + 3)
                nc.scalar.activation(ST[:, 10:12], ST[:, 8:10], ACT.Sqrt).then_inc(sq_out, 1)

        @block.vector
        def _(v):
            v.wait_ge(start, 1)
            v.wait_ge(mask_in, 16)
            TMP = [PR[:, 0, :, :].rearrange("p h n -> p (h n)"), PR[:, 1, :, :].rearrange("p h n -> p (h n)")]

            def rope(src, heads, half, f0):
                n = TT * heads * half
                tmp = [TMP[j // 2][:, (j % 2) * n:(j % 2 + 1) * n].rearrange("p (t h d) -> p t h d", t=TT, h=heads)
                       for j in range(4)]
                cos = bc(tab[:, 0, :, f0:f0 + half], 2, heads)
                sin = bc(tab[:, 1, :, f0:f0 + half], 2, heads)
                x1, x2 = src[:, :, :, 0:half], src[:, :, :, half:2 * half]
                v.nop(nofuse=True)
                v.drain()
                nc.vector.tensor_tensor(tmp[0], x1, cos, ALU.mult)
                nc.vector.tensor_tensor(tmp[1], x2, sin, ALU.mult)
                nc.vector.tensor_tensor(tmp[2], x2, cos, ALU.mult)
                nc.vector.tensor_tensor(tmp[3], x1, sin, ALU.mult)
                v.drain()
                nc.vector.tensor_tensor(x1, tmp[0], tmp[1], ALU.subtract)
                return nc.vector.tensor_tensor(x2, tmp[2], tmp[3], ALU.add)

            def layer_norm(l, nth, LN, ready):
                v.drain()
                for t in range(TT):
                    for j in range(2):
                        nc.vector.bn_stats(BN[:, t, j, :], X[:, t, j * 512:(j + 1) * 512])
                v.drain()
                for t in range(TT):
                    nc.vector.bn_aggr(MV[:, t, :], BN[:, t, :, :].rearrange("p a b -> p (a b)"))
                v.drain()
                nc.vector.tensor_scalar(ST[:, 8:10], MV[:, :, 1], LN_EPS, None, ALU.add).then_inc(sq_in, 1)
                v.wait_ge(sq_out, 3 * l + nth)
                nc.vector.reciprocal(ST[:, 12:14], ST[:, 10:12])
                v.drain()
                for t in range(TT):
                    nc.vector.tensor_scalar(X[:, t, :], X[:, t, :], MV[:, t, 0:1], ST[:, 12 + t:13 + t], ALU.subtract, ALU.mult)
                v.wait_ge(ln_in, (l + 1) * 64)
                v.nop(nofuse=True)
                v.drain()
                nc.vector.tensor_tensor(X[:, :, :], X[:, :, :], bc(LN[:, 0, :], 1, TT), ALU.mult)
                v.drain()
                nc.vector.tensor_tensor(X[:, :, :], X[:, :, :], bc(LN[:, 1, :], 1, TT), ALU.add).then_inc(ready, 1)

            def soften(l, u):
                g, t = divmod(u, 2)
                n = (t + 1) * P
                per = 4 if t == 0 else 2
                m0 = 0 if t == 0 else P
                mask = (DMASK if g == 5 else MASK[:, (0, 0, 1, 2, 3)[g], :])[:, m0:m0 + n]
                if u >= 2:
                    r.filled(v, ("pT", u - 2, (u - 2) % 2), l)
                for j in range(t + 1):
                    key = ("s", u, j)
                    r.filled(v, key, l)
                    r.read_done(nc.vector.scalar_tensor_tensor(
                        PR[:, u % 2, j * per:(j + 1) * per, 0:n],
                        bank[r.bank(key)][:, 0:per * n].rearrange("p (h n) -> p h n", h=per),
                        (QH if g < 2 else HD) ** -0.5, bc(mask, 1, per), ALU.mult, ALU.add), key)
                v.drain()
                nc.vector.tensor_reduce(MX[:, u, :], PR[:, u % 2, :, 0:n], AX, ALU.max)
                v.drain()
                nc.vector.tensor_scalar(MX[:, u, :], MX[:, u, :], -1.0, None, ALU.mult).then_inc(smax, 1)

            def take_out(l, u):
                g, t = divmod(u, 2)
                key = ("o", u)
                r.filled(v, key, l)
                src = bank[r.bank(key)][:, 0:256]
                if 2 <= g < 5:
                    return r.read_done(nc.vector.tensor_copy(OG[:, t, g - 2, :], src), key)
                v.wait_ge(pexp, l * 12 + (u + 1))
                nc.vector.reciprocal(ST[:, 24:28], SM[:, u, :])
                v.drain()
                c0 = 256 * g if g < 2 else 512
                r.read_done(nc.vector.tensor_tensor(
                    O[:, t, c0:c0 + 256].rearrange("p (h d) -> p h d", h=4), src.rearrange("p (h d) -> p h d", h=4),
                    bc(ST[:, 24:28], 2, HD), ALU.mult), key)

            def first_max(dst, src, n, at):
                mx = ST[:, 28:30]
                nc.vector.tensor_reduce(mx, src, AX, ALU.max)
                v.drain()
                nc.vector.tensor_tensor(dst, src, bc(mx, 2, n), ALU.is_equal)
                v.drain()
                nc.vector.tensor_tensor(dst, dst, bc(c["ramp"][:, 0:n], 1, TT), ALU.mult)
                v.drain()
                nc.vector.tensor_reduce(ST[:, 30:32], dst, AX, ALU.max)
                v.drain()
                nc.vector.tensor_tensor(dst, dst, bc(ST[:, 30:32], 2, n), ALU.is_equal)
                v.drain()

            def low_part(l, e, k, s):
                v.wait_ge(hi_done[k], l * NEXP + e + 1)
                nc.vector.tensor_tensor(WL[k][:], stage(k, s), WH[k][:].bitcast(F32), ALU.subtract).then_inc(lo_done[k], 1)

            def hidden(l, e, s, step):
                key = ("up", s)
                r.filled(v, key, l, step)
                r.read(v, ("gate", s), l, step)
                r.read_done(nc.vector.tensor_tensor(SG[s][:], SG[s][:], bank[r.bank(key)][:, :], ALU.mult), key)
                v.wait_ge(gb_in[s], l * 8 * NEXP + 16 * step + 16)
                v.wait_ge(dn_done, l * NEXP + e + 1)
                v.nop(nofuse=True)
                v.drain()
                nc.vector.tensor_tensor(HF[:].rearrange("p (f n) -> p f n", f=2), SG[s][:].rearrange("p (f n) -> p f n", f=2),
                                        bc(GB[s][:], 1, 2), ALU.mult)
                v.drain()
                nc.vector.tensor_copy(HH[s][:], HF[:])
                v.drain()
                nc.vector.tensor_tensor(HL[s][:], HF[:], HH[s][:].bitcast(F32), ALU.subtract).then_inc(h_rdy, 1)

            v.drain().then_inc(x_ready, 1)
            with v.Fori(0, DEPTH, 1) as l:
                for t in range(TT):
                    r.read(v, ("u", 0, t), l)
                for t in range(TT):
                    for j, (c0, c1) in enumerate(((C_CQ, C_CKV), (C_CKV, C_KPE))):
                        nc.vector.tensor_tensor_reduce(CQN[:, t, c0:c1], U[:, t, c0:c1], U[:, t, c0:c1],
                                                       1.0 / (c1 - c0), 0.0, ALU.mult, ALU.add, ST[:, 2 * t + j:2 * t + j + 1])
                v.drain()
                nc.vector.tensor_scalar(ST[:, 0:4], ST[:, 0:4], RMS_EPS, None, ALU.add).then_inc(sq_in, 1)
                v.wait_ge(sq_out, 3 * l + 1)
                v.wait_ge(consts_in, (l + 1) * 16 * 9)
                nc.vector.reciprocal(ST[:, 4:8], ST[:, 4:8])
                v.drain()
                for t in range(TT):
                    for j, (c0, c1) in enumerate(((C_CQ, C_CKV), (C_CKV, C_KPE))):
                        last = nc.vector.scalar_tensor_tensor(CQN[:, t, c0:c1], U[:, t, c0:c1], ST[:, 4 + 2 * t + j:5 + 2 * t + j],
                                                              GN[:, c0:c1], ALU.mult, ALU.mult)
                last.then_inc(cqn, 1)
                for n in (1, 2):
                    for t in range(TT):
                        r.read(v, ("u", n, t), l)
                rope(U[:, :, C_KPE:C_KPE + ROPE].unsqueeze(2), 1, HALF_M, 0)
                rope(U[:, :, C_BQ:C_BV].rearrange("p t (h d) -> p t h d", d=HD), 5, HALF_H, HALF_M)
                rope(U[:, :, C_QI:C_WI].rearrange("p t (h d) -> p t h d", d=IDX_D), 9, HALF_I, HALF_M + HALF_H)
                nc.vector.tensor_scalar(U[:, :, C_WI:C_DIL], U[:, :, C_WI:C_DIL], IDX_D ** -0.5 * IDX_H ** -0.5, None, ALU.mult)
                nc.vector.tensor_copy(KM[:, :, :, NOPE:QH], bc(U[:, :, C_KPE:C_KPE + ROPE], 2, MLA_H))
                v.drain().then_inc(rope_b, 1)
                for n in range(2):
                    for t in range(TT):
                        r.read(v, ("q", n, t), l)
                rope(QM.rearrange("p t (h d) -> p t h d", d=QH)[:, :, :, NOPE:QH], MLA_H, HALF_M, 0).then_inc(rope_q, 1)
                for n in range(3, N_IN):
                    for t in range(TT):
                        r.read(v, ("u", n, t), l)
                rope(U[:, :, C_DIL:C_DIL + 2 * DIL_COLS].rearrange("p t (h d) -> p t h d", d=HD), 24, HALF_H, HALF_M).then_inc(rope_c, 1)
                for t in range(TT):
                    n = (t + 1) * P
                    m0 = 0 if t == 0 else P
                    per = 4 if t == 0 else 2
                    sc = DMASK[:, m0:m0 + n]
                    for h in range(IDX_H):
                        if h % per == 0:
                            r.read(v, ("rel", t, h // per), l)
                        last = nc.vector.scalar_tensor_tensor(sc, REL[:, h, 0:n], U[:, t, C_WI + h:C_WI + h + 1],
                                                              MASK[:, 0, m0:m0 + n] if h == 0 else sc, ALU.mult, ALU.add)
                        v.drain()
                    if t == 0:
                        v.drain().then_inc(sc0, 1)
                    for _ in range(TOPK // 8):
                        nc.vector.max(M8[:], sc)
                        v.drain()
                        nc.vector.match_replace(sc, M8[:], sc, TAKEN)
                        v.drain()
                    nc.vector.tensor_scalar(sc, sc, 0.5 * TAKEN, NEG, ALU.is_gt, ALU.mult)
                    v.drain()
                    nc.vector.tensor_tensor(sc, sc, MASK[:, 0, m0:m0 + n], ALU.add)
                v.drain()
                soften(l, 0)
                for u in range(12):
                    if u < 11:
                        soften(l, u + 1)
                    take_out(l, u)
                    if u == 9:
                        v.drain()
                        mg = MX[:, 4:10, :].rearrange("p (g t) h -> p t h g", g=3)
                        nc.vector.tensor_reduce(DW[:, 2, :, 0, :], mg, AX, ALU.min)
                        v.drain()
                        nc.vector.tensor_tensor(DW[:, 0], bc(DW[:, 2, :, 0, :], 2, 3),
                                                MX[:, 4:10, :].rearrange("p (g t) h -> p t g h", g=3), ALU.subtract).then_inc(dilm, 1)
                    if u == 10:
                        v.wait_ge(dile, l + 1)
                        nc.vector.tensor_tensor(DW[:, 0], DW[:, 1], SM[:, 4:10, :].rearrange("p (g t) h -> p t g h", g=3), ALU.mult)
                        v.drain()
                        nc.vector.tensor_reduce(DW[:, 2, :, 0, :], DW[:, 0].rearrange("p t g h -> p t h g"), AX, ALU.add)
                        v.drain()
                        nc.vector.reciprocal(DW[:, 2, :, 1, :], DW[:, 2, :, 0, :])
                        v.drain()
                        nc.vector.tensor_tensor(DW[:, 1], DW[:, 1], bc(DW[:, 2, :, 1, :], 2, 3), ALU.mult)
                        v.drain()
                        for t in range(TT):
                            og = OG[:, t].rearrange("p g (h d) -> p g h d", d=HD)
                            nc.vector.tensor_tensor(og, og, bc(DW[:, 1, t], 3, HD), ALU.mult)
                        v.drain()
                        nc.vector.tensor_tensor(O[:, :, 768:1024], OG[:, :, 0, :], OG[:, :, 1, :], ALU.add)
                        v.drain()
                        nc.vector.tensor_tensor(O[:, :, 768:1024], O[:, :, 768:1024], OG[:, :, 2, :], ALU.add)
                v.drain().then_inc(o_ready, 1)
                for n in range(2):
                    for t in range(TT):
                        key = ("mix", n, t)
                        xs = X[:, t, n * CHUNK:(n + 1) * CHUNK]
                        r.filled(v, key, l)
                        r.read_done(nc.vector.scalar_tensor_tensor(xs, xs, ALPHA, bank[r.bank(key)][:, :], ALU.mult, ALU.add), key)
                layer_norm(l, 2, LN1, x_ready)
                v.wait_ge(xh_done, l + 1)
                nc.vector.tensor_tensor(XL[:], XT[:], XH[:].bitcast(F32), ALU.subtract).then_inc(xl_done, 1)
                low_part(l, 0, 0, 0)
                low_part(l, 0, 1, 0)
                v.wait_ge(consts_in, (l + 1) * 16 * 9)
                for t in range(TT):
                    key = ("rout", t)
                    r.filled(v, key, l)
                    r.read_done(nc.vector.tensor_tensor(RT[:, 0, t, :], bank[r.bank(key)][:, 0:NROUT], RB[:], ALU.add), key)
                v.drain()
                lg, le = RT[:, 0, :, 0:GROUPS], RT[:, 0, :, GROUPS:]
                ghot = RT[:, 2, :, 0:GROUPS]
                first_max(ghot, lg, GROUPS, 3)
                nc.vector.tensor_tensor(RT[:, 1, :, 0:GROUPS], lg, bc(ST[:, 28:30], 2, GROUPS), ALU.subtract).then_inc(rexp_in, 1)
                le4 = le.rearrange("p t (g e) -> p t g e", g=GROUPS)
                sel4 = RT[:, 3, :, 0:NEXP].rearrange("p t (g e) -> p t g e", g=GROUPS)
                nc.vector.tensor_tensor(sel4, le4, bc(ghot, 3, EXP_PER), ALU.mult)
                v.drain()
                les = RT[:, 4, :, 0:8]
                nc.vector.tensor_reduce(les, RT[:, 3, :, 0:NEXP].rearrange("p t (g e) -> p t e g", g=GROUPS), AX, ALU.add)
                v.drain()
                hot1, hot2 = RT[:, 4, :, 8:16], RT[:, 4, :, 16:24]
                first_max(hot1, les, 8, 3)
                nc.vector.tensor_copy(ST[:, 16:18], ST[:, 28:30])
                nc.vector.scalar_tensor_tensor(les, hot1, TAKEN, les, ALU.mult, ALU.add)
                v.drain()
                first_max(hot2, les, 8, 3)
                nc.vector.tensor_tensor(ST[:, 18:20], ST[:, 28:30], ST[:, 16:18], ALU.subtract).then_inc(rexp_in, 1)
                v.wait_ge(rexp_out, 2 * l + 2)
                nc.vector.tensor_reduce(ST[:, 32:34], RT[:, 1, :, 0:GROUPS], AX, ALU.add)
                nc.vector.tensor_scalar(ST[:, 34:36], ST[:, 20:22], 1.0, None, ALU.add)
                v.drain()
                nc.vector.tensor_tensor(ST[:, 32:34], ST[:, 32:34], ST[:, 34:36], ALU.mult)
                v.drain()
                nc.vector.reciprocal(ST[:, 36:38], ST[:, 32:34])
                v.drain()
                nc.vector.tensor_tensor(ST[:, 38:40], ST[:, 36:38], ST[:, 20:22], ALU.mult)
                nc.vector.tensor_tensor(hot1, hot1, bc(ST[:, 36:38], 2, 8), ALU.mult)
                v.drain()
                nc.vector.tensor_tensor(hot2, hot2, bc(ST[:, 38:40], 2, 8), ALU.mult)
                v.drain()
                nc.vector.tensor_tensor(hot1, hot1, hot2, ALU.add)
                v.drain()
                nc.vector.tensor_tensor(RT[:, 5, :, 0:NEXP].rearrange("p t (g e) -> p t g e", g=GROUPS),
                                        bc(ghot, 3, EXP_PER), bc(hot1, 2, GROUPS), ALU.mult).then_inc(gate_rdy, 1)
                low_part(l, 0, 2, 0)
                low_part(l, 1, 0, 1)
                hidden(l, 0, 0, 0)
                low_part(l, 1, 1, 1)
                with v.Fori(0, NEXP // 2 - 1, 1) as i:
                    for s, step in ((1, i), (0, i + 1)):
                        e = 2 * step + s
                        low_part(l, e + 1, 0, 1 - s)
                        hidden(l, e, s, step)
                        low_part(l, e + 1, 1, 1 - s)
                        low_part(l, e, 2, s)
                hidden(l, NEXP - 1, 1, NEXP // 2 - 1)
                low_part(l, NEXP - 1, 2, 1)
                for t in range(TT):
                    for n in range(2):
                        key = ("y", t, n)
                        xs = X[:, t, n * CHUNK:(n + 1) * CHUNK]
                        r.filled(v, key, l)
                        r.read_done(nc.vector.scalar_tensor_tensor(xs, xs, ALPHA, bank[r.bank(key)][:, :], ALU.mult, ALU.add), key)
                layer_norm(l, 3, LN2, x_ready)


def setup(nc, io, c, X):
    ident, snake, ramp, tab = c["ident"], c["snake"], c["ramp"], c["tab"]
    with ExitStack() as ctx:
        def sb(name, shape, dt=F32):
            return ctx.enter_context(nc.sbuf_tensor(name, shape, dt))

        posi = sb("posi", [P, TT], I32)
        posf = sb("posf", [P, TT])
        freq = sb("freq", [P, NFREQ])
        ang = sb("ang", [P, TT, NFREQ])
        turns = sb("turns", [P, TT, NFREQ])
        absr = sb("absr", [P, 2, TT, NFREQ])
        loaded = ctx.enter_context(nc.semaphore("setup_loaded"))
        reduced = ctx.enter_context(nc.semaphore("setup_reduced"))
        block = ctx.enter_context(nc.Block())

        @block.sync
        def _(sp):
            sp.dma_start(posi[:].unsqueeze(2), io["positions"].rearrange("b (t p) -> p t b", p=P), allow_slow_non_contiguous=True).then_inc(loaded, 16)
            sp.dma_start(freq[:], io["freqs"].partition_broadcast(P)).then_inc(loaded, 16)
            sp.dma_start(ramp[:], io["ramp"].partition_broadcast(P)).then_inc(loaded, 16)
            sp.dma_start(ident[:], io["ident"]).then_inc(loaded, 16)
            sp.dma_start(snake[:], io["snake"]).then_inc(loaded, 16)
            sp.dma_start(X[:], io["x"][0].rearrange("(t p) n -> p t n", p=P)).then_inc(loaded, 16)
            sp.wait_ge(loaded, 96)

        @block.vector
        def _(v):
            v.wait_ge(loaded, 96)
            nc.vector.tensor_copy(posf[:], posi[:])
            v.drain()
            nc.vector.tensor_tensor(ang[:], bc(posf[:], 2, NFREQ), bc(freq[:], 1, TT), ALU.mult)
            v.drain()
            big = 1.5 * 2.0 ** 23
            nc.vector.tensor_scalar(turns[:], ang[:], 1.0 / (2 * math.pi), big, ALU.mult, ALU.add)
            v.drain()
            nc.vector.tensor_scalar(turns[:], turns[:], big, None, ALU.subtract)
            v.drain()
            c1 = 6.28125
            c2 = float(np.float32(round((2 * math.pi - c1) * 2 ** 21) / 2 ** 21))
            c3 = float(np.float32(2 * math.pi - c1 - c2))
            for part in (c1, c2, c3):
                nc.vector.scalar_tensor_tensor(ang[:], turns[:], -part, ang[:], ALU.mult, ALU.add)
                v.drain()
            nc.vector.tensor_scalar(ang[:], ang[:], 3.1415925, -3.1415925, ALU.min, ALU.max)
            v.drain()
            nc.vector.tensor_copy(absr[:, 1], ang[:])
            nc.vector.tensor_scalar(absr[:, 0], ang[:], -1.0, None, ALU.mult)
            v.drain()
            nc.vector.tensor_tensor(absr[:, 0], absr[:, 0], ang[:], ALU.max)
            v.drain()
            nc.vector.tensor_scalar(absr[:, 0], absr[:, 0], -1.0, math.pi / 2, ALU.mult, ALU.add).then_inc(reduced, 1)

        @block.scalar
        def _(act):
            act.wait_ge(reduced, 1)
            nc.scalar.activation(tab[:], absr[:], ACT.Sin)


def constants(nc, ctx):
    def sb(name, shape):
        return ctx.enter_context(nc.sbuf_tensor(name, shape, F32))

    c = {"ident": sb("ident", [P, P]), "snake": sb("snake_perm", [P, P]), "ramp": sb("ramp", [P, 8]),
         "tab": sb("tab", [P, 2, TT, NFREQ])}
    c["banks"] = [ctx.enter_context(nc.psum_tensor(f"bank{b}", [P, 512], F32)) for b in range(8)]
    return c


SLOTS = 2
NEGCLAMP = 43.0
GH, GK, GV, GR = 4, 128, 256, 16
GDK, GDV = 512, 1024
GLA_IN = 2 * GDK + 2 * GDV + 2 * GR
GATE_NORM = 16.0
DFF = 4096
NF = DFF // P
SDI, SH, SG_, SR_, SN = 2048, 32, 8, 4, 128
SCONV = 5
S_X, S_B, S_C, S_DT = 2048, 4096, 5120, 6144
NX = SDI // P
ADA = 6 * D


class Stage:

    def __init__(self, src, width, last):
        self.src, self.width, self.last = src, width, last


NB = 8
PIECES = 4


def mlp_steps():
    out = [("f1", 0, j) for j in range(4)]
    for b in range(NB):
        if b + 1 < NB:
            out += [("f1", b + 1, j) for j in range(4)]
        out += [("f2", b, n, kp) for n in range(2) for kp in range(2)]
    return out


def plan_block2(full, empty):
    r = Ring(full, empty)
    keys = [("cc",)]

    def ada(i):
        out = [("ada", i, n) for n in range(12) if i == 0] + [("mc", i)]
        return out + [("mb", i, k, s, n) for k in range(2) for s in range(2 if i == 0 else 1) for n in range(2)]

    def turned(tag):
        return [("uT", tag, k) for k in range(KT)]

    def plan_ffn(i):
        nt = 4 if i == 0 else 2
        sums = 0
        for kind, b, *rest in mlp_steps():
            if kind == "f1":
                r.plan(("f1", i, 4 * b + rest[0]), rest[0] % (2 if nt == 4 else 4))
            elif rest[1] == 1 and (nt == 4 or b == NB - 1):
                for t in range(nt):
                    r.plan(("f2", i, b, rest[0], t), 2 + sums % 6 if nt == 4 else 4 + sums)
                    sums += 1

    keys += ada(0) + turned("m0")
    keys += [("gq", h) for h in range(GH)] + [("gk", h) for h in range(GH)] + [("ga", z) for z in range(2)]
    keys += [("gl", h, z) for h in range(2) for z in range(2)] + [("gv", n, t) for n in range(2) for t in range(4)]
    keys += [("gl", h, z) for h in range(2, 4) for z in range(2)] + [("gg", n, t) for n in range(2) for t in range(4)]

    def head_pre(h):
        return [("kT", h, z) for z in range(2)] + [("A", h, z) for z in range(2)]

    keys += head_pre(0)
    for h in range(GH):
        if h + 1 < GH:
            keys += head_pre(h + 1)
        keys += [("ada", 1, 3 * h)] + [("kvs", h, n) for n in range(3)]
        keys += [("ada", 1, 3 * h + 1)] + [("go", h, s) for s in range(2)] + [("ada", 1, 3 * h + 2)]
    keys += turned("o0") + [("gy", n, t) for n in range(2) for t in range(4)] + turned("f0")
    for n, k in enumerate(keys):
        r.plan(k, n % 8)
    plan_ffn(0)
    keys = ada(1) + [("cw",)] + turned("m1")
    conv = []
    for m in range(NX + 2 * SG_ + 1):
        if m < NX + 2 * SG_:
            conv.append(("sc", m))
        if 1 <= m <= NX + SG_:
            conv.append(("xt", m - 1))
    keys += conv
    keys += [("dt", t) for t in range(4)] + [("cum",), ("cd",)]
    for n, k in enumerate(keys):
        r.plan(k, n % 8)
    for g in range(-1, SG_):
        if g + 1 < SG_:
            r.plan(("cb", g + 1), (g + 1) % 2)
            r.plan(("ss", g + 1), 2)
        if g >= 0:
            r.plan(("sz", g // 2, g % 2), 3)
            for t in range(2):
                r.plan(("yo", g, t), 4 + t)
            for t in range(2):
                r.plan(("yi", g, t), 6 + t)
    keys = [("yT", j) for j in range(8)] + [("sy", n, t) for n in range(2) for t in range(2)] + turned("f1")
    for n, k in enumerate(keys):
        r.plan(k, n % 8)
    plan_ffn(1)
    return r


def plan_chunks(io):
    def cols(name, c0, c1, r0=0, lead=0):
        w = io[name][lead]
        return w[r0:r0 + D, c0:c1].rearrange("(k p) n -> p k n", p=P)

    out = {}

    def add(key, src, last):
        out[key] = Stage(src, src.shape[2], last)

    def ada(i):
        for n in range(12):
            add(("ada", i, n), cols("ada_w_2", n * CHUNK, (n + 1) * CHUNK, lead=i), ("ada", i, n))

    def ffn(i):
        for q, (kind, b, *rest) in enumerate(mlp_steps()):
            if q % 4 == 0:
                split = 64 * i + q + 4
                if kind == "f1":
                    add(("f1", i, b), cols("ffn_w1_2", b * CHUNK, (b + 1) * CHUNK, lead=i), split)
                else:
                    add(("f2", i, b), io["ffn_w2_2"][i, b * CHUNK:(b + 1) * CHUNK, :].rearrange("(k p) n -> p k n", p=P), split)

    ada(0)
    add("gq", cols("gla_w_in_2", 0, GDK), ("gq", 3))
    add("gk", cols("gla_w_in_2", GDK, 2 * GDK), ("gk", 3))
    add("ga", cols("gla_w_in_2", 2 * GDK + 2 * GDV, GLA_IN), ("ga", 1))
    for what, c0 in (("gv", 2 * GDK), ("gg", 2 * GDK + GDV)):
        for n in range(2):
            add((what, n), cols("gla_w_in_2", c0 + n * CHUNK, c0 + (n + 1) * CHUNK), (what, n, 3))
    ada(1)
    for n in range(2):
        add(("gy", n), cols("gla_w_out_2", n * CHUNK, (n + 1) * CHUNK), ("gy", n, 3))
    ffn(0)
    for n in range(8):
        add(("sc", n), cols("ssd_w_in_2", S_X + n * CHUNK, S_X + (n + 1) * CHUNK), ("sc", 4 * n + 3))
    add("dt", cols("ssd_w_in_2", S_DT, S_DT + 2 * SH), ("dt", 3))
    for n in range(4):
        add(("sz", n), cols("ssd_w_in_2", n * CHUNK, (n + 1) * CHUNK), ("sz", n, 1))
    for n in range(2):
        for c in range(2):
            add(("sy", n, c), cols("ssd_w_out_2", n * CHUNK, (n + 1) * CHUNK, r0=c * D), ("sy", n, 1) if c == 1 else None)
    ffn(1)
    return out


def block2_constants():
    j = np.arange(P)[:, None, None] + P * np.arange(2)[None, :, None]
    i = np.arange(2 * P)[None, None, :]
    uf, ub = (j <= i).astype(np.float32), (j >= i).astype(np.float32)
    neg = np.stack([np.where(uf > 0, 0, NEG), np.where(ub > 0, 0, NEG)], 1).astype(np.float32)
    first = np.ones(512, np.float32)
    first[::P] = 0.0
    a = np.arange(P)
    tri = np.stack([a[:, None] <= a[None, :], a[:, None] >= a[None, :]], 1).astype(np.float32)
    return {"sums": np.stack([uf, ub], 1), "neg": neg, "restart": first, "tri": tri}


def block2(nc, io, c, XA, dram_cum, dram_ada):
    with ExitStack() as ctx:
        def sb(name, shape, dt=F32):
            return ctx.enter_context(nc.sbuf_tensor(name, shape, dt))

        def sem(name):
            return ctx.enter_context(nc.semaphore(name))

        ident, snake, bank = c["ident"], c["snake"], c["banks"]
        with ExitStack() as low:
            XLO = low.enter_context(nc.sbuf_tensor("XLO", [P, KT, 2 * SEQ], F32R))
            WLO = low.enter_context(nc.sbuf_tensor("WLO", [P, SLOTS, KT, CHUNK], F32R))
        UT = sb("UT", [P, KT, 2 * SEQ])
        W = sb("W", [P, SLOTS, KT, CHUNK])
        MB = sb("MB", [P, 2, 2, D])
        LNP = sb("LNP", [P, 2, D])
        NEGM = sb("NEGM", [P, 2, 2, SEQ])
        SC = sb("SC", [P, 2, KT])
        COLS = sb("COLS", [P, 4, KT, 2])
        GB2 = sb("GB2", [P, 8])
        ST = sb("ST2", [P, 96])
        BN = sb("BN2", [P, 4, 2, 6])
        MV = sb("MV2", [P, 4, 2])
        ARENA = 26624
        with ExitStack() as mlp:
            def ml(name, shape, dt=F32R):
                return mlp.enter_context(nc.sbuf_tensor(name, shape, dt))

            UH, UL = ml("UH", [P, KT, 2 * SEQ]), ml("UL", [P, KT, 2 * SEQ])
            WPH = [ml(f"WPH{q}", [P, 1024]) for q in range(PIECES)]
            WPL = [ml(f"WPL{q}", [P, 1024]) for q in range(PIECES)]
            HH = [ml(f"MHH{q}", [P, 4, 512]) for q in range(2)]
            HL = [ml(f"MHL{q}", [P, 4, 512]) for q in range(2)]
            HF = ml("MHF", [P, 512], F32)
            TMPF = ml("TMPF", [P, 2, 512], F32)
        with ExitStack() as conv:
            for name, n in (("ahead_of_XHI", 14336), ("XHI", 4096), ("ahead_of_PHI", 5120), ("PHI", 3072)):
                part = conv.enter_context(nc.sbuf_tensor(name, [P, n], F32R))
                if name == "XHI":
                    XHI = part[:].rearrange("p (k n) -> p k n", k=KT)
            PHI = part[:].rearrange("p (b k n) -> p b k n", b=3, k=KT)
        A_ = sb("ARENA", [P, ARENA])
        cur = [0]

        def carve(n):
            a = cur[0]
            cur[0] += n
            assert cur[0] <= ARENA, cur[0]
            return A_[:, a:a + n]

        QD = carve(2048).rearrange("p (h n) -> p h n", h=GH)
        KD = carve(2048).rearrange("p (h n) -> p h n", h=GH)
        V = carve(4096).rearrange("p (t n) -> p t n", t=4)
        G = carve(4096).rearrange("p (t n) -> p t n", t=4)
        lg = carve(4096)
        LG = lg.rearrange("p (h z n) -> p h z n", h=GH, z=2)
        OT = lg.rearrange("p (h t n) -> p h t n", h=GH, t=4)
        HAT = carve(4096).rearrange("p (b z a n) -> p b z a n", b=2, z=2, a=2)
        KTOK = carve(2048).rearrange("p (b z c n) -> p b z c n", b=2, z=2, c=4)
        AM = carve(1024).rearrange("p (b n) -> p b n", b=2)
        S = carve(512).rearrange("p (z n) -> p z n", z=2)
        TRI = carve(256).rearrange("p (z n) -> p z n", z=2)
        RST = carve(512)
        SRS = carve(1536).rearrange("p (s z n) -> p s z n", s=3, z=2)
        GGAIN = carve(256)
        CC = A_[0:8, 12288:12672].rearrange("p (a n) -> p a n", a=3)
        MROW = A_[0:2, 0:ADA]
        ABIAS = A_[0:2, ADA:2 * ADA]
        AT = A_[0:GR, 20480:21504].rearrange("p (z n) -> p z n", z=2)
        WA2 = A_[0:GR, 21504:22528].rearrange("p (z n) -> p z n", z=2)
        TMPR = A_[:, 18432:19456].rearrange("p (b n) -> p b n", b=2)
        cur[0] = 0
        BDL = carve(2048).rearrange("p (g n) -> p g n", g=SG_)
        CDL = carve(2048).rearrange("p (g n) -> p g n", g=SG_)
        XTOK = carve(8192).rearrange("p (t n) -> p t n", t=4)
        NG = carve(2048)
        BTOK = NG.rearrange("p (t g n) -> p t g n", t=2, g=SG_)
        Z = carve(4096).rearrange("p (t n) -> p t n", t=2)
        CBC = carve(2048).rearrange("p (z h n) -> p z h n", z=2, h=4)
        SEG = carve(4096).rearrange("p (j z h n) -> p j z h n", j=2, z=2, h=4)
        SSB = carve(1024).rearrange("p (b n) -> p b n", b=2)
        YI = carve(1024).rearrange("p (t n) -> p t n", t=2)
        CDS = A_[0:32, 25600:26112].rearrange("p (z n) -> p z n", z=2)
        XW = MB[:, :, 1, :].rearrange("p b (t n) -> p b t n", t=2)
        o = 18432
        PRE = A_[:, o:o + 1040].rearrange("p (b s n) -> p b s n", b=2, s=2)
        ACC = A_[:, o + 1040:o + 2064].rearrange("p (b s n) -> p b s n", b=2, s=2)
        XD = A_[:, o + 2064:o + 3088].rearrange("p (b n) -> p b n", b=2)
        CW = A_[:, o + 3088:o + 3280].rearrange("p (m k) -> p m k", k=6)
        SUMS = A_[:, o + 4096:o + 5120].rearrange("p (z j n) -> p z j n", z=2, j=2)
        CVR = A_[0:6, 12288:16384]
        DT = sb("DT", [P, 4, 64])
        DA = sb("DA", [P, 4, 64])
        CUM = sb("CUM", [P, 5, 64])
        WST = sb("WST", [P, 2, 64])
        EC = sb("EC", [P, 2, 64])
        NCUM = sb("NCUM", [P, 2, 64])
        DROW = sb("DROW", [P, 3, 64])

        full = [sem(f"b_full{b}") for b in range(8)]
        empty = [sem(f"b_empty{b}") for b in range(8)]
        r = plan_block2(full, empty)
        chunks = plan_chunks(io)
        order = list(chunks)
        number = {k: n for n, k in enumerate(order)}
        landed = [sem(f"b_weights_landed{s}") for s in range(SLOTS)]
        part_done = sem("b_partial_chunk_used")
        partial = [k for k in order if chunks[k].last is None]
        hi_done, lo_done = sem("b_pieces_high"), sem("b_pieces_low")
        sum_used = sem("b_sum_pieces_used")
        ul_done = sem("b_x_low_part")
        conv_hi, conv_lo = sem("b_conv_weights_high"), sem("b_conv_weights_low")
        x_low = sem("b_mixer_x_low")
        x_whole = sem("b_mixer_x_whole")
        start = sem("b_counters_started")
        rows_in = sem("b_rows_in")
        abias_in = sem("b_ada_bias")
        w2_in = sem("b_gla_small")
        ln_in = sem("b_ln_params")
        conv_in = sem("b_conv_rows")
        ssd_in = sem("b_ssd_small")
        ng_in = sem("b_norm_gain")
        gn_in = sem("b_gate_weights")
        gain_in = sem("b_gla_gain")
        cum_st = sem("b_cum_stored")
        cbc_in = sem("b_cum_spread")
        sums_in = sem("b_sum_matrices")
        mrow = sem("b_ada_rows")
        ada_st, ada_in = sem("b_ada_rows_stored"), sem("b_ada_rows_back")
        cols_rdy = sem("b_ada_cols")
        x_rdy = sem("b_x_ready")
        sq_in, sq_out = sem("b_var"), sem("b_std")
        lsg_in, lsg_out = sem("b_gate_exponent"), sem("b_gate_log")
        hx_in, hx_out = sem("b_decay_exponents"), sem("b_decays")
        hats = sem("b_hats")
        am_rdy = sem("b_attn_masked")
        st_rdy = sem("b_states")
        o_rdy = sem("b_gla_out")
        acc_rdy = sem("b_conv_sum")
        pads = sem("b_conv_pads")
        xd_rdy = sem("b_conv_out")
        sp_in, sp_out = sem("b_dt_exponent"), sem("b_dt_log")
        da_rdy = sem("b_dt_ready")
        ec_in, ec_out = sem("b_cum_ready"), sem("b_cum_exp")
        xw_rdy = sem("b_state_inputs")
        seg_rdy, seg_exp = sem("b_segments"), sem("b_segments_exp")
        w_rdy = sem("b_segment_weights")
        y_rdy = sem("b_ssd_out")

        STEPS_F = mlp_steps()

        def rows_view(slot):
            return W[:, slot].rearrange("p k n -> p (k n)").rearrange("p (k n) -> p k n", k=4)

        def piece_src(i, q):
            kind, b, *rest = STEPS_F[q]
            slot = number[(kind, i, b)] % SLOTS
            if kind == "f1":
                return W[:, slot, :, rest[0] * P:(rest[0] + 1) * P]
            return rows_view(slot)[:, 2 * rest[1]:2 * rest[1] + 2, rest[0] * CHUNK:(rest[0] + 1) * CHUNK]

        def piece_view(ring, q):
            k = 8 if STEPS_F[q][0] == "f1" else 2
            return ring[q % PIECES][:].rearrange("p (k n) -> p k n", k=k)

        def piece_used(eng, i, q):
            kind, b, *rest = STEPS_F[q]
            nt = 4 if i == 0 else 2
            if kind == "f1":
                r.filled(eng, ("f1", i, 4 * b + rest[0]))
            elif rest[1] == 1 and (nt == 4 or b == NB - 1):
                r.filled(eng, ("f2", i, b, rest[0], nt - 1))
            else:
                eng.wait_ge(sum_used, silent.index((i, q)) + 1)

        silent = [(i, q) for i in range(2) for q, st in enumerate(STEPS_F)
                  if st[0] == "f2" and not (st[3] == 1 and (i == 0 or st[1] == NB - 1))]

        block = ctx.enter_context(nc.Block())

        @block.sync
        def _(sp):
            for s in full + empty:
                sp.sem_inc(s, 1)
            sp.sem_inc(start, 1)
            for n, key in enumerate(order):
                if n >= SLOTS:
                    old = order[n - SLOTS]
                    if chunks[old].last is None:
                        sp.wait_ge(part_done, partial.index(old) + 1)
                    elif isinstance(chunks[old].last, int):
                        sp.wait_ge(lo_done, chunks[old].last)
                    else:
                        r.filled(sp, chunks[old].last)
                for half in range(2):
                    if key[0] == "f2":
                        dst = rows_view(n % SLOTS)[:, 2 * half:2 * half + 2, :]
                        src = chunks[key].src[:, 2 * half:2 * half + 2, :]
                    else:
                        dst = W[:, n % SLOTS, 4 * half:4 * half + 4, 0:chunks[key].width]
                        src = chunks[key].src[:, 4 * half:4 * half + 4, :]
                    sp.dma_start(dst, src).then_inc(landed[n % SLOTS], 16)

        @block.gpsimd
        def _(pool):
            pool.wait_ge(start, 1)
            pool.dma_start(CC[:, 0, :], io["c_2"].rearrange("b (k p) -> (b k) p", p=P)).then_inc(rows_in, 16)
            pool.dma_start(CC[:, 1, :], io["c_ctx_2"].rearrange("(k p) -> k p", p=P)).then_inc(rows_in, 16)
            pool.dma_start(CC[:, 2, :], io["gla_b_a2_2"][0].rearrange("z (h p) -> (z h) p", p=P)).then_inc(rows_in, 16)
            pool.dma_start(ABIAS, io["ada_b_2"][0, :].partition_broadcast(2)).then_inc(abias_in, 16)
            pool.dma_start(TRI, io["tri"]).then_inc(w2_in, 16)
            pool.dma_start(RST, io["restart"].partition_broadcast(P)).then_inc(w2_in, 16)
            pool.dma_start(XA[:, 2:4, :], io["ctx_2"][0].rearrange("(t p) n -> p t n", p=P)).then_inc(w2_in, 16)
            pool.dma_start(NEGM[:], io["neg"]).then_inc(w2_in, 16)

            def ln_load(i, j):
                n = 2 * i + j
                if n:
                    pool.wait_ge(x_rdy, n)
                pool.dma_start(LNP[:, 0, :], io["ln_g_2"][i, j, :].partition_broadcast(P)).then_inc(ln_in, 16)
                pool.dma_start(LNP[:, 1, :], io["ln_b_2"][i, j, :].partition_broadcast(P)).then_inc(ln_in, 16)

            ln_load(0, 0)
            r.read(pool, ("mb", 0, 1, 1, 1))
            pool.dma_start(WA2, io["gla_w_a2_2"][0].rearrange("z r n -> r z n")).then_inc(gn_in, 16)
            pool.dma_start(GGAIN, io["gla_norm_2"][0, :].partition_broadcast(P)).then_inc(gain_in, 16)
            for n in range(12):
                r.read(pool, ("ada", 1, n))
                pool.dma_start(dram_ada[:, n * CHUNK:(n + 1) * CHUNK], UT[0:2, n % KT, :]).then_inc(ada_st, 16)
                pool.wait_ge(ada_st, 16 * (n + 1))
            ln_load(0, 1)
            r.read(pool, ("f2", 0, NB - 1, 1, 3))
            pool.dma_start(MROW, dram_ada).then_inc(ada_in, 16)
            pool.dma_start(ABIAS, io["ada_b_2"][1, :].partition_broadcast(2)).then_inc(abias_in, 16)
            for k in range(SCONV):
                pool.dma_start(CVR[k:k + 1, :], io["ssd_conv_w_2"][0, k:k + 1, :]).then_inc(conv_in, 16)
            pool.dma_start(CVR[5:6, :], io["ssd_conv_b_2"][0:1, :]).then_inc(conv_in, 16)
            pool.dma_start(DROW[:, 0, :], io["ssd_dt_bias_2"].rearrange("a z h -> a (z h)")[0, :].partition_broadcast(P)).then_inc(ssd_in, 16)
            pool.dma_start(DROW[:, 1, :], io["ssd_a_log_2"].rearrange("a z h -> a (z h)")[0, :].partition_broadcast(P)).then_inc(ssd_in, 16)
            pool.dma_start(DROW[:, 2, 0:SH], io["ssd_d_2"][0, :].partition_broadcast(P)).then_inc(ssd_in, 16)
            ln_load(1, 0)
            r.read(pool, ("mb", 1, 1, 0, 1))
            pool.dma_start(SUMS, io["sums"]).then_inc(sums_in, 16)
            r.read(pool, ("cd",))
            pool.dma_start(dram_cum.rearrange("z h n -> h z n"), CDS[:]).then_inc(cum_st, 16)
            pool.wait_ge(cum_st, 16)
            for g in range(SG_):
                if g >= 1:
                    pool.wait_ge(seg_rdy, 2 * g)
                for z in range(2):
                    pool.dma_start(CBC[:, z], dram_cum[z, 4 * g:4 * g + 4, :].partition_broadcast(P)).then_inc(cbc_in, 16)
            r.filled(pool, ("ss", SG_ - 1))
            pool.dma_start(NG, io["ssd_norm_2"][0, :].partition_broadcast(P)).then_inc(ng_in, 16)
            ln_load(1, 1)

        @block.tensor
        def _(pe):
            pe.wait_ge(start, 1)

            def weights(key):
                n = number[key]
                pe.wait_ge(landed[n % SLOTS], 32 * (n // SLOTS + 1))
                return W[:, n % SLOTS]

            def mm(key, cols, lhs, rhs, start=True, stop=True, rows=P):
                return nc.tensor.matmul(bank[r.bank(key)][0:rows, cols[0]:cols[1]], lhs, rhs, start=start, stop=stop)

            def turn(key, j, src):
                m = src.shape[1]
                k = src.shape[0]
                return nc.tensor.transpose(bank[r.bank(key)][0:m, j * P:j * P + k], src, ident[0:k, 0:k])

            def ada_chunk(i, n):
                w = weights(("ada", i, n))
                key = ("ada", i, n)
                r.claim(pe, key)
                for k in range(KT):
                    last = mm(key, (0, CHUNK), SC[:, :, k], w[:, k, :], k == 0, k == KT - 1, rows=2)
                r.fill_done(last, key)

            def ada(i):
                if i == 0:
                    for n in range(12):
                        ada_chunk(0, n)
                pe.wait_ge(mrow, i + 1)
                key = ("mc", i)
                r.claim(pe, key)
                for a, kind in enumerate((0, 1, 3, 4)):
                    for k in range(KT):
                        c0 = (a * KT + k) * 2
                        last = nc.tensor.transpose(bank[r.bank(key)][:, c0:c0 + 2],
                                                   MROW[:, kind * D + k * P:kind * D + (k + 1) * P], ident[0:2, 0:2])
                r.fill_done(last, key)
                for a, kind in enumerate((2, 5)):
                    for s in range(2 if i == 0 else 1):
                        for n in range(2):
                            key = ("mb", i, a, s, n)
                            r.claim(pe, key)
                            last = mm(key, (0, CHUNK), ident[0:2, s:s + 1].broadcast_to([2, P]),
                                      MROW[:, kind * D + n * CHUNK:kind * D + (n + 1) * CHUNK])
                            r.fill_done(last, key)

            def turned(tag, src, nt, snaked):
                for k in range(KT):
                    key = ("uT", tag, k)
                    r.claim(pe, key)
                    for t in range(nt):
                        if snaked and t < 2:
                            last = mm(key, (t * P, (t + 1) * P), src(t, k), snake[:])
                        else:
                            last = turn(key, t, src(t, k))
                    r.fill_done(last, key)

            def x_tile(t, k):
                return XA[:, t, k * P:(k + 1) * P]

            def out_tile(t, k):
                return OT[:, k // 2, t, (k % 2) * P:(k % 2 + 1) * P]

            def await_turned(tag):
                for k in range(KT):
                    r.read(pe, ("uT", tag, k))

            def across(key, w, m, n0, n1, rows=P):
                r.claim(pe, key)
                for k in range(KT):
                    last = mm(key, (0, n1 - n0), w[:, k, m[0]:m[1]], UT[:, k, n0:n1], k == 0, k == KT - 1, rows=m[1] - m[0])
                r.fill_done(last, key)

            def along(key, w, t, width):
                r.claim(pe, key)
                for k in range(KT):
                    last = mm(key, (0, width), UT[:, k, t * P:(t + 1) * P], w[:, k, 0:width], k == 0, k == KT - 1)
                r.fill_done(last, key)

            def ffn(i, nt, nth):
                pe.wait_ge(x_rdy, nth)
                turned(f"f{i}", x_tile, nt, False)
                pe.wait_ge(ul_done, KT * (i + 1))
                for q, (kind, b, *rest) in enumerate(STEPS_F):
                    pe.wait_ge(lo_done, 64 * i + q + 1)
                    wh, wl = piece_view(WPH, q), piece_view(WPL, q)
                    if kind == "f1":
                        key = ("f1", i, 4 * b + rest[0])
                        r.claim(pe, key)
                        for k in range(KT):
                            for z, (a, x) in enumerate(((wh, UH), (wh, UL), (wl, UH))):
                                last = mm(key, (0, nt * P), a[:, k, :], x[:, k, 0:nt * P], k == 0 and z == 0, k == KT - 1 and z == 2)
                        r.fill_done(last, key)
                        continue
                    n, kp = rest
                    if n == 0 and kp == 0:
                        for j in range(4):
                            r.read(pe, ("f1", i, 4 * b + j))
                    last_block = nt == 4 or b == NB - 1
                    for t in range(nt):
                        key = ("f2", i, b if nt == 4 else NB - 1, n, t)
                        first = kp == 0 and (nt == 4 or b == 0)
                        if first:
                            r.claim(pe, key)
                        for k in range(2):
                            tok = slice(t * P, (t + 1) * P)
                            hh, hl = HH[b % 2][:, 2 * kp + k, tok], HL[b % 2][:, 2 * kp + k, tok]
                            for z, (a, x) in enumerate(((hh, wh), (hh, wl), (hl, wh))):
                                last = nc.tensor.matmul(bank[r.bank(key)][:, :], a, x[:, k, :], start=first and k == 0 and z == 0,
                                                        stop=last_block and kp == 1 and k == 1 and z == 2, skip_group_check=True)
                        if last_block and kp == 1:
                            r.fill_done(last, key)
                    if not (last_block and kp == 1):
                        last.then_inc(sum_used, 1)

            pe.wait_ge(rows_in, 48)
            key = ("cc",)
            r.claim(pe, key)
            for j in range(3):
                last = nc.tensor.transpose(bank[r.bank(key)][:, 8 * j:8 * j + 8], CC[:, j, :], ident[0:8, 0:8])
            r.fill_done(last, key)
            r.read(pe, key)
            ada(0)
            pe.wait_ge(w2_in, 64)
            turned("m0", x_tile, 4, True)
            await_turned("m0")
            w = weights("gq")
            for h in range(GH):
                across(("gq", h), w, (h * P, (h + 1) * P), 0, 512)
            w = weights("gk")
            for h in range(GH):
                across(("gk", h), w, (h * P, (h + 1) * P), 0, 512)
            w = weights("ga")
            for z in range(2):
                across(("ga", z), w, (z * GR, (z + 1) * GR), 0, 512)
            pe.wait_ge(gn_in, 16)
            for z in range(2):
                r.read(pe, ("ga", z))

            def logits(h):
                for z in range(2):
                    key = ("gl", h, z)
                    r.claim(pe, key)
                    r.fill_done(mm(key, (0, 512), WA2[:, z, h * P:(h + 1) * P], AT[:, z, :]), key)

            for what, h0 in (("gv", 0), ("gg", 2)):
                logits(h0)
                logits(h0 + 1)
                for n in range(2):
                    w = weights((what, n))
                    for t in range(4):
                        along((what, n, t), w, t, CHUNK)
            for n in range(2):
                for t in range(4):
                    r.read(pe, ("gv", n, t))

            def head_pre(h):
                pe.wait_ge(hats, h + 1)
                for z in range(2):
                    key = ("kT", h, z)
                    r.claim(pe, key)
                    for ch in range(4):
                        last = turn(key, ch, HAT[:, h % 2, z, 1, ch * P:(ch + 1) * P])
                    r.fill_done(last, key)
                for z in range(2):
                    key = ("A", h, z)
                    r.claim(pe, key)
                    for ch in range(4):
                        sl = slice(ch * P, (ch + 1) * P)
                        last = mm(key, (ch * P, (ch + 1) * P), HAT[:, h % 2, z, 1, sl], HAT[:, h % 2, z, 0, sl])
                    r.fill_done(last, key)

            STEPS = ((2, 3), (3, 2), (0, 1))
            head_pre(0)
            for h in range(GH):
                if h + 1 < GH:
                    head_pre(h + 1)
                ada_chunk(1, 3 * h)
                vcol = slice(h * GV, (h + 1) * GV)
                for z in range(2):
                    r.read(pe, ("kT", h, z))
                for n in range(3):
                    key = ("kvs", h, n)
                    r.claim(pe, key)
                    for z in range(2):
                        ch = STEPS[n][z]
                        last = mm(key, (z * GV, (z + 1) * GV), KTOK[:, h % 2, z, ch, :], V[:, ch, vcol])
                    r.fill_done(last, key)
                ada_chunk(1, 3 * h + 1)
                pe.wait_ge(am_rdy, h + 1)
                pe.wait_ge(st_rdy, h + 1)
                enter = {(3, 0): 0, (0, 0): 1, (1, 0): 2, (2, 1): 0, (1, 1): 1, (0, 1): 2}
                for s in range(2):
                    key = ("go", h, s)
                    r.claim(pe, key)
                    for j in range(2):
                        ch = 2 * s + j
                        cols = (j * GV, (j + 1) * GV)
                        terms = [(AM[:, h % 2, ch * P:(ch + 1) * P], V[:, ch, vcol])]
                        for z in range(2):
                            if (ch, z) in enter:
                                terms.append((HAT[:, h % 2, z, 0, ch * P:(ch + 1) * P], SRS[:, enter[(ch, z)], z, :]))
                        for q, (a, b) in enumerate(terms):
                            last = mm(key, cols, a, b, q == 0, q == len(terms) - 1)
                    r.fill_done(last, key)
                ada_chunk(1, 3 * h + 2)
            pe.wait_ge(o_rdy, 1)
            turned("o0", out_tile, 4, True)
            await_turned("o0")
            for n in range(2):
                w = weights(("gy", n))
                for t in range(4):
                    along(("gy", n, t), w, t, CHUNK)
            ffn(0, 4, 1)
            pe.wait_ge(x_rdy, 2)
            ada(1)
            pe.wait_ge(conv_in, 96)
            key = ("cw",)
            r.claim(pe, key)
            for m in range(NX + 2 * SG_):
                last = nc.tensor.transpose(bank[r.bank(key)][:, 6 * m:6 * m + 6], CVR[:, m * P:(m + 1) * P], ident[0:6, 0:6])
            r.fill_done(last, key)
            turned("m1", x_tile, 4, True)
            pe.wait_ge(x_low, KT)
            for m in range(NX + 2 * SG_ + 1):
                if m < NX + 2 * SG_:
                    key = ("sc", m)
                    pe.wait_ge(conv_lo, m + 1)
                    hi = PHI[:, m % 3]
                    lo = WLO[:, number[("sc", m // 4)] % SLOTS, :, (m % 4) * P:(m % 4 + 1) * P]
                    width = 512 if m < NX + SG_ else SEQ
                    r.claim(pe, key)
                    for k in range(KT):
                        for z, (a, x) in enumerate(((hi, XHI), (hi, XLO), (lo, XHI))):
                            last = mm(key, (0, width), a[:, k, :], x[:, k, 0:width], k == 0 and z == 0, k == KT - 1 and z == 2)
                    r.fill_done(last, key)
                if 1 <= m <= NX + SG_:
                    key = ("xt", m - 1)
                    pe.wait_ge(xd_rdy, m)
                    r.claim(pe, key)
                    for t in range(4) if m - 1 < NX else range(2, 4):
                        last = turn(key, t, XD[:, (m - 1) % 2, t * P:(t + 1) * P])
                    r.fill_done(last, key)
            w = weights("dt")
            pe.wait_ge(x_whole, 1)
            for t in range(4):
                along(("dt", t), w, t, 64)
            pe.wait_ge(da_rdy, 1)
            pe.wait_ge(sums_in, 16)
            key = ("cum",)
            r.claim(pe, key)
            for s in range(2):
                for it in range(2):
                    for z in range(2):
                        terms = [jt for jt in range(2) if (jt <= it if z == 0 else jt >= it)]
                        c0 = (2 * s + it) * 64 + z * 32
                        for q, jt in enumerate(terms):
                            last = mm(key, (c0, c0 + 32), SUMS[:, z, jt, it * P:(it + 1) * P], DA[:, 2 * s + jt, z * 32:z * 32 + 32],
                                      q == 0, q == len(terms) - 1)
            for jt in range(2):
                last = mm(key, (256, 320), SUMS[:, 0, 0, P:2 * P], DA[:, 2 + jt, :], jt == 0, jt == 1)
            r.fill_done(last, key)
            key = ("cd",)
            r.claim(pe, key)
            for z in range(2):
                for jt in range(2):
                    last = mm(key, (z * SEQ, (z + 1) * SEQ), DA[:, jt, z * 32:z * 32 + 32], SUMS[:, z, jt, :], jt == 0, jt == 1, rows=32)
            r.fill_done(last, key)

            def group_pre(g):
                key = ("cb", g)
                r.claim(pe, key)
                for jt in range(2):
                    last = mm(key, (jt * SEQ, (jt + 1) * SEQ), BDL[:, g, jt * P:(jt + 1) * P], CDL[:, g, :])
                r.fill_done(last, key)
                pe.wait_ge(xw_rdy, g + 1)
                key = ("ss", g)
                r.claim(pe, key)
                for t in range(2):
                    last = mm(key, (0, 512), BTOK[:, t, g, :], XW[:, g % 2, t, :], t == 0, t == 1)
                r.fill_done(last, key)

            pe.wait_ge(xd_rdy, NX + 2 * SG_)
            r.read(pe, ("xt", NX + SG_ - 1))
            group_pre(0)
            for g in range(SG_):
                if g + 1 < SG_:
                    group_pre(g + 1)
                if g % 2 == 0:
                    w = weights(("sz", g // 2))
                along(("sz", g // 2, g % 2), w, g % 2, CHUNK)
                pe.wait_ge(w_rdy, 2 * g + 2)
                for it in range(2):
                    key = ("yo", g, it)
                    r.claim(pe, key)
                    for h in range(4):
                        for jt in range(2):
                            last = mm(key, (h * HD, (h + 1) * HD), SEG[:, jt, 1, h, it * P:(it + 1) * P],
                                      XTOK[:, jt, g * 256 + h * HD:g * 256 + (h + 1) * HD], jt == 0, jt == 1)
                    r.fill_done(last, key)
                r.read(pe, ("ss", g))
                for it in range(2):
                    key = ("yi", g, it)
                    r.claim(pe, key)
                    r.fill_done(mm(key, (0, 512), CDL[:, g, it * P:(it + 1) * P], SSB[:, g % 2, :]), key)
            pe.wait_ge(y_rdy, 1)
            for j in range(8):
                key = ("yT", j)
                r.claim(pe, key)
                for q in range(2):
                    for t in range(2):
                        k = 2 * j + q
                        last = mm(key, ((2 * q + t) * P, (2 * q + t + 1) * P), XTOK[:, t, k * P:(k + 1) * P], snake[:])
                r.fill_done(last, key)
            for j in range(8):
                r.read(pe, ("yT", j))
            YT = UT[:, :, :].rearrange("p k (q n) -> p (k q) n", q=2)
            for n in range(2):
                for c2 in range(2):
                    w = weights(("sy", n, c2))
                    for t in range(2):
                        key = ("sy", n, t)
                        if c2 == 0:
                            r.claim(pe, key)
                        for k in range(KT):
                            kk = c2 * KT + k
                            last = mm(key, (0, CHUNK), YT[:, kk, t * P:(t + 1) * P], w[:, k, :], kk == 0, kk == 15)
                        if c2 == 1:
                            r.fill_done(last, key)
                    if c2 == 0:
                        last.then_inc(part_done, 1)
            ffn(1, 2, 3)

        @block.scalar
        def _(act):
            act.wait_ge(start, 1)

            def copy(key, dst, src, func=ACT.Copy, **kw):
                r.filled(act, key)
                r.read_done(nc.scalar.activation(dst, src, func, **kw), key)

            def ada(i):
                for a in range(2):
                    for s in range(2 if i == 0 else 1):
                        for n in range(2):
                            key = ("mb", i, a, s, n)
                            copy(key, MB[:, a, s, n * CHUNK:(n + 1) * CHUNK], bank[r.bank(key)][:, :])

            def turned(tag, nt, kind):
                for k in range(KT):
                    key = ("uT", tag, k)
                    b = bank[r.bank(key)]
                    r.filled(act, key)
                    if kind is None:
                        last = nc.scalar.activation(UT[:, k, 0:nt * P], b[:, 0:nt * P], ACT.Copy)
                    else:
                        for s in range(nt // 2):
                            last = nc.scalar.activation(UT[:, k, s * SEQ:(s + 1) * SEQ], b[:, s * SEQ:(s + 1) * SEQ], ACT.Identity,
                                                        bias=COLS[:, kind, k, s:s + 1], scale=COLS[:, kind + 1, k, s:s + 1])
                    r.read_done(last, key)

            def turned_split(tag, nt, kind, high):
                for k in range(KT):
                    key = ("uT", tag, k)
                    b = bank[r.bank(key)]
                    r.filled(act, key)
                    for dst in (UT, high):
                        for s in range(nt // 2):
                            last = nc.scalar.activation(dst[:, k, s * SEQ:(s + 1) * SEQ], b[:, s * SEQ:(s + 1) * SEQ], ACT.Identity,
                                                        bias=COLS[:, kind, k, s:s + 1], scale=COLS[:, kind + 1, k, s:s + 1])
                    r.read_done(last, key)

            def high_parts(i):
                for q, (kind, b, *rest) in enumerate(STEPS_F):
                    if q % 4 == 0:
                        n = number[(kind, i, b)]
                        act.wait_ge(landed[n % SLOTS], 32 * (n // SLOTS + 1))
                    if q >= PIECES:
                        piece_used(act, i, q - PIECES)
                    nc.scalar.activation(piece_view(WPH, q), piece_src(i, q), ACT.Copy).then_inc(hi_done, 1)

            def std(n, w):
                act.wait_ge(sq_in, n)
                nc.scalar.activation(ST[:, 16:16 + w], ST[:, 0:w], ACT.Sqrt).then_inc(sq_out, 1)

            key = ("cc",)
            r.filled(act, key)
            b = bank[r.bank(key)]
            nc.scalar.activation(SC[:], b[:, 0:16].rearrange("p (s k) -> p s k", s=2), ACT.Silu)
            r.read_done(nc.scalar.activation(GB2[:], b[:, 16:24], ACT.Copy), key)
            ada(0)
            act.wait_ge(cols_rdy, 1)
            turned("m0", 4, 0)
            for h in range(GH):
                copy(("gq", h), QD[:, h, :], bank[r.bank(("gq", h))][:, :], scale=GK ** -0.5)
            for h in range(GH):
                copy(("gk", h), KD[:, h, :], bank[r.bank(("gk", h))][:, :])
            for z in range(2):
                copy(("ga", z), AT[:, z, :], bank[r.bank(("ga", z))][0:GR, :])

            def log_sigmoid(h):
                for z in range(2):
                    act.wait_ge(lsg_in, 2 * h + z + 1)
                    sl = HAT[:, h % 2, z, 0, :]
                    nc.scalar.activation(sl, sl, ACT.Exp)
                    act.drain()
                    nc.scalar.activation(sl, sl, ACT.Ln, bias=1.0).then_inc(lsg_out, 1)

            def decays(h):
                act.wait_ge(hx_in, h + 1)
                hat = HAT[:, h % 2]
                nc.scalar.activation(hat[:, 0], hat[:, 0], ACT.Exp)
                nc.scalar.activation(hat[:, 1], hat[:, 1], ACT.Exp)
                f = ST[:, 40 + 24 * (h % 2):64 + 24 * (h % 2)]
                nc.scalar.activation(f, f, ACT.Exp).then_inc(hx_out, 1)

            for what, func, dst in (("gv", ACT.Copy, V), ("gg", ACT.Silu, G)):
                for n in range(2):
                    for t in range(4):
                        key = (what, n, t)
                        copy(key, dst[:, t, n * CHUNK:(n + 1) * CHUNK], bank[r.bank(key)][:, :], func)

            def key_turns(h):
                for z in range(2):
                    key = ("kT", h, z)
                    if h >= 2 and z == 0:
                        r.filled(act, ("kvs", h - 2, 2))
                    copy(key, KTOK[:, h % 2, z], bank[r.bank(key)][:, :].rearrange("p (c n) -> p c n", c=4))

            def ada_rows(chunks):
                for n in chunks:
                    if n >= KT:
                        act.wait_ge(ada_st, 16 * (n - KT + 1))
                    copy(("ada", 1, n), UT[0:2, n % KT, :], bank[r.bank(("ada", 1, n))][0:2, :])

            log_sigmoid(0)
            decays(0)
            key_turns(0)
            for h in range(1, GH):
                log_sigmoid(h)
                decays(h)
                key_turns(h)
                ada_rows(range(max(3 * h - 4, 0), 3 * h - 1))
            std(1, 16)
            ada_rows(range(3 * GH - 4, 12))
            act.wait_ge(ada_st, 16 * 12)
            turned("o0", 4, None)
            std(2, 4)
            turned_split("f0", 4, 2, UH)
            high_parts(0)
            std(3, 4)
            ada(1)
            act.wait_ge(cols_rdy, 2)
            act.wait_ge(pads, 1)
            copy(("cw",), CW, bank[r.bank(("cw",))][:, 0:192].rearrange("p (m k) -> p m k", k=6))
            turned_split("m1", 4, 0, XHI)

            def conv_high(m):
                n = number[("sc", m // 4)]
                if m % 4 == 0:
                    act.wait_ge(landed[n % SLOTS], 32 * (n // SLOTS + 1))
                if m >= 3:
                    r.filled(act, ("sc", m - 3))
                nc.scalar.activation(PHI[:, m % 3], W[:, n % SLOTS, :, (m % 4) * P:(m % 4 + 1) * P], ACT.Copy).then_inc(conv_hi, 1)

            conv_high(0)
            conv_high(1)
            for m in range(NX + 2 * SG_ + 1):
                if m + 2 < NX + 2 * SG_:
                    conv_high(m + 2)
                if m < NX + 2 * SG_:
                    key = ("sc", m)
                    ns = 2 if m < NX + SG_ else 1
                    if m >= 2:
                        act.wait_ge(acc_rdy, m - 1)
                    copy(key, PRE[:, m % 2, 0:ns, 2:2 + SEQ], bank[r.bank(key)][:, 0:ns * SEQ].rearrange("p (s n) -> p s n", s=ns))
                if m >= 1:
                    q = m - 1
                    act.wait_ge(acc_rdy, m)
                    if 2 <= q < NX + SG_:
                        r.filled(act, ("xt", q - 2))
                    acc = ACC[:, q % 2]
                    bias = CW[:, q, 5:6]
                    if q < NX:
                        nc.scalar.activation(XD[:, q % 2, :].rearrange("p (s n) -> p s n", s=2), acc, ACT.Silu, bias=bias).then_inc(xd_rdy, 1)
                    elif q < NX + SG_:
                        nc.scalar.activation(BDL[:, q - NX, :], acc[:, 0, :], ACT.Silu, bias=bias)
                        nc.scalar.activation(XD[:, q % 2, SEQ:2 * SEQ], acc[:, 1, :], ACT.Silu, bias=bias).then_inc(xd_rdy, 1)
                    else:
                        nc.scalar.activation(CDL[:, q - NX - SG_, :], acc[:, 0, :], ACT.Silu, bias=bias).then_inc(xd_rdy, 1)
                    if q < NX + SG_:
                        key = ("xt", q)
                        b = bank[r.bank(key)][:, :].rearrange("p (t n) -> p t n", t=4)
                        if q < NX:
                            copy(key, XTOK[:, :, q * P:(q + 1) * P], b)
                        else:
                            copy(key, BTOK[:, :, q - NX, :], b[:, 2:4, :])
            act.wait_ge(sp_in, 1)
            nc.scalar.activation(DA[:], DA[:], ACT.Exp)
            act.drain()
            nc.scalar.activation(DA[:], DA[:], ACT.Ln, bias=1.0)
            nc.scalar.activation(DROW[:, 1, :], DROW[:, 1, :], ACT.Exp).then_inc(sp_out, 1)
            copy(("cum",), CUM[:], bank[r.bank(("cum",))][:, 0:320].rearrange("p (t n) -> p t n", t=5))
            copy(("cd",), CDS[:], bank[r.bank(("cd",))][0:32, :].rearrange("p (z n) -> p z n", z=2))
            act.wait_ge(ec_in, 1)
            nc.scalar.activation(WST[:], WST[:], ACT.Exp)
            nc.scalar.activation(EC[:], CUM[:, 0:2, :], ACT.Exp).then_inc(ec_out, 1)

            def state_copy(g):
                if g >= 2:
                    r.filled(act, ("yi", g - 2, 1))
                copy(("ss", g), SSB[:, g % 2, :], bank[r.bank(("ss", g))][:, :])

            state_copy(0)
            for g in range(SG_):
                if g + 1 < SG_:
                    state_copy(g + 1)
                key = ("sz", g // 2, g % 2)
                copy(key, Z[:, g % 2, (g // 2) * CHUNK:(g // 2 + 1) * CHUNK], bank[r.bank(key)][:, :], ACT.Silu)
                for jt in range(2):
                    act.wait_ge(seg_rdy, 2 * g + jt + 1)
                    for z in range(2):
                        i0, i1 = (jt * P, SEQ) if z == 0 else (0, (jt + 1) * P)
                        for h in range(4):
                            col = z * SH + 4 * g + h
                            last = nc.scalar.activation(SEG[:, jt, z, h, :], SEG[:, jt, z, h, :], ACT.Exp,
                                                        bias=NCUM[:, jt, col:col + 1])
                    last.then_inc(seg_exp, 1)
            std(4, 2)
            for j in range(8):
                key = ("yT", j)
                copy(key, UT[:, j, :], bank[r.bank(key)][:, :])
            std(5, 2)
            turned_split("f1", 2, 2, UH)
            high_parts(1)
            std(6, 2)

        @block.vector
        def _(v):
            v.wait_ge(start, 1)

            def ada(i):
                v.wait_ge(abias_in, 16 * (i + 1))
                if i == 1:
                    v.wait_ge(ada_in, 16)
                    nc.vector.tensor_tensor(MROW, MROW, ABIAS, ALU.add)
                for n in range(12 if i == 0 else 0):
                    key = ("ada", i, n)
                    sl = slice(n * CHUNK, (n + 1) * CHUNK)
                    r.filled(v, key)
                    r.read_done(nc.vector.tensor_tensor(MROW[:, sl], bank[r.bank(key)][0:2, :], ABIAS[:, sl], ALU.add), key)
                v.drain().then_inc(mrow, 1)
                key = ("mc", i)
                r.filled(v, key)
                b = bank[r.bank(key)][:, 0:64].rearrange("p (a k s) -> p a k s", a=4, k=KT)
                nc.vector.tensor_copy(COLS[:, 0::2], b[:, 0::2])
                r.read_done(nc.vector.tensor_scalar(COLS[:, 1::2], b[:, 1::2], 1.0, None, ALU.add), key)
                v.drain().then_inc(cols_rdy, 1)

            def residual(name, args, nt, a):
                for n in range(2):
                    sl = slice(n * CHUNK, (n + 1) * CHUNK)
                    for t in range(nt):
                        key = (name, *args, n, t)
                        tmp = TMPR[:, (n * nt + t) % 2, :]
                        r.filled(v, key)
                        r.read_done(nc.vector.tensor_tensor(tmp, bank[r.bank(key)][:, :], MB[:, a, t // 2, sl], ALU.mult), key)
                        v.drain()
                        nc.vector.scalar_tensor_tensor(XA[:, t, sl], XA[:, t, sl], ALPHA, tmp, ALU.mult, ALU.add)

            def layer_norm(nth, nsq, nt):
                v.drain()
                for t in range(nt):
                    for j in range(2):
                        nc.vector.bn_stats(BN[:, t, j, :], XA[:, t, j * 512:(j + 1) * 512])
                v.drain()
                for t in range(nt):
                    nc.vector.bn_aggr(MV[:, t, :], BN[:, t, :, :].rearrange("p a b -> p (a b)"))
                v.drain()
                nc.vector.tensor_scalar(ST[:, 0:nt], MV[:, 0:nt, 1], LN_EPS, None, ALU.add).then_inc(sq_in, 1)
                v.wait_ge(sq_out, nsq)
                nc.vector.reciprocal(ST[:, 32:32 + nt], ST[:, 16:16 + nt])
                v.drain()
                for t in range(nt):
                    nc.vector.tensor_scalar(XA[:, t, :], XA[:, t, :], MV[:, t, 0:1], ST[:, 32 + t:33 + t], ALU.subtract, ALU.mult)
                v.wait_ge(ln_in, 32 * nth)
                v.drain()
                nc.vector.tensor_tensor(XA[:, 0:nt, :], XA[:, 0:nt, :], bc(LNP[:, 0, :], 1, nt), ALU.mult)
                v.drain()
                nc.vector.tensor_tensor(XA[:, 0:nt, :], XA[:, 0:nt, :], bc(LNP[:, 1, :], 1, nt), ALU.add)
                v.drain().then_inc(x_rdy, 1)

            def ffn(i, nt):
                for k in range(KT):
                    r.read(v, ("uT", f"f{i}", k))
                    nc.vector.tensor_tensor(UL[:, k, 0:nt * P], UT[:, k, 0:nt * P], UH[:, k, 0:nt * P].bitcast(F32),
                                            ALU.subtract).then_inc(ul_done, 1)

                def low_part(q):
                    v.wait_ge(hi_done, 64 * i + q + 1)
                    nc.vector.tensor_tensor(piece_view(WPL, q), piece_src(i, q), piece_view(WPH, q).bitcast(F32),
                                            ALU.subtract).then_inc(lo_done, 1)

                def hidden(b, j):
                    key = ("f1", i, 4 * b + j)
                    src = bank[r.bank(key)][:, 0:nt * P]
                    v.drain()
                    hf, hh = HF[:, 0:nt * P], HH[b % 2][:, j, 0:nt * P]
                    r.filled(v, key)
                    if b >= 2:
                        piece_used(v, i, STEPS_F.index(("f2", b - 2, 1, 1)))
                    nc.vector.tensor_scalar(hf, src, 0.0, None, ALU.max)
                    v.drain()
                    nc.vector.tensor_tensor(hf, hf, src, ALU.mult)
                    v.drain()
                    nc.vector.tensor_copy(hh, hf)
                    v.drain()
                    r.read_done(nc.vector.tensor_tensor(HL[b % 2][:, j, 0:nt * P], hf, hh.bitcast(F32), ALU.subtract), key)

                def sums(b, n):
                    if nt == 2 and b < NB - 1:
                        return
                    sl = slice(n * CHUNK, (n + 1) * CHUNK)
                    for t in range(nt):
                        key = ("f2", i, b, n, t)
                        r.filled(v, key)
                        r.read_done(nc.vector.tensor_tensor(TMPF[:, t % 2, :], bank[r.bank(key)][:, :], MB[:, 1, t // 2, sl], ALU.mult), key)
                        v.drain()
                        nc.vector.scalar_tensor_tensor(XA[:, t, sl], XA[:, t, sl], ALPHA if nt == 2 or b == 0 else 1.0, TMPF[:, t % 2, :],
                                                       ALU.mult, ALU.add)

                for q in range(2):
                    low_part(q)
                for q, (kind, b, *rest) in enumerate(STEPS_F):
                    if q + 2 < len(STEPS_F):
                        low_part(q + 2)
                    if kind == "f1":
                        hidden(b, rest[0])
                    elif rest[1] == 1:
                        sums(b, rest[0])

            ada(0)
            v.wait_ge(w2_in, 64)
            r.read(v, ("cc",))

            def gate_logits(h):
                for z in range(2):
                    key = ("gl", h, z)
                    r.filled(v, key)
                    r.read_done(nc.vector.tensor_scalar(LG[:, h, z, :], bank[r.bank(key)][:, :], GB2[:, z * GH + h:z * GH + h + 1],
                                                        None, ALU.add), key)

            for h in range(GH):
                gate_logits(h)
            v.drain()

            def head_hats(h):
                hat = HAT[:, h % 2]
                for z in range(2):
                    L = LG[:, h, z, :]
                    if h >= 2 and z == 0:
                        r.filled(v, ("go", h - 2, 1))
                    nc.vector.scalar_tensor_tensor(hat[:, z, 0, :], L, -1.0, L, ALU.mult, ALU.min).then_inc(lsg_in, 1)
                for z in range(2):
                    L = LG[:, h, z, :]
                    v.wait_ge(lsg_out, 2 * h + z + 1)
                    nc.vector.scalar_tensor_tensor(L, L, 0.0, hat[:, z, 0, :], ALU.min, ALU.subtract)
                    v.drain()
                    cum = hat[:, z, 1, :]
                    nc.vector.tensor_tensor_scan(cum, RST, L, 0.0, ALU.mult, ALU.add)
                    v.drain()
                    cu = cum.rearrange("p (c n) -> p c n", c=4)
                    f = ST[:, 40 + 24 * (h % 2) + 12 * z:52 + 24 * (h % 2) + 12 * z]
                    if z == 1:
                        nc.vector.tensor_tensor(L, L, cum, ALU.subtract)
                        nc.vector.tensor_copy(f[:, 0:4], cu[:, :, P - 1])
                        v.drain()
                        nc.vector.tensor_tensor(cu, L.rearrange("p (c n) -> p c n", c=4), bc(f[:, 0:4], 2, P), ALU.add)
                        v.drain()
                    end, mid = (P - 1, P // 2 - 1) if z == 0 else (0, P // 2)
                    nc.vector.tensor_scalar(f[:, 0:4], cu[:, :, end], 1.0 / GATE_NORM, None, ALU.mult)
                    nc.vector.tensor_scalar(f[:, 4:8], cu[:, :, mid], 1.0 / GATE_NORM, None, ALU.mult)
                    v.drain()
                    nc.vector.tensor_tensor(f[:, 8:12], f[:, 0:4], f[:, 4:8], ALU.subtract)
                    nc.vector.scalar_tensor_tensor(cu, cu, 1.0 / GATE_NORM, bc(f[:, 4:8], 2, P), ALU.mult, ALU.subtract)
                    v.drain()
                    nc.vector.tensor_scalar(hat[:, z, 0, :], cum, NEGCLAMP, None, ALU.min)
                    v.drain()
                    last = nc.vector.tensor_scalar(cum, cum, -1.0, NEGCLAMP, ALU.mult, ALU.min)
                v.drain().then_inc(hx_in, 1)
                v.wait_ge(hx_out, h + 1)
                for z in range(2):
                    nc.vector.tensor_tensor(hat[:, z, 0, :], hat[:, z, 0, :], QD[:, h, :], ALU.mult)
                    nc.vector.tensor_tensor(hat[:, z, 1, :], hat[:, z, 1, :], KD[:, h, :], ALU.mult)
                v.drain().then_inc(hats, 1)

            def attn_mask(h):
                am = AM[:, h % 2].rearrange("p (c n) -> p c n", c=4)
                tmp = LG[:, h, 0, :].rearrange("p (c n) -> p c n", c=4)
                for z, dst in ((0, am), (1, tmp)):
                    key = ("A", h, z)
                    r.filled(v, key)
                    r.read_done(nc.vector.tensor_tensor(dst, bank[r.bank(key)][:, :].rearrange("p (c n) -> p c n", c=4),
                                                        bc(TRI[:, z, :], 1, 4), ALU.mult), key)
                v.drain()
                nc.vector.tensor_tensor(am, am, tmp, ALU.add).then_inc(am_rdy, 1)

            STEPS = ((2, 3), (3, 2), (0, 1))

            def states(h):
                for n in range(3):
                    key = ("kvs", h, n)
                    r.filled(v, key)
                    b = bank[r.bank(key)]
                    for z in range(2):
                        f = ST[:, 40 + 24 * (h % 2) + 12 * z:52 + 24 * (h % 2) + 12 * z]
                        ch = STEPS[n][z]
                        kv = b[:, z * GV:(z + 1) * GV]
                        if n == 0:
                            last = nc.vector.tensor_scalar(S[:, z, :], kv, f[:, 8 + ch:9 + ch], None, ALU.mult)
                        else:
                            nc.vector.tensor_scalar(S[:, z, :], S[:, z, :], f[:, ch:ch + 1], None, ALU.mult)
                            v.drain()
                            last = nc.vector.scalar_tensor_tensor(S[:, z, :], kv, f[:, 8 + ch:9 + ch], S[:, z, :], ALU.mult, ALU.add)
                    r.read_done(last, key)
                    v.drain()
                    for z in range(2):
                        f = ST[:, 40 + 24 * (h % 2) + 12 * z:52 + 24 * (h % 2) + 12 * z]
                        nxt = (STEPS[n + 1] if n < 2 else (1, 0))[z]
                        nc.vector.tensor_scalar(SRS[:, n, z, :], S[:, z, :], f[:, 4 + nxt:5 + nxt], None, ALU.mult)
                    v.drain()
                v.drain().then_inc(st_rdy, 1)

            head_hats(0)
            attn_mask(0)
            for h in range(GH):
                if h + 1 < GH:
                    head_hats(h + 1)
                    attn_mask(h + 1)
                states(h)
                for s in range(2):
                    key = ("go", h, s)
                    r.filled(v, key)
                    r.read_done(nc.vector.tensor_copy(OT[:, h, 2 * s:2 * s + 2, :],
                                                      bank[r.bank(key)][:, :].rearrange("p (j n) -> p j n", j=2)), key)
            v.drain()
            SQ = HAT.rearrange("p b z a (c n) -> p (b z a c) n", n=GV)
            for t in range(4):
                for h in range(GH):
                    sl = OT[:, h, t, :]
                    nc.vector.tensor_tensor_reduce(SQ[:, t * GH + h, :], sl, sl, 1.0 / GV, 0.0,
                                                   ALU.mult, ALU.add, ST[:, t * GH + h:t * GH + h + 1])
            v.wait_ge(gain_in, 16)
            v.drain()
            for t in range(4):
                nc.vector.tensor_tensor(G[:, t].rearrange("p (h n) -> p h n", h=GH), G[:, t].rearrange("p (h n) -> p h n", h=GH),
                                        bc(GGAIN, 1, GH), ALU.mult)
            nc.vector.tensor_scalar(ST[:, 0:16], ST[:, 0:16], RMS_EPS, None, ALU.add).then_inc(sq_in, 1)
            v.wait_ge(sq_out, 1)
            nc.vector.reciprocal(ST[:, 16:32], ST[:, 16:32])
            v.drain()
            for t in range(4):
                for h in range(GH):
                    sl = slice(h * GV, (h + 1) * GV)
                    nc.vector.scalar_tensor_tensor(OT[:, h, t, :], OT[:, h, t, :], ST[:, 16 + t * GH + h:17 + t * GH + h], G[:, t, sl],
                                                   ALU.mult, ALU.mult)
            v.drain().then_inc(o_rdy, 1)
            residual("gy", (), 4, 0)
            layer_norm(1, 2, 4)
            ffn(0, 4)
            layer_norm(2, 3, 4)
            ada(1)
            for b in range(2):
                nc.vector.memset(PRE[:, b], 0.0)
            v.drain().then_inc(pads, 1)
            r.read(v, ("cw",))
            for k in range(KT):
                r.read(v, ("uT", "m1", k))
                nc.vector.tensor_tensor(XLO[:, k], UT[:, k], XHI[:, k].bitcast(F32), ALU.subtract).then_inc(x_low, 1)

            def conv_low(m):
                w = (slice(None), number[("sc", m // 4)] % SLOTS, slice(None), slice((m % 4) * P, (m % 4 + 1) * P))
                v.wait_ge(conv_hi, m + 1)
                nc.vector.tensor_tensor(WLO[w], W[w], PHI[:, m % 3].bitcast(F32), ALU.subtract).then_inc(conv_lo, 1)

            conv_low(0)
            conv_low(1)
            for m in range(NX + 2 * SG_):
                if m + 2 < NX + 2 * SG_:
                    conv_low(m + 2)
                key = ("sc", m)
                ns = 2 if m < NX + SG_ else 1
                r.read(v, key)
                if m >= 2:
                    v.wait_ge(xd_rdy, m - 1)
                acc = ACC[:, m % 2, 0:ns]
                for k in range(SCONV):
                    src = PRE[:, m % 2, 0:ns, k:k + SEQ]
                    if k == 0:
                        last = nc.vector.tensor_scalar(acc, src, CW[:, m, 0:1], None, ALU.mult)
                    else:
                        last = nc.vector.scalar_tensor_tensor(acc, src, CW[:, m, k:k + 1], acc, ALU.mult, ALU.add)
                    if k < SCONV - 1:
                        v.drain()
                last.then_inc(acc_rdy, 1)
            r.filled(v, ("sc", NX + 2 * SG_ - 1))
            nc.vector.tensor_tensor(UT[:], XLO[:].bitcast(F32), XHI.bitcast(F32), ALU.add).then_inc(x_whole, 1)
            v.wait_ge(ssd_in, 48)
            for t in range(4):
                key = ("dt", t)
                r.filled(v, key)
                r.read_done(nc.vector.tensor_tensor(DT[:, t, :], bank[r.bank(key)][:, 0:64], DROW[:, 0, :], ALU.add), key)
            v.drain()
            nc.vector.scalar_tensor_tensor(DA[:], DT[:], -1.0, DT[:], ALU.mult, ALU.min).then_inc(sp_in, 1)
            v.wait_ge(sp_out, 1)
            nc.vector.scalar_tensor_tensor(DT[:], DT[:], 0.0, DA[:], ALU.max, ALU.add)
            nc.vector.tensor_scalar(DROW[:, 1, :], DROW[:, 1, :], -1.0, None, ALU.mult)
            v.drain()
            nc.vector.tensor_tensor(DA[:], DT[:], bc(DROW[:, 1, :], 1, 4), ALU.mult).then_inc(da_rdy, 1)
            r.read(v, ("cum",))
            nc.vector.tensor_tensor(WST[:], bc(CUM[:, 4, :], 1, 2), CUM[:, 2:4, :], ALU.subtract)
            nc.vector.tensor_scalar(NCUM[:], CUM[:, 0:2, :], -1.0, None, ALU.mult)
            v.drain().then_inc(ec_in, 1)
            v.wait_ge(ec_out, 1)
            nc.vector.tensor_tensor(WST[:], WST[:], DT[:, 2:4, :], ALU.mult)
            for t in range(2):
                r.read(v, ("xt", NX - 1))
            v.drain()

            def state_inputs(g):
                if g >= 2:
                    r.filled(v, ("ss", g - 2))
                for t in range(2):
                    for z in range(2):
                        last = nc.vector.tensor_tensor(
                            XW[:, g % 2, t, z * 256:(z + 1) * 256].rearrange("p (h n) -> p h n", h=4),
                            XTOK[:, 2 + t, g * 256:(g + 1) * 256].rearrange("p (h n) -> p h n", h=4),
                            bc(WST[:, t, z * SH + 4 * g:z * SH + 4 * g + 4], 2, HD), ALU.mult)
                last.then_inc(xw_rdy, 1)

            def group_weights(g):
                v.wait_ge(cbc_in, 32 * (g + 1))
                if g >= 1:
                    r.filled(v, ("yo", g - 1, 1))
                for jt in range(2):
                    for z in range(2):
                        nc.vector.tensor_tensor(SEG[:, jt, z], CBC[:, z], bc(NEGM[:, z, jt, :], 1, 4), ALU.add)
                    v.drain().then_inc(seg_rdy, 1)

            def group_finish(g):
                key = ("cb", g)
                for jt in range(2):
                    v.wait_ge(seg_exp, 2 * g + jt + 1)
                    for h in range(4):
                        for z in range(2):
                            col = z * SH + 4 * g + h
                            sl = SEG[:, jt, z, h, :]
                            if z == 0:
                                nc.vector.tensor_scalar(sl, sl, DT[:, jt, col:col + 1], None, ALU.mult)
                    v.drain()
                    for h in range(4):
                        col = SH + 4 * g + h
                        nc.vector.scalar_tensor_tensor(SEG[:, jt, 1, h, :], SEG[:, jt, 1, h, :], DT[:, jt, col:col + 1],
                                                       SEG[:, jt, 0, h, :], ALU.mult, ALU.add)
                    if jt == 0:
                        r.filled(v, key)
                    v.drain()
                    last = nc.vector.tensor_tensor(SEG[:, jt, 1], SEG[:, jt, 1], bc(bank[r.bank(key)][:, jt * SEQ:(jt + 1) * SEQ], 1, 4), ALU.mult)
                    if jt == 1:
                        r.read_done(last, key)
                    v.drain().then_inc(w_rdy, 1)

            def group_outputs(g):
                gs = slice(g * 256, (g + 1) * 256)
                for t in range(2):
                    xs = XTOK[:, t, gs].rearrange("p (h n) -> p h n", h=4)
                    key = ("yo", g, t)
                    if t == 0:
                        r.filled(v, ("yo", g, 1))
                    r.filled(v, key)
                    nc.vector.tensor_tensor(xs, xs, bc(DROW[:, 2, 4 * g:4 * g + 4], 2, HD), ALU.mult)
                    v.drain()
                    r.read_done(nc.vector.tensor_tensor(xs, xs, bank[r.bank(key)][:, 0:256].rearrange("p (h n) -> p h n", h=4), ALU.add), key)
                    key = ("yi", g, t)
                    r.filled(v, key)
                    yi = YI[:, t].rearrange("p (z h n) -> p z h n", z=2, h=4)
                    b = bank[r.bank(key)][:, :].rearrange("p (z h n) -> p z h n", z=2, h=4)
                    for z in range(2):
                        last = nc.vector.tensor_tensor(yi[:, z], b[:, z], bc(EC[:, t, z * SH + 4 * g:z * SH + 4 * g + 4], 2, HD), ALU.mult)
                    r.read_done(last, key)
                    for z in range(2):
                        v.drain()
                        nc.vector.tensor_tensor(xs, xs, yi[:, z], ALU.add)

            state_inputs(0)
            for g in range(SG_):
                if g + 1 < SG_:
                    state_inputs(g + 1)
                group_weights(g)
                group_finish(g)
                group_outputs(g)
            v.drain()
            for g in range(SG_):
                r.read(v, ("sz", g // 2, g % 2))
            Y = XTOK[:, 0:2, :]
            nc.vector.tensor_tensor(Y, Y, Z, ALU.mult)
            v.drain()
            for t in range(2):
                nc.vector.tensor_tensor_reduce(Z[:, t, :], XTOK[:, t, :], XTOK[:, t, :], 1.0 / SDI, 0.0, ALU.mult, ALU.add, ST[:, t:t + 1])
            v.drain()
            nc.vector.tensor_scalar(ST[:, 0:2], ST[:, 0:2], RMS_EPS, None, ALU.add).then_inc(sq_in, 1)
            v.wait_ge(sq_out, 4)
            nc.vector.reciprocal(ST[:, 16:18], ST[:, 16:18])
            v.drain()
            v.wait_ge(ng_in, 16)
            for t in range(2):
                nc.vector.scalar_tensor_tensor(XTOK[:, t, :], XTOK[:, t, :], ST[:, 16 + t:17 + t], NG, ALU.mult, ALU.mult)
            v.drain().then_inc(y_rdy, 1)
            residual("sy", (), 2, 0)
            layer_norm(3, 5, 2)
            ffn(1, 2)
            layer_norm(4, 6, 2)


_FIRST = ["x", "positions", "w_in", "mla_q_norm", "mla_kv_norm", "mla_w_uq", "mla_w_ukv", "w_o", "ln1_g", "ln1_b",
          "router_group_w", "router_group_b", "router_expert_w", "router_expert_b", "expert_w_gate",
          "expert_w_up", "expert_w_down", "ln2_g", "ln2_b"]
_SECOND = ["c_2", "ctx_2", "c_ctx_2", "ada_w_2", "ada_b_2", "ln_g_2", "ln_b_2", "ffn_w1_2", "ffn_w2_2",
           "gla_w_in_2", "gla_w_a2_2", "gla_b_a2_2", "gla_norm_2", "gla_w_out_2", "ssd_w_in_2", "ssd_conv_w_2",
           "ssd_conv_b_2", "ssd_dt_bias_2", "ssd_a_log_2", "ssd_d_2", "ssd_norm_2", "ssd_w_out_2"]
PARTS = (1, 2)


def hybrid_kernel(nc, io, out):
    with ExitStack() as ctx:
        c = constants(nc, ctx)
        XA = ctx.enter_context(nc.sbuf_tensor("XA", [P, 4, D], F32))
        X = XA[:, 0:TT, :]
        dram_gate = nc.dram_tensor("gate_rows", [DEPTH, NEXP, SEQ], F32, kind="Internal").ap()
        dram_ada = nc.dram_tensor("ada_rows", [2, ADA], F32, kind="Internal").ap()
        dram_cum = nc.dram_tensor("cum_rows", [2, SH, SEQ], F32, kind="Internal").ap()
        setup(nc, io, c, X)
        if 1 in PARTS:
            block1(nc, io, c, X, dram_gate)
        if 2 in PARTS:
            block2(nc, io, c, XA, dram_cum, dram_ada)
        stored = ctx.enter_context(nc.semaphore("stored"))
        block = ctx.enter_context(nc.Block())

        @block.sync
        def _(sp):
            sp.dma_start(out[0].rearrange("(t p) n -> p t n", p=P), X).then_inc(stored, 16)
            sp.wait_ge(stored, 16)


def kernel(**inputs):
    import numpy as _np
    import concourse.bacc as _bacc
    from concourse import mybir as _mybir
    from concourse.bass_utils import run_bass_kernel_spmd as _run

    nc = _bacc.Bacc("TRN2", target_bir_lowering=False, num_devices=1)
    arrays, io = {}, {}
    for name, a in [(n, inputs[n]) for n in _FIRST + _SECOND] + list(host_constants().items()) + list(block2_constants().items()):
        a = _np.ascontiguousarray(a)
        arrays[f"in_{name}"] = a
        io[name] = nc.dram_tensor(f"in_{name}", a.shape, _mybir.dt.from_np(a.dtype), kind="ExternalInput").ap()
    out = nc.dram_tensor("out_0", (1, SEQ, D), F32, kind="ExternalOutput").ap()
    hybrid_kernel(nc, io, out)
    r = _run(nc, [arrays], core_ids=[0])
    return r.results[0]["out_0"]
```
